# Optimizing a Trainium2 kernel written in Bass

```python
import jax, jax.numpy as jnp
from jax import lax
import numpy as np

D_MODEL = 2048
BATCH = 1
SEQ = 256
DEPTH = 1

POOL_WIDTH = D_MODEL // 2
POOL_WINDOWS = (2, 4, 8, 16)
N_POOL_GROUPS = len(POOL_WINDOWS)
POOL_GROUP = POOL_WIDTH // N_POOL_GROUPS
N_Q_HEADS = 16
N_KV_HEADS = 4
GROUP = N_Q_HEADS // N_KV_HEADS
HEAD_DIM = D_MODEL // N_Q_HEADS
NSA_WIDTH = N_Q_HEADS * HEAD_DIM
KV_WIDTH = N_KV_HEADS * HEAD_DIM
CMP_BLOCK = 32
CMP_STRIDE = 16
CMP_HIDDEN = 2 * HEAD_DIM
SEL_BLOCK = 64
N_SEL = 16
WINDOW = 512
Q_BLOCK = 128
ROPE_THETA = 10000.0
EPS = 1e-6
NEG = -1e30
FORCE = 1e6
N_BRANCHES = 2
IN_SPLITS = (POOL_WIDTH, POOL_WIDTH, NSA_WIDTH, KV_WIDTH, KV_WIDTH, KV_WIDTH, KV_WIDTH,
             KV_WIDTH, KV_WIDTH, NSA_WIDTH, 3 * N_Q_HEADS)
D_IN = sum(IN_SPLITS)


def rmsnorm(x, w):
    xf = x.astype(jnp.float32)
    y = xf * lax.rsqrt(jnp.mean(xf * xf, axis=-1, keepdims=True) + EPS)
    return (y * w.astype(jnp.float32)).astype(x.dtype)

def rope(x, pos):
    half = HEAD_DIM // 2
    inv = ROPE_THETA ** (-jnp.arange(half, dtype=jnp.float32) / half)
    ang = pos.astype(jnp.float32)[:, None] * inv[None, :]
    cos = jnp.cos(ang)[None, :, None, :]
    sin = jnp.sin(ang)[None, :, None, :]
    xf = x.astype(jnp.float32)
    x1, x2 = xf[..., :half], xf[..., half:]
    return jnp.concatenate([x1 * cos - x2 * sin, x2 * cos + x1 * sin], axis=-1).astype(x.dtype)

def pool_mixer(u, mix, scale):
    b, s, _ = u.shape
    ug = u.reshape(b, s, N_POOL_GROUPS, POOL_GROUP)
    uf = ug.astype(jnp.float32)
    c = jnp.pad(jnp.cumsum(uf, axis=1), ((0, 0), (1, 0), (0, 0), (0, 0)))
    t = np.arange(s)
    win = np.array(POOL_WINDOWS)
    lo = np.maximum(t[:, None] + 1 - win[None, :], 0)
    cnt = jnp.asarray(np.minimum(t[:, None] + 1, win[None, :]).astype(np.float32))
    c_lo = c[:, lo, np.arange(N_POOL_GROUPS)[None, :]]
    mean = (c[:, 1:] - c_lo) / cnt[None, :, :, None]
    pooled = (mean - uf).astype(u.dtype)
    z = jnp.einsum("bsgc,gcd->bsgd", pooled, mix).reshape(b, s, POOL_WIDTH)
    return z * scale

def compress(kraw, pe, w1, w2):
    s = kraw.shape[1]
    n_cmp = (s - CMP_BLOCK) // CMP_STRIDE + 1
    idx = np.arange(n_cmp)[:, None] * CMP_STRIDE + np.arange(CMP_BLOCK)[None, :]
    kb = kraw[:, idx] + pe[None, None, :, None, :]
    hdn = jax.nn.silu(jnp.einsum("bnlhd,ldf->bnhf", kb, w1))
    return jnp.einsum("bnhf,fe->bnhe", hdn, w2)

def nsa_attention(q, kc, vc, ks, vs, kw, vw, gates):
    b, s = q.shape[0], q.shape[1]
    n_cmp = kc.shape[1]
    n_blk = s // SEL_BLOCK
    n_sel = min(N_SEL, n_blk)
    scale = HEAD_DIM ** -0.5
    cmp_end = jnp.arange(n_cmp) * CMP_STRIDE + CMP_BLOCK - 1
    ratio = SEL_BLOCK // CMP_STRIDE
    sub = CMP_BLOCK // CMP_STRIDE
    sel_idx = (np.arange(n_blk)[:, None, None] * ratio + np.arange(ratio)[None, :, None]
               - np.arange(sub)[None, None, :]).reshape(n_blk, ratio * sub)
    sel_valid = jnp.asarray((sel_idx >= 0) & (sel_idx < n_cmp))
    sel_idx = np.clip(sel_idx, 0, n_cmp - 1)
    ks_blk = ks.reshape(b, n_blk, SEL_BLOCK, N_KV_HEADS, HEAD_DIM).transpose(0, 3, 1, 2, 4)
    vs_blk = vs.reshape(b, n_blk, SEL_BLOCK, N_KV_HEADS, HEAD_DIM).transpose(0, 3, 1, 2, 4)
    kw_pad = jnp.pad(kw, ((0, 0), (WINDOW, 0), (0, 0), (0, 0)))
    vw_pad = jnp.pad(vw, ((0, 0), (WINDOW, 0), (0, 0), (0, 0)))
    gather = jax.vmap(jax.vmap(lambda kt, ix: kt[ix]))
    jblk = jnp.arange(n_blk)

    def block(i):
        s0 = i * Q_BLOCK
        qb = lax.dynamic_slice_in_dim(q, s0, Q_BLOCK, axis=1)
        gb = lax.dynamic_slice_in_dim(gates, s0, Q_BLOCK, axis=1)
        tpos = s0 + jnp.arange(Q_BLOCK)
        sc = jnp.einsum("bqhgd,bnhd->bhgqn", qb, kc, preferred_element_type=jnp.float32) * scale
        cvalid = cmp_end[None, :] <= tpos[:, None]
        p_c = jnp.where(cvalid, jax.nn.softmax(jnp.where(cvalid, sc, NEG), axis=-1), 0.0)
        o_c = jnp.einsum("bhgqn,bnhe->bqhge", p_c.astype(vc.dtype), vc)
        imp_c = p_c.sum(axis=2)
        imp = jnp.where(sel_valid, imp_c[..., sel_idx], 0.0).sum(-1)
        jt = (tpos // SEL_BLOCK)[:, None]
        forced = (jblk[None, :] == 0) | (jblk[None, :] == jt) | (jblk[None, :] == jt - 1)
        imp = jnp.where(forced, FORCE, imp)
        imp = jnp.where(jblk[None, :] > jt, NEG, imp)
        _, top = lax.top_k(imp, n_sel)
        kg = gather(ks_blk, top)
        vg = gather(vs_blk, top)
        kpos = top[..., None] * SEL_BLOCK + jnp.arange(SEL_BLOCK)
        svalid = kpos <= tpos[None, None, :, None, None]
        ss = jnp.einsum("bqhgd,bhqnld->bhgqnl", qb, kg, preferred_element_type=jnp.float32) * scale
        ss = jnp.where(svalid[:, :, None], ss, NEG)
        p_s = jax.nn.softmax(ss.reshape(ss.shape[:4] + (-1,)), axis=-1).reshape(ss.shape)
        o_s = jnp.einsum("bhgqnl,bhqnle->bqhge", p_s.astype(vg.dtype), vg)
        kwb = lax.dynamic_slice_in_dim(kw_pad, s0, WINDOW + Q_BLOCK, axis=1)
        vwb = lax.dynamic_slice_in_dim(vw_pad, s0, WINDOW + Q_BLOCK, axis=1)
        wpos = s0 - WINDOW + jnp.arange(WINDOW + Q_BLOCK)
        diff = tpos[:, None] - wpos[None, :]
        wvalid = (diff >= 0) & (diff < WINDOW) & (wpos[None, :] >= 0)
        sw = jnp.einsum("bqhgd,bkhd->bhgqk", qb, kwb, preferred_element_type=jnp.float32) * scale
        p_w = jax.nn.softmax(jnp.where(wvalid, sw, NEG), axis=-1)
        o_w = jnp.einsum("bhgqk,bkhe->bqhge", p_w.astype(vwb.dtype), vwb)
        return gb[..., 0:1] * o_c + gb[..., 1:2] * o_s + gb[..., 2:3] * o_w

    out = lax.map(block, jnp.arange(s // Q_BLOCK))
    return out.transpose(1, 0, 2, 3, 4, 5).reshape(b, s, NSA_WIDTH)

def first_inputs(seed: int = 0) -> dict:
    key = jax.random.key(seed)
    ks = jax.random.split(key, 20)
    f32 = jnp.float32
    nrm = lambda k, shape, fan: jax.random.normal(k, shape, f32) * (fan ** -0.5)
    L = DEPTH
    return {
        "x": jax.random.normal(ks[0], (BATCH, SEQ, D_MODEL), f32),
        "norm_w": 1.0 + 0.05 * jax.random.normal(ks[1], (L, D_MODEL), f32),
        "w_in": nrm(ks[2], (L, D_MODEL, D_IN), D_MODEL),
        "pool_mix": nrm(ks[3], (L, N_POOL_GROUPS, POOL_GROUP, POOL_GROUP), POOL_GROUP),
        "pool_scale": 1.0 + 0.1 * jax.random.normal(ks[4], (L, POOL_WIDTH), f32),
        "cmp_pe_k": 0.1 * jax.random.normal(ks[5], (L, CMP_BLOCK, HEAD_DIM), f32),
        "cmp_w1_k": nrm(ks[6], (L, CMP_BLOCK, HEAD_DIM, CMP_HIDDEN), CMP_BLOCK * HEAD_DIM),
        "cmp_w2_k": nrm(ks[7], (L, CMP_HIDDEN, HEAD_DIM), CMP_HIDDEN),
        "cmp_pe_v": 0.1 * jax.random.normal(ks[8], (L, CMP_BLOCK, HEAD_DIM), f32),
        "cmp_w1_v": nrm(ks[9], (L, CMP_BLOCK, HEAD_DIM, CMP_HIDDEN), CMP_BLOCK * HEAD_DIM),
        "cmp_w2_v": nrm(ks[10], (L, CMP_HIDDEN, HEAD_DIM), CMP_HIDDEN),
        "w_pool_out": nrm(ks[11], (L, POOL_WIDTH, D_MODEL), POOL_WIDTH),
        "w_nsa_out": nrm(ks[12], (L, NSA_WIDTH, D_MODEL), NSA_WIDTH),
        "w_merge": nrm(ks[13], (L, D_MODEL, N_BRANCHES * D_MODEL), D_MODEL),
        "b_merge": 0.01 * jax.random.normal(ks[14], (L, N_BRANCHES * D_MODEL), f32),
        "w_out": nrm(ks[15], (L, D_MODEL, D_MODEL), D_MODEL),
        "final_norm_w": 1.0 + 0.05 * jax.random.normal(ks[16], (D_MODEL,), f32),
    }

def first_block(x, norm_w, w_in, pool_mix, pool_scale, cmp_pe_k, cmp_w1_k, cmp_w2_k,
              cmp_pe_v, cmp_w1_v, cmp_w2_v, w_pool_out, w_nsa_out, w_merge, b_merge,
              w_out, final_norm_w):
    b, s, _ = x.shape
    pos = jnp.arange(s)
    n_cmp = (s - CMP_BLOCK) // CMP_STRIDE + 1
    cmp_pos = jnp.arange(n_cmp) * CMP_STRIDE + CMP_BLOCK - 1
    split_at = np.cumsum(IN_SPLITS)[:-1].tolist()
    for layer in range(DEPTH):
        h = rmsnorm(x, norm_w[layer])
        proj = h @ w_in[layer]
        (u_pool, g_pool, q, kc_raw, vc_raw, k_sel, v_sel, k_win, v_win,
         g_nsa, g_br) = jnp.split(proj, split_at, axis=-1)
        y_pool = pool_mixer(u_pool, pool_mix[layer], pool_scale[layer]) * jax.nn.silu(g_pool)
        y_a = y_pool @ w_pool_out[layer]
        heads = lambda t, n: t.reshape(b, s, n, HEAD_DIM)
        qh = rope(heads(q, N_Q_HEADS), pos).reshape(b, s, N_KV_HEADS, GROUP, HEAD_DIM)
        kc = rope(compress(heads(kc_raw, N_KV_HEADS), cmp_pe_k[layer], cmp_w1_k[layer],
                           cmp_w2_k[layer]), cmp_pos)
        vc = compress(heads(vc_raw, N_KV_HEADS), cmp_pe_v[layer], cmp_w1_v[layer], cmp_w2_v[layer])
        ksh = rope(heads(k_sel, N_KV_HEADS), pos)
        kwh = rope(heads(k_win, N_KV_HEADS), pos)
        gates = jax.nn.sigmoid(g_br).reshape(b, s, N_KV_HEADS, GROUP, 3)
        o_nsa = nsa_attention(qh, kc, vc, ksh, heads(v_sel, N_KV_HEADS), kwh,
                              heads(v_win, N_KV_HEADS), gates)
        y_b = (o_nsa * jax.nn.silu(g_nsa)) @ w_nsa_out[layer]
        gm = jax.nn.sigmoid(h @ w_merge[layer] + b_merge[layer]).reshape(b, s, N_BRANCHES, D_MODEL)
        merged = gm[:, :, 0] * y_a + gm[:, :, 1] * y_b
        x = x + merged @ w_out[layer]
    return rmsnorm(x, final_norm_w)


FOX_HEADS = 8
FOX_HEAD_DIM = 128
FOX_WIDTH = FOX_HEADS * FOX_HEAD_DIM
ATTN_BLOCK = 128
MLSTM_HEADS = 4
MLSTM_QK_DIM = 128
MLSTM_V_DIM = 256
MLSTM_QK_WIDTH = MLSTM_HEADS * MLSTM_QK_DIM
MLSTM_V_WIDTH = MLSTM_HEADS * MLSTM_V_DIM
MLSTM_CONV = 4
MLSTM_CHUNK = 128
MIX_WIDTH = FOX_WIDTH + MLSTM_V_WIDTH
IN_SPLITS_2 = (FOX_WIDTH, FOX_WIDTH, FOX_WIDTH, FOX_HEADS, MLSTM_QK_WIDTH, MLSTM_QK_WIDTH, MLSTM_V_WIDTH, MLSTM_HEADS, MLSTM_HEADS, MLSTM_V_WIDTH)
IN_WIDTH = 3 * FOX_WIDTH + FOX_HEADS + 2 * MLSTM_QK_WIDTH + 2 * MLSTM_V_WIDTH + 2 * MLSTM_HEADS
PEER_HEADS = 8
PEER_KEY_DIM = 256
PEER_N_KEYS = 128
PEER_TOPK = 16
PEER_N_EXPERTS = PEER_N_KEYS * PEER_N_KEYS
PEER_TOKEN_BLOCK = 128
NORM_EPS = 1e-6


def rmsnorm_2(x, w):
    xf = x.astype(jnp.float32)
    y = xf * lax.rsqrt(jnp.mean(xf * xf, axis=-1, keepdims=True) + NORM_EPS)
    return (y * w).astype(x.dtype)

def head_rmsnorm(h, w):
    B, S, H, dh = h.shape
    hf = h.astype(jnp.float32)
    hf = hf * lax.rsqrt(jnp.mean(hf * hf, axis=-1, keepdims=True) + NORM_EPS)
    return (hf.reshape(B, S, H * dh) * w).astype(h.dtype)

def causal_depthwise_conv(x, w, b):
    K = w.shape[0]
    S = x.shape[1]
    xp = jnp.pad(x, ((0, 0), (K - 1, 0), (0, 0)))
    y = b
    for j in range(K):
        y = y + w[j] * xp[:, j:j + S]
    return y

def forgetting_attention(q, k, v, f_logit):
    B, S, H, Dh = q.shape
    nb = S // ATTN_BLOCK
    F = jnp.cumsum(jax.nn.log_sigmoid(f_logit.astype(jnp.float32)), axis=1).transpose(0, 2, 1)
    qh = q.transpose(0, 2, 1, 3) * (Dh ** -0.5)
    kh = k.transpose(0, 2, 1, 3)
    vh = v.transpose(0, 2, 1, 3)
    q_blocks = qh.reshape(B, H, nb, ATTN_BLOCK, Dh).transpose(2, 0, 1, 3, 4)
    F_blocks = F.reshape(B, H, nb, ATTN_BLOCK).transpose(2, 0, 1, 3)
    q_pos = jnp.arange(S).reshape(nb, ATTN_BLOCK)
    k_pos = jnp.arange(S)

    def block(args):
        qb, Fb, pos = args
        s = jnp.einsum('bhqd,bhkd->bhqk', qb, kh, preferred_element_type=jnp.float32)
        s = s + Fb[..., :, None] - F[..., None, :]
        s = jnp.where(pos[:, None] >= k_pos[None, :], s, -jnp.inf)
        p = jax.nn.softmax(s, axis=-1)
        return jnp.einsum('bhqk,bhkd->bhqd', p.astype(vh.dtype), vh)

    out = lax.map(block, (q_blocks, F_blocks, q_pos))
    return out.transpose(1, 0, 3, 2, 4).reshape(B, S, H, Dh)

def mlstm_chunkwise(q, k, v, i_pre, f_pre):
    B, S, H, dk = q.shape
    dv = v.shape[-1]
    L = MLSTM_CHUNK
    nc = S // L
    f32 = jnp.float32

    def to_chunks(a):
        a = jnp.moveaxis(a, 2, 1)
        return a.reshape(B, H, nc, L, *a.shape[3:])

    qc = to_chunks(q).astype(f32)
    kc = to_chunks(k).astype(f32) * (dk ** -0.5)
    vc = to_chunks(v).astype(f32)
    ic = to_chunks(i_pre).astype(f32)
    b = jnp.cumsum(jax.nn.log_sigmoid(to_chunks(f_pre).astype(f32)), axis=-1)
    b_last = b[..., -1]

    w_end = b_last[..., None] - b + ic
    m_loc = jnp.max(w_end, axis=-1)
    a_end = jnp.exp(w_end - m_loc[..., None])
    C_loc = jnp.einsum('bhcl,bhcld,bhcle->bhcde', a_end, kc, vc)
    n_loc = jnp.einsum('bhcl,bhcld->bhcd', a_end, kc)

    def step(carry, inp):
        C, n, m = carry
        Cl, nl, ml, bl = inp
        m_new = jnp.maximum(bl + m, ml)
        a_prev = jnp.exp(bl + m - m_new)
        a_loc = jnp.exp(ml - m_new)
        C_new = a_prev[..., None, None] * C + a_loc[..., None, None] * Cl
        n_new = a_prev[..., None] * n + a_loc[..., None] * nl
        return (C_new, n_new, m_new), (C, n, m)

    init = (jnp.zeros((B, H, dk, dv), f32), jnp.zeros((B, H, dk), f32), jnp.zeros((B, H), f32))
    xs = (jnp.moveaxis(C_loc, 2, 0), jnp.moveaxis(n_loc, 2, 0), jnp.moveaxis(m_loc, 2, 0), jnp.moveaxis(b_last, 2, 0))
    _, (C_prev, n_prev, m_prev) = lax.scan(step, init, xs)
    C_prev = jnp.moveaxis(C_prev, 0, 2)
    n_prev = jnp.moveaxis(n_prev, 0, 2)
    m_prev = jnp.moveaxis(m_prev, 0, 2)

    g = b + m_prev[..., None]
    D = b[..., :, None] - b[..., None, :] + ic[..., None, :]
    causal = jnp.tril(jnp.ones((L, L), dtype=bool))
    D = jnp.where(causal, D, -jnp.inf)
    m_t = jnp.maximum(g, jnp.max(D, axis=-1))
    Sm = jnp.einsum('bhctd,bhcsd->bhcts', qc, kc) * jnp.exp(D - m_t[..., None])
    inter = jnp.exp(g - m_t)
    num = jnp.einsum('bhcts,bhcse->bhcte', Sm, vc) + inter[..., None] * jnp.einsum('bhctd,bhcde->bhcte', qc, C_prev)
    den = jnp.sum(Sm, axis=-1) + inter * jnp.einsum('bhctd,bhcd->bhct', qc, n_prev)
    h = num / jnp.maximum(jnp.abs(den), jnp.exp(-m_t))[..., None]
    return h.reshape(B, H, S, dv).transpose(0, 2, 1, 3).astype(v.dtype)

def peer_ffn(x, w_q, keys, u, v):
    B, S, D = x.shape
    T = B * S
    xt = x.reshape(T, D)
    q = (xt @ w_q).reshape(T, PEER_HEADS, 2, PEER_KEY_DIM // 2)
    scores = jnp.einsum('thpd,pnd->thpn', q, keys, preferred_element_type=jnp.float32)
    s_top, i_top = lax.top_k(scores, PEER_TOPK)
    cand = (s_top[:, :, 0, :, None] + s_top[:, :, 1, None, :]).reshape(T, PEER_HEADS, PEER_TOPK * PEER_TOPK)
    cand_idx = (i_top[:, :, 0, :, None] * PEER_N_KEYS + i_top[:, :, 1, None, :]).reshape(T, PEER_HEADS, PEER_TOPK * PEER_TOPK)
    s_fin, pos = lax.top_k(cand, PEER_TOPK)
    idx = jnp.take_along_axis(cand_idx, pos, axis=-1)
    gate = jax.nn.softmax(s_fin, axis=-1)
    nblk = T // PEER_TOKEN_BLOCK

    def blk(args):
        xb, ib, gb = args
        ub = jnp.take(u, ib, axis=0)
        act = jax.nn.gelu(jnp.einsum('thkd,td->thk', ub, xb, preferred_element_type=jnp.float32), approximate=False) * gb
        vb = jnp.take(v, ib, axis=0)
        return jnp.einsum('thk,thkd->td', act.astype(vb.dtype), vb)

    y = lax.map(blk, (xt.reshape(nblk, PEER_TOKEN_BLOCK, D),
                      idx.reshape(nblk, PEER_TOKEN_BLOCK, PEER_HEADS, PEER_TOPK),
                      gate.reshape(nblk, PEER_TOKEN_BLOCK, PEER_HEADS, PEER_TOPK)))
    return y.reshape(B, S, D)

def second_inputs(seed: int = 0) -> dict:
    key = jax.random.key(seed)
    ks = jax.random.split(key, 18)
    f32 = jnp.float32

    def nrm(k, shape, scale):
        return jax.random.normal(k, shape, f32) * scale

    return {
        "x": nrm(ks[0], (BATCH, SEQ, D_MODEL), 1.0),
        "norm1_w": 1.0 + nrm(ks[1], (DEPTH, D_MODEL), 0.02),
        "w_in": nrm(ks[2], (DEPTH, D_MODEL, IN_WIDTH), D_MODEL ** -0.5),
        "fox_f_bias": jnp.linspace(2.0, 6.0, FOX_HEADS, dtype=f32)[None] + nrm(ks[3], (DEPTH, FOX_HEADS), 0.1),
        "mlstm_conv_w": nrm(ks[4], (DEPTH, MLSTM_CONV, 2 * MLSTM_QK_WIDTH), MLSTM_CONV ** -0.5),
        "mlstm_conv_b": nrm(ks[5], (DEPTH, 2 * MLSTM_QK_WIDTH), 0.01),
        "mlstm_i_bias": nrm(ks[6], (DEPTH, MLSTM_HEADS), 0.1),
        "mlstm_f_bias": jnp.linspace(3.0, 6.0, MLSTM_HEADS, dtype=f32)[None] + nrm(ks[7], (DEPTH, MLSTM_HEADS), 0.1),
        "fox_out_norm_w": 1.0 + nrm(ks[8], (DEPTH, FOX_WIDTH), 0.02),
        "mlstm_out_norm_w": 1.0 + nrm(ks[9], (DEPTH, MLSTM_V_WIDTH), 0.02),
        "w_out": nrm(ks[10], (DEPTH, MIX_WIDTH, D_MODEL), MIX_WIDTH ** -0.5),
        "norm2_w": 1.0 + nrm(ks[11], (DEPTH, D_MODEL), 0.02),
        "peer_w_q": nrm(ks[12], (DEPTH, D_MODEL, PEER_HEADS * PEER_KEY_DIM), D_MODEL ** -0.5),
        "peer_keys": nrm(ks[13], (DEPTH, 2, PEER_N_KEYS, PEER_KEY_DIM // 2), (PEER_KEY_DIM // 2) ** -0.5),
        "peer_u": nrm(ks[14], (DEPTH, PEER_N_EXPERTS, D_MODEL), D_MODEL ** -0.5),
        "peer_v": nrm(ks[15], (DEPTH, PEER_N_EXPERTS, D_MODEL), PEER_HEADS ** -0.5),
        "final_norm_w": 1.0 + nrm(ks[16], (D_MODEL,), 0.02),
    }

def second_block(x, norm1_w, w_in, fox_f_bias, mlstm_conv_w, mlstm_conv_b, mlstm_i_bias, mlstm_f_bias,
              fox_out_norm_w, mlstm_out_norm_w, w_out, norm2_w, peer_w_q, peer_keys, peer_u, peer_v,
              final_norm_w):
    B, S, _ = x.shape
    split_points = [int(p) for p in np.cumsum(IN_SPLITS_2)[:-1]]
    for l in range(DEPTH):
        h = rmsnorm_2(x, norm1_w[l])
        z = h @ w_in[l]
        fq, fk, fv, ff, mq, mk, mv, mi, mf, mo = jnp.split(z, split_points, axis=-1)

        att = forgetting_attention(fq.reshape(B, S, FOX_HEADS, FOX_HEAD_DIM),
                                   fk.reshape(B, S, FOX_HEADS, FOX_HEAD_DIM),
                                   fv.reshape(B, S, FOX_HEADS, FOX_HEAD_DIM),
                                   ff + fox_f_bias[l])

        mqk = jax.nn.silu(causal_depthwise_conv(jnp.concatenate([mq, mk], axis=-1), mlstm_conv_w[l], mlstm_conv_b[l]))
        mq_c, mk_c = jnp.split(mqk, 2, axis=-1)
        cell = mlstm_chunkwise(mq_c.reshape(B, S, MLSTM_HEADS, MLSTM_QK_DIM),
                               mk_c.reshape(B, S, MLSTM_HEADS, MLSTM_QK_DIM),
                               mv.reshape(B, S, MLSTM_HEADS, MLSTM_V_DIM),
                               mi + mlstm_i_bias[l], mf + mlstm_f_bias[l])
        cell = jax.nn.sigmoid(mo.astype(jnp.float32)).astype(cell.dtype).reshape(B, S, MLSTM_HEADS, MLSTM_V_DIM) * cell

        mixed = jnp.concatenate([head_rmsnorm(att, fox_out_norm_w[l]),
                                 head_rmsnorm(cell, mlstm_out_norm_w[l])], axis=-1)
        x = x + mixed @ w_out[l]

        x = x + peer_ffn(rmsnorm_2(x, norm2_w[l]), peer_w_q[l], peer_keys[l], peer_u[l], peer_v[l])
    return rmsnorm_2(x, final_norm_w)


def setup_inputs(seed=0):
    out = dict(first_inputs(seed))
    for name, value in second_inputs(seed + 1).items():
        if name != "x":
            out[name + "_2"] = value
    return out


def reference(
    x, norm_w, w_in, pool_mix, pool_scale, cmp_pe_k, cmp_w1_k, cmp_w2_k, cmp_pe_v, cmp_w1_v,
    cmp_w2_v, w_pool_out, w_nsa_out, w_merge, b_merge, w_out, final_norm_w, norm1_w_2, w_in_2,
    fox_f_bias_2, mlstm_conv_w_2, mlstm_conv_b_2, mlstm_i_bias_2, mlstm_f_bias_2,
    fox_out_norm_w_2, mlstm_out_norm_w_2, w_out_2, norm2_w_2, peer_w_q_2, peer_keys_2, peer_u_2,
    peer_v_2, final_norm_w_2,
):
    x = first_block(
        x, norm_w, w_in, pool_mix, pool_scale, cmp_pe_k, cmp_w1_k, cmp_w2_k, cmp_pe_v, cmp_w1_v,
        cmp_w2_v, w_pool_out, w_nsa_out, w_merge, b_merge, w_out, final_norm_w,
    )
    return second_block(
        x, norm1_w_2, w_in_2, fox_f_bias_2, mlstm_conv_w_2, mlstm_conv_b_2, mlstm_i_bias_2,
        mlstm_f_bias_2, fox_out_norm_w_2, mlstm_out_norm_w_2, w_out_2, norm2_w_2, peer_w_q_2,
        peer_keys_2, peer_u_2, peer_v_2, final_norm_w_2,
    )


_drawn_inputs = setup_inputs


def setup_inputs(seed=0):
    import zlib

    import numpy as np

    out = dict(_drawn_inputs(seed))
    spreads = {}
    factors = {'cmp_pe_k': 8.0,
     'cmp_pe_v': 3.001,
     'b_merge': 22.689,
     'mlstm_conv_b_2': 6.068,
     'mlstm_i_bias_2': 64.0,
     'fox_out_norm_w_2': 9.419,
     'mlstm_out_norm_w_2': 9.397,
     'norm2_w_2': 9.888,
     'final_norm_w_2': 7.703}
    for name, (base, spread) in spreads.items():
        noise = np.random.default_rng([zlib.crc32(name.encode()), seed]).standard_normal(out[name].shape)
        drawn = base * np.exp(spread * noise) if base else spread * noise
        out[name] = __import__('jax').numpy.asarray(drawn.astype(out[name].dtype))
    for name, factor in factors.items():
        out[name] = (out[name] * factor).astype(out[name].dtype)
    return out
```

```python
from contextlib import ExitStack

import numpy as np

import concourse.bass as bass
from concourse import mybir

ALU = mybir.AluOpType
ACT = mybir.ActivationFunctionType
AX = mybir.AxisListType
F32 = mybir.dt.float32
U32 = mybir.dt.uint32

P = 128
T = 256
TB = T // P
D = 2048
KC = D // P
EPS = 1e-6
NEG = -1e30
LOWEST = -3.0e38
RING = 4
SLOT = 2048

POOL_W = 1024
WINDOWS = (2, 4, 8, 16)
NG = len(WINDOWS)
HQ, HKV, DH = 16, 4, 128
GQ = HQ // HKV
CB, CS, CH = 32, 16, 256
NCMP = (T - CB) // CS + 1
NC4 = HKV * NCMP
FH = 8
MH, MV = 4, 256
PH, NK, TOPK = 8, 128, 16
HK = PH * TOPK
NE_BLOCKS = NK

SCALE = float(DH) ** -0.5

PHASES = [("in_t", 16), ("in_n", 2), ("cmp", 2), ("merge", 8), ("pool_out", 2), ("nsa_out", 4),
          ("out1", 4), ("in2_t", 6), ("in2_n", 6), ("out2", 4), ("wq", 4), ("peer_u", 32), ("peer_v", 32)]
GROUPS = sum(n for _, n in PHASES)

PARAMS = [("ident", 128), ("mask", 256), ("cos", 256), ("sin", 256), ("ccos", NC4), ("csin", NC4),
          ("cmask", TB * NCMP), ("cvalid", TB * NCMP), ("iota", 128),
          ("norm1", KC), ("norm2", KC), ("norm3", KC), ("mixnorm", KC), ("pscale", 8), ("bmerge", 32),
          ("pek", CB), ("pev", CB), ("convw", 32), ("convb", 8), ("fbias", 1), ("ibias", 1), ("mfbias", 1),
          ("keysT", 2 * NK), ("wrows", KC * 16)]
STAGE1 = [("mixw", 2048), ("invcnt", NG * T), ("wgbr", KC * 48), ("w2k", 2 * DH), ("w2v", 2 * DH)]


def offsets(table):
    at, out = 0, {}
    for name, width in table:
        out[name] = (at, width)
        at += width
    return out, at


def first_groups():
    at, out = 0, {}
    for name, n in PHASES:
        out[name] = (at, n)
        at += n
    return out


def fills_per_bank(name, n):
    if name in ("in_t", "merge", "nsa_out", "in2_t", "wq", "peer_u"):
        return (n, n, 0, 0)
    if name in ("in_n", "out1", "in2_n", "out2"):
        return (n // 2,) * 4
    if name == "pool_out":
        return (n,) * 4
    return (0,) * 4


def earlier_fills():
    at, out = [1] * 4, {}
    for name, n in PHASES:
        out[name] = tuple(at)
        at = [a + f for a, f in zip(at, fills_per_bank(name, n))]
    return out


def build_two_blocks(nc, x, stream, params, stage1, fnw1, fnw, out):
    PO, n_params = offsets(PARAMS)
    S1, n_stage1 = offsets(STAGE1)
    G0 = first_groups()
    B0 = earlier_fills()

    with ExitStack() as ctx:
        def sb(name, shape, dt=F32):
            return ctx.enter_context(nc.sbuf_tensor(name, shape, dt))

        def sem(name):
            return ctx.enter_context(nc.semaphore(name))

        bank = [ctx.enter_context(nc.psum_tensor(f"bank{b}", [P, 512], F32)) for b in range(8)]

        ring = [sb(f"ring{s}", [P, SLOT]) for s in range(RING)]
        xres = sb("xres", [P, TB, D])
        hT = sb("hT", [P, KC, T])
        par = sb("par", [P, n_params])
        R = sb("R", [P, NK * T])
        idxT = sb("idxT", [P, 3, T])
        pairs = sb("pairs", [P, 2, 2, 2, P])
        gelu_u = pairs[:].rearrange("p a b c k -> p (a b c k)").rearrange("p (a k) -> p a k", a=2)
        st = sb("st", [P, 320])

        def prm(name, a=0, b=None):
            o, w = PO[name]
            return par[:, o + a:o + (w if b is None else b)]

        def prm_rows(name, n):
            o, _ = PO[name]
            return par[0:n, o:o + 1]

        def region(a, n):
            return R[:, a:a + n]

        ident = prm("ident")
        tri = prm("mask", 128, 256)

        pT = region(0, 64 * T).rearrange("p (j t) -> p j t", t=T)
        U0, GP0, KCR0, VCR0, KS0, KW0, Q0, GN0 = 0, 8, 16, 20, 24, 28, 32, 48
        vN1 = region(16384, 2048).rearrange("p (g b c) -> p g b c", g=2, b=TB)
        fnw1_sb = region(16384, D)
        scr = region(18432, 4096)
        scr2 = scr.rearrange("p (b d) -> p b d", b=TB)
        kb_at = (22528, 24448)
        kb = [region(a, CB * NC4).rearrange("p (l c) -> p l c", l=CB) for a in kb_at]
        stage1_at = 26368
        SP = region(30720, 1024).rearrange("p (a k) -> p a k", a=2)
        PT = region(31744, 1024).rearrange("p (a k) -> p a k", a=2)

        def s1(name):
            o, w = S1[name]
            return region(stage1_at + o, w)
        k0 = kb_at[0]
        vcs = R[0:NCMP, k0:k0 + 512]
        kcT = region(k0 + 512, NC4)
        kcS = region(k0 + 576, NC4)
        PcT = R[0:NCMP, k0 + 640:k0 + 896].rearrange("p (a q) -> p a q", a=2)
        Pc = region(k0 + 896, 32).rearrange("p (a k) -> p a k", a=2)
        hdn = region(k0 + 928, 4 * NC4).rearrange("p (v f c) -> p v f c", v=2, f=2)
        assert 928 + 4 * NC4 <= CB * NC4 and stage1_at + n_stage1 <= 30720
        gate0 = pT[:, 16:32, :]
        gate1 = pT[:, 32:48, :]

        FQ0, FK0, MQ0, MK0 = 0, 8, 16, 20
        vN2 = region(6144, 6144).rearrange("p (g b c) -> p g b c", g=6, b=TB)
        conv = region(12288, 2048).rearrange("p (j t) -> p j t", t=T)
        rows = region(14336, 4096).rearrange("p (j t) -> p j t", t=T)
        knat = region(22528, 512).rearrange("p (h d) -> p h d", h=MH)
        av = region(23040, 264)
        CN = region(23304, 4 * 264).rearrange("p (h e) -> p h e", h=MH)
        Dm = region(24360, 256).rearrange("p (a s) -> p a s", a=2)
        Sm = region(24616, 256).rearrange("p (a s) -> p a s", a=2)
        SmT = region(24872, 256).rearrange("p (a s) -> p a s", a=2)
        numt = region(25128, 512).rearrange("p (a e) -> p a e", a=2)
        smalls = region(25640, 32).rearrange("p (b c) -> p b c", b=TB)
        natc = region(25672, 64)

        qT3 = region(0, 4096).rearrange("p (j t) -> p j t", t=T)
        scores = region(4096, 4096).rearrange("p (b j n) -> p b j n", b=TB, j=2 * PH)
        work = region(8192, 4096).rearrange("p (b j n) -> p b j n", b=TB, j=2 * PH)
        topv = region(12288, 512).rearrange("p (b j k) -> p b j k", b=TB, j=2 * PH)
        topi = region(12800, 512).bitcast(U32).rearrange("p (b j k) -> p b j k", b=TB, j=2 * PH)
        topf = region(13312, 512).rearrange("p (b j k) -> p b j k", b=TB, j=2 * PH)
        cand = region(13824, 4096).rearrange("p (b h c) -> p b h c", b=TB, h=PH)
        cwork = region(17920, 4096).rearrange("p (b h c) -> p b h c", b=TB, h=PH)
        finv = region(22016, 256).rearrange("p (b h k) -> p b h k", b=TB, h=PH)
        fini = region(22272, 256).bitcast(U32).rearrange("p (b h k) -> p b h k", b=TB, h=PH)
        fab_u = region(22528, 512).bitcast(U32).rearrange("p (s b c) -> p s b c", s=2, b=TB)
        fab = region(23040, 512).rearrange("p (s b h k) -> p s b h k", s=2, b=TB, h=PH)
        onehot = region(23552, 2048).rearrange("p (h k j) -> p h k j", h=PH, k=TOPK)
        chosen = region(25600, 768).rearrange("p (b s c) -> p b s c", b=TB, s=3)
        G = R[:].rearrange("p (i t) -> p i t", t=T)

        ssq, msq, rt, rstd = st[:, 0:2], st[:, 2:4], st[:, 4:6], st[:, 6:8]
        gates = st[:, 8:104].rearrange("p (b c) -> p b c", b=TB)
        mx = st[:, 104:112].rearrange("p (a c) -> p a c", a=2)
        ngm = st[:, 112:120].rearrange("p (a c) -> p a c", a=2)
        sums = st[:, 120:128].rearrange("p (a c) -> p a c", a=2)
        rz = st[:, 128:136].rearrange("p (a c) -> p a c", a=2)
        gz = st[:, 136:144].rearrange("p (a c) -> p a c", a=2)
        mst = st[:, 144:160].rearrange("p (a c) -> p a c", a=2)
        hss = st[:, 160:184].rearrange("p (b c) -> p b c", b=TB)
        hrt = st[:, 184:208].rearrange("p (b c) -> p b c", b=TB)
        zs = st[:, 208:224].rearrange("p (b h) -> p b h", b=TB)
        rowst = st[0:8, 224:232]

        slot_full = [sem(f"slot_full{s}") for s in range(RING)]
        slot_used = [sem(f"slot_used{s}") for s in range(RING)]
        bank_free = [sem(f"bank_free{b}") for b in range(4)]
        x_in, params_in, stage1_in, fnw_in, out_done = (sem(n) for n in (
            "x_in", "params_in", "stage1_in", "fnw_in", "out_done"))
        sq_done, ms_ready, rt_done, xn_ready, turned, hT_part = (sem(n) for n in (
            "sq_done", "ms_ready", "rt_done", "xn_ready", "turned", "hT_part"))
        (gbr_ready, gates_ready, pooled, z_ready, y_pool, silu_done, swapped, roped, kb_ready, hid_ready,
         hid_silu, kc_ready, kc_copied, kc_roped, vc_ready, vc_copied) = (sem(n) for n in (
             "gbr_ready", "gates_ready", "pooled", "z_ready", "y_pool", "silu_done", "swapped", "roped",
             "kb_ready", "hid_ready", "hid_silu", "kc_ready", "kc_copied", "kc_roped", "vc_ready", "vc_copied"))
        (scores_ready, scores_read, max_ready, exp_done, probs_ready, probsT_ready, probsT_copied, o_done,
         o_read) = (sem(n) for n in (
             "scores_ready", "scores_read", "max_ready", "exp_done", "probs_ready", "probsT_ready",
             "probsT_copied", "o_done", "o_read"))
        merged_ready, x1_ready, x1_normed, x2_ready, fnw1_in = (sem(n) for n in (
            "merged_ready", "x1_ready", "x1_normed", "x2_ready", "fnw1_in"))
        (sm_ready, sm_copied, rowsT_ready, row_e, row_l, row_y, rows_ready, nat_ready, nat_copied, a_ready,
         conv_done, conv_silu, q_ready, knat_ready, knat_copied, av_ready, C_ready, C_copied) = (sem(n) for n in (
             "sm_ready", "sm_copied", "rowsT_ready", "row_e", "row_l", "row_y", "rows_ready", "nat_ready",
             "nat_copied", "a_ready", "conv_done", "conv_silu", "q_ready", "knat_ready", "knat_copied",
             "av_ready", "C_ready", "C_copied"))
        (f_scores, f_read, f_max, f_exp, f_T, f_copied, f_o, f_oread) = (sem(n) for n in (
            "f_scores", "f_read", "f_max", "f_exp", "f_T", "f_copied", "f_o", "f_oread"))
        (m_scores, m_max, m_exp, m_sm, m_T, m_copied, m_num, m_read) = (sem(n) for n in (
            "m_scores", "m_max", "m_exp", "m_sm", "m_T", "m_copied", "m_num", "m_read"))
        mo_sig, cells, head_sq, head_ms, head_rt = (sem(n) for n in (
            "mo_sig", "cells", "head_sq", "head_ms", "head_rt"))
        (qs_ready, qs_copied, gate_arg, gate_exp, chosen_ready, chosenT, chosenT_copied, pair_ready, pair_free,
         g_evac) = (sem(n) for n in (
             "qs_ready", "qs_copied", "gate_arg", "gate_exp", "chosen_ready", "chosenT", "chosenT_copied",
             "pair_ready", "pair_free", "g_evac"))
        gated = [sem("gated0"), sem("gated1")]
        zeros_ready, y_done, yT_dve, yT_act, y_turned, x3_ready, result = (sem(n) for n in (
            "zeros_ready", "y_done", "yT_dve", "yT_act", "y_turned", "x3_ready", "result"))
        dve_step, act_step, pool_step = sem("dve_step"), sem("act_step"), sem("pool_step")

        def stepper(eng, s):
            n = [0]

            def step(ins):
                n[0] += 1
                ins.then_inc(s, 1)
                eng.wait_ge(s, n[0])
            return step

        def bc(ap, shape):
            return ap.to_broadcast(shape)

        block = ctx.enter_context(nc.Block())

        @block.sync
        def _(sp):
            sp.dma_start(xres[:], x.rearrange("o (b p) d -> p (o b) d", p=P)).then_inc(x_in, 16)
            sp.dma_start(par[:], params).then_inc(params_in, 16)
            for s in range(RING):
                sp.dma_start(ring[s][:], stream[s]).then_inc(slot_full[s], 16)
            sp.dma_start(region(stage1_at, n_stage1), stage1).then_inc(stage1_in, 16)
            with sp.Fori(1, GROUPS) as g:
                for s in range(RING):
                    sp.wait_ge(slot_used[s], g)
                    sp.dma_start(ring[s][:], stream[g * RING + s]).then_inc(slot_full[s], 16)
            sp.wait_ge(slot_used[0], GROUPS)
            sp.dma_start(ring[0][:], fnw.partition_broadcast(P)).then_inc(fnw_in, 16)
            sp.wait_ge(result, TB)
            sp.dma_start(out.rearrange("o (b p) d -> p (o b) d", p=P),
                         R[:, 0:TB * D].rearrange("p (b d) -> p b d", b=TB)).then_inc(out_done, 16)
            sp.wait_ge(out_done, 16)

        @block.tensor
        def _(pe):
            mm = nc.tensor.matmul

            def turn_norm(n):
                for b in range(TB):
                    pe.wait_ge(xn_ready, TB * n + b + 1)
                    for j in range(4):
                        if b > 0:
                            pe.wait_ge(hT_part, 8 * n + 4 * (b - 1) + j + 1)
                        for c in range(4):
                            last = nc.tensor.transpose(bank[4 + j][:, c * P:(c + 1) * P],
                                                       scr2[:, b, (4 * j + c) * P:(4 * j + c + 1) * P], ident)
                        last.then_inc(turned, 1)

            def phase_t(name, rhs):
                g0, n = G0[name]
                with pe.Fori(0, n) as i:
                    for s in range(RING):
                        b = s // 2
                        if s % 2 == 0:
                            pe.wait_ge(bank_free[b], i + B0[name][b])
                        pe.wait_ge(slot_full[s], i * 16 + 16 * (g0 + 1))
                        for k in range(KC):
                            last = mm(bank[b][:, (s % 2) * T:(s % 2 + 1) * T], ring[s][:, k * P:(k + 1) * P],
                                      rhs[:, k, :], start=(k == 0), stop=(k == KC - 1))
                        last.then_inc(slot_used[s], 1)

            def phase_n(name, lhs):
                g0, n = G0[name]
                with pe.Fori(0, n // 2) as i:
                    for h in range(2):
                        for b in range(TB):
                            pe.wait_ge(bank_free[2 * h + b], i + B0[name][2 * h + b])
                        for s in range(RING):
                            pe.wait_ge(slot_full[s], i * 32 + 16 * (g0 + h + 1))
                            for kk in range(4):
                                k = 4 * s + kk
                                for b in range(TB):
                                    last = mm(bank[2 * h + b][:], lhs[:, k, b * P:(b + 1) * P],
                                              ring[s][:, kk * 512:(kk + 1) * 512], start=(k == 0), stop=(k == KC - 1))
                            last.then_inc(slot_used[s], 1)

            for s_ in (*bank_free, *gated):
                pe.sem_inc(s_, 1)
            pe.wait_ge(params_in, 16)
            turn_norm(0)
            pe.wait_ge(hT_part, 8)
            phase_t("in_t", hT)
            phase_n("in_n", hT)
            pe.wait_ge(stage1_in, 16)
            wg = s1("wgbr").rearrange("p (k c) -> p k c", k=KC)
            for b in range(TB):
                for k in range(KC):
                    last = mm(bank[4 + b][:, 0:48], hT[:, k, b * P:(b + 1) * P], wg[:, k, :],
                              start=(k == 0), stop=(k == KC - 1))
            last.then_inc(gbr_ready, 1)
            for v in range(2):
                pe.wait_ge(kb_ready, v + 1)
                if v == 0:
                    pe.wait_ge(gates_ready, 1)
                for s in range(RING):
                    pe.wait_ge(slot_full[s], 16 * (G0["cmp"][0] + v + 1))
                    for ll in range(8):
                        l = 8 * s + ll
                        for f in range(2):
                            last = mm(bank[4 + 2 * v + f][:, 0:NC4], ring[s][:, ll * CH + f * P:ll * CH + (f + 1) * P],
                                      kb[v][:, l, :], start=(l == 0), stop=(l == CB - 1))
                    last.then_inc(slot_used[s], 1)
            pe.wait_ge(hid_silu, 1)
            w2k = s1("w2k").rearrange("p (f e) -> p f e", f=2)
            w2v = s1("w2v").rearrange("p (f e) -> p f e", f=2)
            for f in range(2):
                last = mm(bank[4][:, 0:NC4], w2k[:, f, :], hdn[:, 0, f, :], start=(f == 0), stop=(f == 1))
            last.then_inc(kc_ready, 1)
            pe.wait_ge(hid_silu, 2)
            for h in range(HKV):
                for f in range(2):
                    last = mm(bank[5][0:NCMP, h * DH:(h + 1) * DH], hdn[:, 1, f, h * NCMP:(h + 1) * NCMP],
                              w2v[:, f, :], start=(f == 0), stop=(f == 1))
            last.then_inc(vc_ready, 1)

            def nsa_scores(u):
                h, qb = divmod(u, TB)
                a, kv, nk = u % 2, h // GQ, (qb + 1) * P
                if u >= 2:
                    pe.wait_ge(scores_read, u - 1)
                    pe.wait_ge(probsT_copied, u - 1)
                q = pT[:, Q0 + h, qb * P:(qb + 1) * P]
                mm(bank[4 + a][:, 0:nk], q, pT[:, KS0 + kv, 0:nk], start=True, stop=True)
                mm(bank[4 + a][:, T:T + nk], q, pT[:, KW0 + kv, 0:nk], start=True, stop=True)
                mm(bank[a][:, 0:NCMP], q, kcT[:, kv * NCMP:(kv + 1) * NCMP], start=True,
                   stop=True).then_inc(scores_ready, 1)

            def nsa_turn(u):
                qb, a = u % TB, u % 2
                nb = qb + 1
                pe.wait_ge(probs_ready, u + 1)
                if u >= 2:
                    pe.wait_ge(probsT_copied, u - 1)
                for br in range(2):
                    for k in range(nb):
                        j = br * nb + k
                        nc.tensor.transpose(bank[6 + a][:, j * P:(j + 1) * P],
                                            SP[:, a, br * T + k * P:br * T + (k + 1) * P], ident)
                nc.tensor.transpose(bank[a][0:NCMP, P:2 * P], Pc[:, a, 0:NCMP], ident).then_inc(probsT_ready, 1)

            def nsa_values(u):
                h, qb = divmod(u, TB)
                a, kv, nb = u % 2, h // GQ, qb + 1
                pe.wait_ge(probsT_copied, u + 1)
                if qb == 0 and h >= 2:
                    pe.wait_ge(o_read, h - 1)
                o = bank[2 + h % 2][:, qb * P:(qb + 1) * P]
                mm(o, vcs[:, kv * DH:(kv + 1) * DH], PcT[:, a, :], start=True, stop=False)
                for br in range(2):
                    for k in range(nb):
                        j = br * nb + k
                        last = mm(o, vN1[:, br, k, kv * DH:(kv + 1) * DH], PT[:, a, j * P:(j + 1) * P],
                                  start=False, stop=(j == 2 * nb - 1))
                last.then_inc(o_done, 1)

            units = HQ * TB
            pe.wait_ge(roped, 6)
            pe.wait_ge(kc_roped, 1)
            pe.wait_ge(vc_copied, 1)
            for b in range(4):
                pe.wait_ge(bank_free[b], B0["merge"][b])
            nsa_scores(0)
            nsa_scores(1)
            for u in range(units):
                nsa_turn(u)
                if u + 2 < units:
                    nsa_scores(u + 2)
                nsa_values(u)
            pe.wait_ge(pooled, NG)
            pe.wait_ge(probsT_copied, units)
            mixw = s1("mixw").rearrange("p (g c e) -> p g c e", g=NG, c=2)
            for g in range(NG):
                for e in range(2):
                    for c in range(2):
                        last = mm(bank[4 + g][:, e * T:(e + 1) * T], mixw[:, g, c, e * P:(e + 1) * P],
                                  pT[:, U0 + 2 * g + c, :], start=(c == 0), stop=(c == 1))
                last.then_inc(z_ready, 1)
            pe.wait_ge(o_read, HQ)
            phase_t("merge", hT)
            g0, n = G0["pool_out"]
            pe.wait_ge(y_pool, NG)
            with pe.Fori(0, n) as i:
                for s in range(RING):
                    pe.wait_ge(bank_free[s], i + B0["pool_out"][s])
                    pe.wait_ge(slot_full[s], i * 16 + 16 * (g0 + 1))
                    for e in range(2):
                        for k in range(8):
                            last = mm(bank[s][:, e * T:(e + 1) * T], ring[s][:, (e * 8 + k) * P:(e * 8 + k + 1) * P],
                                      pT[:, U0 + k, :], start=(k == 0), stop=(k == 7))
                    last.then_inc(slot_used[s], 1)
            phase_t("nsa_out", pT[:, GN0:GN0 + 16, :])
            pe.wait_ge(merged_ready, 2 * G0["nsa_out"][1])
            phase_n("out1", gate0)

            turn_norm(1)
            pe.wait_ge(hT_part, 16)
            wr = prm("wrows").rearrange("p (k c) -> p k c", k=KC)
            for b in range(TB):
                for k in range(KC):
                    last = mm(bank[4][:, b * 16:(b + 1) * 16], hT[:, k, b * P:(b + 1) * P], wr[:, k, :],
                              start=(k == 0), stop=(k == KC - 1))
            last.then_inc(sm_ready, 1)
            pe.wait_ge(sm_copied, 1)
            for b in range(TB):
                for r, (c0, c1) in enumerate(((0, 8), (8, 12), (12, 16))):
                    last = nc.tensor.transpose(bank[5 + r][0:c1 - c0, b * P:(b + 1) * P], smalls[:, b, c0:c1], ident)
            last.then_inc(rowsT_ready, 1)
            phase_t("in2_t", hT)
            phase_n("in2_n", hT)
            pe.wait_ge(rows_ready, 1)
            for c in range(TB):
                nc.tensor.transpose(bank[4][:, 8 * c:8 * c + 8], rows[0:8, 6, c * P:(c + 1) * P], ident[0:8, 0:8])
                nc.tensor.transpose(bank[4][:, 16 + 4 * c:20 + 4 * c], rows[0:4, 8, c * P:(c + 1) * P],
                                    ident[0:4, 0:4])
                nc.tensor.transpose(bank[4][:, 24 + 4 * c:28 + 4 * c], rows[0:4, 10, c * P:(c + 1) * P],
                                    ident[0:4, 0:4])
            nc.tensor.transpose(bank[4][:, 32:36], rows[0:4, 11, 0:P], ident[0:4, 0:4]).then_inc(nat_ready, 1)
            pe.wait_ge(q_ready, 2)
            for h in range(MH):
                last = nc.tensor.transpose(bank[5][:, h * P:(h + 1) * P], conv[:, 4 + h, 0:P], ident)
            last.then_inc(knat_ready, 1)
            pe.wait_ge(knat_copied, 1)
            for h in range(MH):
                pe.wait_ge(av_ready, h + 1)
                mm(bank[6][:, 0:MV + 1], knat[:, h, :], av[:, 0:MV + 1], start=True, stop=True).then_inc(C_ready, 1)

            def fox_scores(u):
                h, qb = divmod(u, TB)
                a, nk = u % 2, (qb + 1) * P
                if u >= 2:
                    pe.wait_ge(f_read, u - 1)
                mm(bank[4 + a][:, 0:nk], pT[:, FQ0 + h, qb * P:(qb + 1) * P], pT[:, FK0 + h, 0:nk],
                   start=True, stop=False)
                mm(bank[4 + a][:, 0:nk], bc(ident[0:8, h:h + 1], [8, P]), rows[0:8, 7, 0:nk],
                   start=False, stop=True).then_inc(f_scores, 1)

            def fox_turn(u):
                qb, a = u % TB, u % 2
                pe.wait_ge(f_exp, u + 1)
                if u >= 2:
                    pe.wait_ge(f_copied, u - 1)
                for k in range(qb + 1):
                    last = nc.tensor.transpose(bank[6 + a][:, k * P:(k + 1) * P], SP[:, a, k * P:(k + 1) * P], ident)
                last.then_inc(f_T, 1)

            def fox_values(u):
                h, qb = divmod(u, TB)
                a = u % 2
                pe.wait_ge(f_copied, u + 1)
                if u >= 2:
                    pe.wait_ge(f_oread, u - 1)
                for k in range(qb + 1):
                    last = mm(bank[2 + a][:, 0:DH], PT[:, a, k * P:(k + 1) * P],
                              vN2[:, h // 4, k, (h % 4) * DH:(h % 4 + 1) * DH], start=(k == 0), stop=(k == qb))
                last.then_inc(f_o, 1)

            units = FH * TB
            pe.wait_ge(nat_copied, 1)
            pe.wait_ge(C_copied, MH)
            for b in range(4):
                pe.wait_ge(bank_free[b], B0["out2"][b])
            fox_scores(0)
            fox_scores(1)
            for u in range(units):
                fox_turn(u)
                if u + 2 < units:
                    fox_scores(u + 2)
                fox_values(u)
            pe.wait_ge(f_copied, units)
            pe.wait_ge(f_oread, units)

            def m_sc(u):
                c, h = divmod(u, MH)
                a = u % 2
                if u >= 2:
                    pe.wait_ge(m_sm, u - 1)
                cs = slice(c * P, (c + 1) * P)
                mm(bank[4 + a][:, 0:P], conv[:, h, cs], conv[:, 4 + h, cs], start=True, stop=True)
                mm(bank[4 + a][:, P:2 * P], bc(ident[0:4, h:h + 1], [4, P]), rows[0:4, 9, cs],
                   start=True, stop=True).then_inc(m_scores, 1)

            def m_turn(u):
                a = u % 2
                pe.wait_ge(m_sm, u + 1)
                if u >= 2:
                    pe.wait_ge(m_copied, u - 1)
                nc.tensor.transpose(bank[6 + a][:, 0:P], Sm[:, a, :], ident).then_inc(m_T, 1)

            def m_values(u):
                c, h = divmod(u, MH)
                a = u % 2
                pe.wait_ge(m_copied, u + 1)
                if u >= 2:
                    pe.wait_ge(m_read, u - 1)
                if c == 1:
                    mm(bank[a][:, 0:MV + 1], conv[:, h, P:2 * P], CN[:, h, 0:MV + 1], start=True, stop=True)
                mm(bank[2 + a][:, 0:MV], SmT[:, a, :], vN2[:, 2 + h // 2, c, (h % 2) * MV:(h % 2 + 1) * MV],
                   start=True, stop=True).then_inc(m_num, 1)

            units = MH * TB
            m_sc(0)
            m_sc(1)
            for u in range(units):
                m_turn(u)
                if u + 2 < units:
                    m_sc(u + 2)
                m_values(u)
            turn_norm(2)
            pe.wait_ge(hT_part, 24)
            phase_n("out2", hT)
            turn_norm(3)
            pe.wait_ge(hT_part, 32)
            phase_t("wq", hT)
            for b in range(2):
                pe.wait_ge(bank_free[b], B0["peer_u"][b])
            keysT = prm("keysT").rearrange("p (s n) -> p s n", s=2)
            for f in range(TB * 4):
                b, j = divmod(f, 4)
                if f >= 4:
                    pe.wait_ge(qs_copied, f - 3)
                for c in range(4):
                    hp = 4 * j + c
                    last = mm(bank[4 + j][:, c * NK:(c + 1) * NK], qT3[:, hp, b * P:(b + 1) * P],
                              keysT[:, hp % 2, :], start=True, stop=True)
                last.then_inc(qs_ready, 1)
            for b in range(TB):
                pe.wait_ge(chosen_ready, b + 1)
                for s in range(3):
                    last = nc.tensor.transpose(bank[4 + b][:, s * P:(s + 1) * P], chosen[:, b, s, :], ident)
                last.then_inc(chosenT, 1)
            pe.wait_ge(chosenT_copied, TB)
            pe.sem_inc(pair_free, 2)
            with pe.Fori(0, T // 8) as i:
                for q in range(4):
                    if q % 2 == 0:
                        pe.wait_ge(g_evac, i * 2 + q // 2 + 1)
                    pe.wait_ge(pair_ready, i * 4 + q + 1)
                    for t in range(2):
                        c = (q % 2) * 2 + t
                        last = mm(bank[4 + q // 2][:, c * P:(c + 1) * P], pairs[:, q % 2, t, 0, :],
                                  pairs[:, q % 2, t, 1, :], start=True, stop=True)
                    last.then_inc(pair_free, 1)
            phase_t("peer_u", hT)
            pe.wait_ge(zeros_ready, 1)
            for b in range(2):
                pe.wait_ge(gated[b], G0["peer_u"][1] + 1)
            pe.wait_ge(g_evac, 2 + T // 4)
            for b in range(8):
                mm(bank[b][:], ident, gelu_u[:, 0, :], start=True, stop=False, skip_group_check=True)
            g0, n = G0["peer_v"]
            with pe.Fori(0, n) as i:
                for s in range(RING):
                    pe.wait_ge(slot_full[s], i * 16 + 16 * (g0 + 1))
                    for d in range(KC):
                        last = mm(bank[d // 2][:, (d % 2) * T:(d % 2 + 1) * T], ring[s][:, d * P:(d + 1) * P],
                                  R[:, bass.ds(i * (4 * T) + s * T, T)], start=False, stop=False, skip_group_check=True)
                    last.then_inc(slot_used[s], 1)
            for b in range(8):
                last = mm(bank[b][:], ident, gelu_u[:, 0, :], start=False, stop=True, skip_group_check=True)
            last.then_inc(y_done, 1)
            pe.wait_ge(yT_dve, 4)
            pe.wait_ge(yT_act, 4)
            for f in range(8):
                b, j = divmod(f, 4)
                for c in range(4):
                    last = nc.tensor.transpose(bank[f][:, c * P:(c + 1) * P], hT[:, 4 * j + c, b * P:(b + 1) * P],
                                               ident)
                last.then_inc(y_turned, 1)

        @block.scalar
        def _(act):
            step = stepper(act, act_step)
            A = nc.scalar.activation

            def squares(n):
                for b in range(TB):
                    A(scr2[:, b, :], xres[:, b, :], ACT.Square, accum_out=ssq[:, b:b + 1]).then_inc(sq_done, 1)
                act.wait_ge(ms_ready, n + 1)
                A(rt, msq, ACT.Sqrt).then_inc(rt_done, 1)

            def evac_t(name, dst0):
                g0, n = G0[name]
                with act.Fori(0, n) as i:
                    act.wait_ge(slot_used[1], i + g0 + 1)
                    A(R[:, bass.ds(i * (4 * T) + dst0 * T, 2 * T)], bank[0][:], ACT.Copy).then_inc(bank_free[0], 1)

            def evac_n(name, dst, lo):
                g0, n = G0[name]
                for g in range(n):
                    act.wait_ge(slot_used[3], g0 + g + 1)
                    A(dst[:, g, 0, :], bank[2 * (g % 2)][:], ACT.Copy).then_inc(bank_free[2 * (g % 2)], 1)

            act.wait_ge(x_in, 16)
            squares(0)
            evac_t("in_t", 0)
            evac_n("in_n", vN1, 0)
            act.wait_ge(gbr_ready, 1)
            for b in range(TB):
                last = A(gates[:, b, :], bank[4 + b][:, 0:48], ACT.Sigmoid)
            last.then_inc(gates_ready, 1)
            act.wait_ge(bank_free[1], B0["in_n"][1])
            act.wait_ge(bank_free[0], B0["in_n"][0])
            A(pT[:, GP0:GP0 + 8, :], pT[:, GP0:GP0 + 8, :], ACT.Silu).then_inc(silu_done, 1)
            A(pT[:, GN0:GN0 + 16, :], pT[:, GN0:GN0 + 16, :], ACT.Silu).then_inc(silu_done, 1)
            act.wait_ge(xn_ready, TB)
            act.wait_ge(turned, 8)
            for j in range(6):
                if j >= 2:
                    act.wait_ge(roped, j - 1)
                tmp = scr[:, (j % 2) * 1024:(j % 2 + 1) * 1024].rearrange("p (j t) -> p j t", t=T)
                src = pT[:, KS0 + 4 * j:KS0 + 4 * j + 4, :]
                A(tmp[0:64], src[64:128], ACT.Copy)
                A(tmp[64:128], src[0:64], ACT.Copy).then_inc(swapped, 1)
            for v in range(2):
                act.wait_ge(slot_used[3], G0["cmp"][0] + v + 1)
                for f in range(2):
                    last = A(hdn[:, v, f, :], bank[4 + 2 * v + f][:, 0:NC4], ACT.Silu)
                last.then_inc(hid_silu, 1)
            act.wait_ge(kc_ready, 1)
            A(kcT, bank[4][:, 0:NC4], ACT.Copy)
            A(kcS[0:64], bank[4][64:128, 0:NC4], ACT.Copy)
            A(kcS[64:128], bank[4][0:64, 0:NC4], ACT.Copy).then_inc(kc_copied, 1)
            act.wait_ge(vc_ready, 1)
            A(vcs, bank[5][0:NCMP, :], ACT.Copy).then_inc(vc_copied, 1)

            def nsa_exp(u):
                a, nk = u % 2, (u % TB + 1) * P
                act.wait_ge(max_ready, u + 1)
                for br in range(2):
                    sl = SP[:, a, br * T:br * T + nk]
                    A(sl, sl, ACT.Exp, bias=ngm[:, a, br:br + 1], scale=SCALE, accum_out=sums[:, a, br:br + 1])
                A(Pc[:, a, 0:NCMP], Pc[:, a, 0:NCMP], ACT.Exp, bias=ngm[:, a, 2:3], scale=SCALE,
                  accum_out=sums[:, a, 2:3]).then_inc(exp_done, 1)

            def nsa_copy(u):
                a, n = u % 2, 2 * (u % TB + 1) * P
                act.wait_ge(probsT_ready, u + 1)
                if u >= 2:
                    act.wait_ge(o_done, u - 1)
                A(PT[:, a, 0:n], bank[6 + a][:, 0:n], ACT.Copy)
                A(PcT[:, a, :], bank[a][0:NCMP, P:2 * P], ACT.Copy).then_inc(probsT_copied, 1)

            units = HQ * TB
            nsa_exp(0)
            for u in range(units):
                if u + 1 < units:
                    nsa_exp(u + 1)
                nsa_copy(u)
            act.wait_ge(o_done, units)
            act.dma_start(fnw1_sb, fnw1.partition_broadcast(P)).then_inc(fnw1_in, 16)
            g0, n = G0["merge"]
            bm = PO["bmerge"][0]
            with act.Fori(0, n) as i:
                for b in range(2):
                    act.wait_ge(slot_used[2 * b + 1], i + g0 + 1)
                    for e in range(2):
                        last = A(R[:, bass.ds(i * (4 * T) + (16 + 2 * b + e) * T, T)], bank[b][:, e * T:(e + 1) * T],
                                 ACT.Sigmoid, bias=par[:, bass.ds(i * 4 + bm + 2 * b + e, 1)])
                    last.then_inc(bank_free[b], 1)

            act.wait_ge(x1_ready, 8)
            squares(1)
            act.wait_ge(x1_normed, TB)
            squares(2)
            act.wait_ge(sm_ready, 1)
            A(smalls, bank[4][:, 0:32].rearrange("p (b c) -> p b c", b=TB), ACT.Copy).then_inc(sm_copied, 1)
            act.wait_ge(row_y, 1)
            A(rows[0:8, 4, :], rows[0:8, 4, :], ACT.Exp).then_inc(act_step, 1)
            A(rows[0:4, 5, :], rows[0:4, 5, :], ACT.Exp).then_inc(act_step, 1)
            act.wait_ge(act_step, 2)
            A(rows[0:8, 4, :], rows[0:8, 4, :], ACT.Ln, bias=1.0)
            A(rows[0:4, 5, :], rows[0:4, 5, :], ACT.Ln, bias=1.0).then_inc(row_l, 1)
            act.wait_ge(a_ready, 1)
            A(rows[0:4, 11, 0:P], rows[0:4, 9, 0:P], ACT.Exp, bias=rowst[0:4, 1:2]).then_inc(rows_ready, 1)
            evac_t("in2_t", 0)
            evac_n("in2_n", vN2, 0)
            act.wait_ge(conv_done, 8)
            A(conv, conv, ACT.Silu).then_inc(conv_silu, 1)
            act.wait_ge(nat_ready, 1)
            A(natc[:, 0:36], bank[4][:, 0:36], ACT.Copy).then_inc(nat_copied, 1)
            act.wait_ge(knat_ready, 1)
            A(knat, bank[5][:].rearrange("p (h d) -> p h d", h=MH), ACT.Copy).then_inc(knat_copied, 1)
            for b in range(4):
                act.wait_ge(bank_free[b], B0["out2"][b])
            A(vN2[:, 4:6], vN2[:, 4:6], ACT.Sigmoid).then_inc(mo_sig, 1)

            def fox_exp(u):
                a, nk = u % 2, (u % TB + 1) * P
                act.wait_ge(f_max, u + 1)
                A(SP[:, a, 0:nk], SP[:, a, 0:nk], ACT.Exp, bias=ngm[:, a, 0:1],
                  accum_out=sums[:, a, 0:1]).then_inc(f_exp, 1)

            def fox_copy(u):
                a, n = u % 2, (u % TB + 1) * P
                act.wait_ge(f_T, u + 1)
                if u >= 2:
                    act.wait_ge(f_o, u - 1)
                A(PT[:, a, 0:n], bank[6 + a][:, 0:n], ACT.Copy).then_inc(f_copied, 1)

            units = FH * TB
            fox_exp(0)
            for u in range(units):
                if u + 1 < units:
                    fox_exp(u + 1)
                fox_copy(u)

            def m_exps(u):
                a = u % 2
                act.wait_ge(m_max, u + 1)
                A(Dm[:, a, :], Dm[:, a, :], ACT.Exp, bias=mst[:, a, 1:2])
                A(mst[:, a, 3:5], mst[:, a, 1:3], ACT.Exp).then_inc(m_exp, 1)

            def m_copy(u):
                a = u % 2
                act.wait_ge(m_T, u + 1)
                if u >= 2:
                    act.wait_ge(m_num, u - 1)
                A(SmT[:, a, :], bank[6 + a][:, 0:P], ACT.Copy).then_inc(m_copied, 1)

            units = MH * TB
            m_exps(0)
            for u in range(units):
                if u + 1 < units:
                    m_exps(u + 1)
                m_copy(u)
            act.wait_ge(cells, 1)
            A(region(0, 4096), scr, ACT.Square).then_inc(head_sq, 1)
            act.wait_ge(head_ms, 1)
            A(hrt, hss, ACT.Sqrt).then_inc(head_rt, 1)
            act.wait_ge(x2_ready, 8)
            squares(3)
            evac_t("wq", 0)
            for f in range(8):
                b, j = divmod(f, 4)
                act.wait_ge(qs_ready, f + 1)
                A(scores[:, b, 4 * j:4 * j + 4, :], bank[4 + j][:].rearrange("p (c n) -> p c n", c=4),
                  ACT.Copy).then_inc(qs_copied, 1)
            for b in range(TB):
                act.wait_ge(gate_arg, b + 1)
                A(finv[:, b], finv[:, b], ACT.Exp).then_inc(gate_exp, 1)
            for b in range(TB):
                act.wait_ge(chosenT, b + 1)
                A(idxT[:, :, b * P:(b + 1) * P], bank[4 + b][:, 0:3 * P].rearrange("p (s t) -> p s t", s=3),
                  ACT.Copy).then_inc(chosenT_copied, 1)
            act.sem_inc(g_evac, 2)
            with act.Fori(0, T // 8) as i:
                for q in range(2):
                    act.wait_ge(pair_free, i * 4 + 2 * q + 4)
                    A(G[:, :, bass.ds(i * 8 + 4 * q, 4)], bank[4 + q][:].rearrange("p (t n) -> p n t", t=4),
                      ACT.Copy).then_inc(g_evac, 1)
            g0, n = G0["peer_u"]
            act.wait_ge(pair_free, 2 + T // 2)
            with act.Fori(0, n) as i:
                for b in range(2):
                    act.wait_ge(slot_used[2 * b + 1], i + g0 + 1)
                    act.wait_ge(gated[b], i + 1)
                    A(gelu_u[:, b, :], bank[b][:], ACT.Gelu).then_inc(bank_free[b], 1)
            act.wait_ge(y_done, 1)
            for b in range(1, 8, 2):
                A(hT[:, 2 * b:2 * b + 2, :], bank[b][:].rearrange("p (c t) -> p c t", c=2), ACT.Copy).then_inc(yT_act, 1)
            act.wait_ge(x3_ready, 8)
            for b in range(TB):
                A(R[:, b * D:(b + 1) * D], xres[:, b, :], ACT.Square, accum_out=ssq[:, b:b + 1]).then_inc(sq_done, 1)
            act.wait_ge(ms_ready, 5)
            A(rt, msq, ACT.Sqrt).then_inc(rt_done, 1)

        @block.gpsimd
        def _(pool):
            step = stepper(pool, pool_step)
            PAD = 16
            W = T + PAD
            bufs = [region(22528 + a * 2 * W, 2 * W).rearrange("p (c t) -> p c t", c=2) for a in range(2)]
            inv = s1("invcnt").rearrange("p (g t) -> p g t", g=NG)
            pool.wait_ge(stage1_in, 16)
            step(nc.gpsimd.memset(region(22528, 4 * W), 0.0))
            for b in range(2):
                pool.wait_ge(bank_free[b], B0["in_t"][b] + 2)
            for g, w in enumerate(WINDOWS):
                u = pT[:, U0 + 2 * g:U0 + 2 * g + 2, :]
                step(nc.gpsimd.tensor_copy(bufs[0][:, :, PAD:], u))
                a, s = 0, 1
                while s < w:
                    step(nc.gpsimd.tensor_tensor(bufs[1 - a][:, :, PAD:], bufs[a][:, :, PAD:],
                                                 bufs[a][:, :, PAD - s:PAD - s + T], ALU.add))
                    a, s = 1 - a, 2 * s
                step(nc.gpsimd.tensor_tensor(bufs[1 - a][:, :, PAD:], bufs[a][:, :, PAD:],
                                             bc(inv[:, g:g + 1, :], [P, 2, T]), ALU.mult))
                nc.gpsimd.tensor_tensor(u, bufs[1 - a][:, :, PAD:], u, ALU.subtract).then_inc(pooled, 1)
                pool.wait_ge(pooled, g + 1)

        @block.vector
        def _(dve):
            step = stepper(dve, dve_step)
            V = nc.vector

            def root_mean_square(m):
                dve.wait_ge(sq_done, TB * (m + 1))
                V.tensor_scalar(msq, ssq, 1.0 / D, EPS, ALU.mult, ALU.add).then_inc(ms_ready, 1)
                dve.wait_ge(rt_done, m + 1)
                step(V.reciprocal(rstd, rt))

            def norm(n, weight, m):
                root_mean_square(m)
                for b in range(TB):
                    V.tensor_scalar(scr2[:, b, :], xres[:, b, :], rstd[:, b:b + 1], None,
                                    ALU.mult).then_inc(xn_ready, 1)
                read_turned(n, weight)

            def read_turned(n, weight):
                for b in range(TB):
                    for j in range(4):
                        dve.wait_ge(turned, 8 * n + 4 * b + j + 1)
                        V.tensor_tensor(hT[:, 4 * j:4 * j + 4, b * P:(b + 1) * P],
                                        bank[4 + j][:].rearrange("p (c t) -> p c t", c=4),
                                        bc(prm(weight, 4 * j, 4 * j + 4).unsqueeze(2), [P, 4, P]),
                                        ALU.mult).then_inc(hT_part, 1)

            def evac_t(name, dst0):
                g0, n = G0[name]
                with dve.Fori(0, n) as i:
                    dve.wait_ge(slot_used[3], i + g0 + 1)
                    V.tensor_copy(R[:, bass.ds(i * (4 * T) + (dst0 + 2) * T, 2 * T)], bank[1][:]).then_inc(bank_free[1], 1)

            def evac_n(name, dst):
                g0, n = G0[name]
                for g in range(n):
                    dve.wait_ge(slot_used[3], g0 + g + 1)
                    V.tensor_copy(dst[:, g, 1, :], bank[2 * (g % 2) + 1][:]).then_inc(bank_free[2 * (g % 2) + 1], 1)

            def residual(name, done):
                g0, n = G0[name]
                for g in range(n):
                    dve.wait_ge(slot_used[3], g0 + g + 1)
                    for b in range(TB):
                        xs = xres[:, b, g * 512:(g + 1) * 512]
                        step(V.tensor_tensor(xs, bank[2 * (g % 2) + b][:], xs, ALU.add))
                        dve.sem_inc(bank_free[2 * (g % 2) + b], 1)
                        dve.sem_inc(done, 1)

            dve.wait_ge(params_in, 16)
            dve.wait_ge(x_in, 16)
            norm(0, "norm1", 0)
            evac_t("in_t", 0)
            evac_n("in_n", vN1)
            for j in range(6):
                dve.wait_ge(swapped, j + 1)
                tmp = scr[:, (j % 2) * 1024:(j % 2 + 1) * 1024].rearrange("p (j t) -> p j t", t=T)
                xb = pT[:, KS0 + 4 * j:KS0 + 4 * j + 4, :]
                step(V.tensor_tensor(tmp, tmp, bc(prm("sin").unsqueeze(1), [P, 4, T]), ALU.mult))
                step(V.tensor_tensor(xb, xb, bc(prm("cos").unsqueeze(1), [P, 4, T]), ALU.mult))
                V.tensor_tensor(xb, xb, tmp, ALU.add).then_inc(roped, 1)
            dve.wait_ge(pooled, NG)
            dve.wait_ge(bank_free[0], B0["in_n"][0])
            for v, (src, pe_name) in enumerate(((KCR0, "pek"), (VCR0, "pev"))):
                raw = pT[:, src:src + 4, :].rearrange("p h (m r) -> p h m r", r=CS)
                for a in range(2):
                    for h in range(HKV):
                        last = V.tensor_tensor(
                            kb[v][:, a * CS:(a + 1) * CS, h * NCMP:(h + 1) * NCMP].rearrange("p r n -> p n r"),
                            raw[:, h, a:a + NCMP, :],
                            bc(prm(pe_name, a * CS, (a + 1) * CS).unsqueeze(1), [P, NCMP, CS]), ALU.add)
                last.then_inc(kb_ready, 1)
            dve.wait_ge(kc_copied, 1)
            step(V.tensor_tensor(kcS, kcS, prm("csin"), ALU.mult))
            step(V.tensor_tensor(kcT, kcT, prm("ccos"), ALU.mult))
            V.tensor_tensor(kcT, kcT, kcS, ALU.add).then_inc(kc_roped, 1)

            def nsa_mask(u):
                qb, a = u % TB, u % 2
                nk = (qb + 1) * P
                dve.wait_ge(scores_ready, u + 1)
                if u >= 2:
                    dve.wait_ge(probsT_ready, u - 1)
                s3 = SP[:, a, :].rearrange("p (r k) -> p r k", r=2)[:, :, 0:nk]
                m3 = prm("mask", 256 - nk, 256)
                V.tensor_tensor(s3, bank[4 + a][:].rearrange("p (r k) -> p r k", r=2)[:, :, 0:nk],
                                bc(m3.unsqueeze(1), [P, 2, nk]), ALU.add)
                step(V.tensor_tensor(Pc[:, a, 0:NCMP], bank[a][:, 0:NCMP],
                                     prm("cmask", qb * NCMP, (qb + 1) * NCMP), ALU.add))
                V.tensor_reduce(mx[:, a, 0:2], s3, AX.X, ALU.max).then_inc(scores_read, 1)
                step(V.tensor_reduce(mx[:, a, 2:3], Pc[:, a, 0:NCMP], AX.X, ALU.max))
                V.tensor_scalar(ngm[:, a, 0:3], mx[:, a, 0:3], -SCALE, None, ALU.mult).then_inc(max_ready, 1)

            def nsa_scale(u):
                h, qb = divmod(u, TB)
                a, nk = u % 2, (qb + 1) * P
                dve.wait_ge(exp_done, u + 1)
                step(V.reciprocal(rz[:, a, 0:3], sums[:, a, 0:3]))
                step(V.tensor_tensor(gz[:, a, 0:3], rz[:, a, 0:3], gates_for(h, qb), ALU.mult))
                for br in range(2):
                    sl = SP[:, a, br * T:br * T + nk]
                    V.tensor_scalar(sl, sl, gz[:, a, br:br + 1], None, ALU.mult)
                V.scalar_tensor_tensor(out=Pc[:, a, 0:NCMP], in0=Pc[:, a, 0:NCMP], scalar=gz[:, a, 2:3],
                                       in1=prm("cvalid", qb * NCMP, (qb + 1) * NCMP),
                                       op0=ALU.mult, op1=ALU.mult).then_inc(probs_ready, 1)

            def gates_for(h, qb):
                return gates[:, qb, 3 * h:3 * h + 3]

            def nsa_out(h):
                dve.wait_ge(o_done, 2 * h + 2)
                g = pT[:, GN0 + h, :]
                V.tensor_tensor(g, bank[2 + h % 2][:, 0:T], g, ALU.mult).then_inc(o_read, 1)

            units = HQ * TB
            dve.wait_ge(gates_ready, 1)
            dve.wait_ge(silu_done, 2)
            nsa_mask(0)
            for u in range(units):
                if u + 1 < units:
                    nsa_mask(u + 1)
                nsa_scale(u)
                if u % 2 == 1 and u >= 3:
                    nsa_out(u // 2 - 1)
            nsa_out(HQ - 1)
            for g in range(NG):
                dve.wait_ge(z_ready, g + 1)
                for e in range(2):
                    c = 2 * g + e
                    last = V.scalar_tensor_tensor(out=pT[:, U0 + c, :], in0=bank[4 + g][:, e * T:(e + 1) * T],
                                                  scalar=prm("pscale", c, c + 1), in1=pT[:, GP0 + c, :],
                                                  op0=ALU.mult, op1=ALU.mult)
                last.then_inc(y_pool, 1)
            g0, n = G0["pool_out"]
            dve.wait_ge(bank_free[0], B0["pool_out"][0])
            dve.wait_ge(bank_free[1], B0["pool_out"][1])
            with dve.Fori(0, n) as i:
                for s in range(RING):
                    dve.wait_ge(slot_used[s], i + g0 + 1)
                    gsl = R[:, bass.ds(i * (8 * T) + (16 + 2 * s) * T, 2 * T)]
                    V.tensor_tensor(gsl, bank[s][:], gsl, ALU.mult).then_inc(bank_free[s], 1)
            for s in range(RING):
                dve.wait_ge(bank_free[s], B0["nsa_out"][s])
            g0, n = G0["nsa_out"]
            with dve.Fori(0, n) as i:
                for b in range(2):
                    dve.wait_ge(slot_used[2 * b + 1], i + g0 + 1)
                    g1 = R[:, bass.ds(i * (4 * T) + (32 + 2 * b) * T, 2 * T)]
                    gm = R[:, bass.ds(i * (4 * T) + (16 + 2 * b) * T, 2 * T)]
                    V.tensor_tensor(g1, bank[b][:], g1, ALU.mult).then_inc(bank_free[b], 1)
                    dve.wait_ge(bank_free[b], i + B0["nsa_out"][b] + 1)
                    V.tensor_tensor(gm, gm, g1, ALU.add).then_inc(merged_ready, 1)
            residual("out1", x1_ready)
            root_mean_square(1)
            dve.wait_ge(fnw1_in, 16)
            for b in range(TB):
                V.scalar_tensor_tensor(out=xres[:, b, :], in0=xres[:, b, :], scalar=rstd[:, b:b + 1],
                                       in1=fnw1_sb, op0=ALU.mult, op1=ALU.mult).then_inc(x1_normed, 1)

            norm(1, "norm2", 2)
            dve.wait_ge(rowsT_ready, 1)
            V.tensor_scalar(rows[0:8, 0, :], bank[5][0:8, 0:T], prm_rows("fbias", 8), None, ALU.add)
            V.tensor_scalar(rows[0:4, 1, :], bank[6][0:4, 0:T], prm_rows("ibias", 4), None, ALU.add)
            step(V.tensor_scalar(rows[0:4, 2, :], bank[7][0:4, 0:T], prm_rows("mfbias", 4), None, ALU.add))
            step(V.tensor_scalar(rows[0:8, 4, :], rows[0:8, 0, :], -1.0, None, ALU.mult))
            step(V.tensor_scalar(rows[0:4, 5, :], rows[0:4, 2, :], -1.0, None, ALU.mult))
            V.tensor_tensor(rows[0:8, 4, :], rows[0:8, 4, :], rows[0:8, 0, :], ALU.min)
            V.tensor_tensor(rows[0:4, 5, :], rows[0:4, 5, :], rows[0:4, 2, :], ALU.min).then_inc(row_y, 1)
            V.tensor_scalar(rows[0:8, 0, :], rows[0:8, 0, :], 0.0, None, ALU.min)
            step(V.tensor_scalar(rows[0:4, 2, :], rows[0:4, 2, :], 0.0, None, ALU.min))
            dve.wait_ge(row_l, 1)
            V.tensor_tensor(rows[0:8, 0, :], rows[0:8, 0, :], rows[0:8, 4, :], ALU.subtract)
            step(V.tensor_tensor(rows[0:4, 2, :], rows[0:4, 2, :], rows[0:4, 5, :], ALU.subtract))
            ones8 = bc(prm_rows("cone", 8), [8, T])
            V.tensor_tensor_scan(rows[0:8, 6, :], ones8, rows[0:8, 0, :], 0.0, ALU.mult, ALU.add)
            for c in range(TB):
                cs = slice(c * P, (c + 1) * P)
                last = V.tensor_tensor_scan(rows[0:4, 8, cs], bc(prm_rows("cone", 4), [4, P]), rows[0:4, 2, cs], 0.0,
                                            ALU.mult, ALU.add)
            step(last)
            V.tensor_scalar(rows[0:8, 7, :], rows[0:8, 6, :], -1.0, None, ALU.mult)
            step(V.tensor_tensor(rows[0:4, 9, :], rows[0:4, 1, :], rows[0:4, 8, :], ALU.subtract))
            bl = rows[0:4, 8, P - 1:P]
            step(V.tensor_reduce(rowst[0:4, 0:1], rows[0:4, 9, 0:P], AX.X, ALU.max))
            step(V.tensor_tensor(rowst[0:4, 0:1], rowst[0:4, 0:1], bl, ALU.add))
            step(V.tensor_tensor(rowst[0:4, 2:3], rowst[0:4, 0:1], bl, ALU.max))
            V.tensor_copy(rows[0:4, 10, 0:P], rows[0:4, 8, 0:P])
            V.tensor_scalar(rows[0:4, 10, P:T], rows[0:4, 8, P:T], rowst[0:4, 2:3], None, ALU.add)
            V.tensor_tensor(rowst[0:4, 1:2], bl, rowst[0:4, 2:3], ALU.subtract).then_inc(a_ready, 1)
            evac_t("in2_t", 0)
            evac_n("in2_n", vN2)
            dve.wait_ge(bank_free[0], B0["in2_n"][0])
            for j in range(8):
                src, y = pT[:, MQ0 + j, :], conv[:, j, :]
                cw = prm("convw", 4 * j, 4 * j + 4)
                step(V.tensor_scalar(y, src, cw[:, 3:4], prm("convb", j, j + 1), ALU.mult, ALU.add))
                for tap in range(3):
                    sh = 3 - tap
                    last = V.scalar_tensor_tensor(out=y[:, sh:T], in0=src[:, 0:T - sh], scalar=cw[:, tap:tap + 1],
                                                  in1=y[:, sh:T], op0=ALU.mult, op1=ALU.add)
                    if tap < 2:
                        step(last)
                last.then_inc(conv_done, 1)
            V.tensor_scalar(pT[:, FQ0:FQ0 + 8, :], pT[:, FQ0:FQ0 + 8, :], SCALE, None, ALU.mult).then_inc(q_ready, 1)
            dve.wait_ge(conv_silu, 1)
            V.tensor_scalar(conv[:, 4:8, :], conv[:, 4:8, :], SCALE, None, ALU.mult).then_inc(q_ready, 1)
            dve.wait_ge(nat_copied, 1)
            dve.wait_ge(bank_free[0], B0["out2"][0])
            dve.wait_ge(bank_free[2], B0["out2"][2])
            for h in range(MH):
                a_col = natc[:, 32 + h:33 + h]
                if h >= 1:
                    dve.wait_ge(C_ready, h)
                V.tensor_scalar(av[:, 0:MV], vN2[:, 2 + h // 2, 0, (h % 2) * MV:(h % 2 + 1) * MV], a_col, None, ALU.mult)
                V.tensor_copy(av[:, MV:MV + 1], a_col).then_inc(av_ready, 1)
                dve.wait_ge(C_ready, h + 1)
                V.tensor_copy(CN[:, h, 0:MV + 1], bank[6][:, 0:MV + 1]).then_inc(C_copied, 1)

            def fox_mask(u):
                h, qb = divmod(u, TB)
                a, nk = u % 2, (qb + 1) * P
                dve.wait_ge(f_scores, u + 1)
                if u >= 2:
                    dve.wait_ge(f_T, u - 1)
                V.scalar_tensor_tensor(out=SP[:, a, 0:nk], in0=bank[4 + a][:, 0:nk],
                                       scalar=natc[:, 8 * qb + h:8 * qb + h + 1], in1=prm("mask", 256 - nk, 256),
                                       op0=ALU.add, op1=ALU.add).then_inc(f_read, 1)
                dve.wait_ge(f_read, u + 1)
                step(V.tensor_reduce(mx[:, a, 0:1], SP[:, a, 0:nk], AX.X, ALU.max))
                V.tensor_scalar(ngm[:, a, 0:1], mx[:, a, 0:1], -1.0, None, ALU.mult).then_inc(f_max, 1)

            def fox_out(u):
                h, qb = divmod(u, TB)
                a = u % 2
                dve.wait_ge(f_exp, u + 1)
                step(V.reciprocal(rz[:, a, 0:1], sums[:, a, 0:1]))
                dve.wait_ge(f_o, u + 1)
                V.tensor_scalar(scr2[:, qb, h * DH:(h + 1) * DH], bank[2 + a][:, 0:DH], rz[:, a, 0:1], None,
                                ALU.mult).then_inc(f_oread, 1)

            units = FH * TB
            fox_mask(0)
            for u in range(units):
                if u + 1 < units:
                    if u >= 1:
                        fox_out(u - 1)
                    fox_mask(u + 1)
            fox_out(units - 2)
            fox_out(units - 1)

            def m_mask(u):
                c, h = divmod(u, MH)
                a = u % 2
                dve.wait_ge(m_scores, u + 1)
                g_col = natc[:, 24 + 4 * c + h:25 + 4 * c + h]
                step(V.scalar_tensor_tensor(out=Dm[:, a, :], in0=bank[4 + a][:, P:2 * P],
                                            scalar=natc[:, 16 + 4 * c + h:17 + 4 * c + h], in1=tri,
                                            op0=ALU.add, op1=ALU.add))
                step(V.tensor_reduce(mst[:, a, 0:1], Dm[:, a, :], AX.X, ALU.max))
                step(V.tensor_tensor(mst[:, a, 0:1], mst[:, a, 0:1], g_col, ALU.max))
                V.tensor_scalar(mst[:, a, 1:2], mst[:, a, 0:1], -1.0, None, ALU.mult)
                V.tensor_tensor(mst[:, a, 2:3], g_col, mst[:, a, 0:1], ALU.subtract).then_inc(m_max, 1)

            def m_weigh(u):
                a = u % 2
                dve.wait_ge(m_exp, u + 1)
                if u >= 2:
                    dve.wait_ge(m_T, u - 1)
                V.tensor_tensor_reduce(Sm[:, a, :], bank[4 + a][:, 0:P], Dm[:, a, :], 1.0, 0.0, ALU.mult, ALU.add,
                                       mst[:, a, 5:6]).then_inc(m_sm, 1)

            def m_out(u):
                c, h = divmod(u, MH)
                a = u % 2
                dve.wait_ge(m_num, u + 1)
                dve.wait_ge(m_sm, u + 1)
                if c == 1:
                    step(V.tensor_scalar(numt[:, a, :], bank[a][:, 0:MV], mst[:, a, 4:5], None, ALU.mult))
                    V.scalar_tensor_tensor(out=mst[:, a, 5:6], in0=bank[a][:, MV:MV + 1], scalar=mst[:, a, 4:5],
                                           in1=mst[:, a, 5:6], op0=ALU.mult, op1=ALU.add)
                    step(V.tensor_tensor(numt[:, a, :], bank[2 + a][:, 0:MV], numt[:, a, :], ALU.add))
                else:
                    step(V.tensor_copy(numt[:, a, :], bank[2 + a][:, 0:MV]))
                step(V.tensor_scalar(mst[:, a, 6:7], mst[:, a, 5:6], -1.0, None, ALU.mult))
                step(V.tensor_tensor(mst[:, a, 6:7], mst[:, a, 6:7], mst[:, a, 5:6], ALU.max))
                step(V.tensor_tensor(mst[:, a, 6:7], mst[:, a, 6:7], mst[:, a, 3:4], ALU.max))
                step(V.reciprocal(mst[:, a, 7:8], mst[:, a, 6:7]))
                V.tensor_scalar(scr2[:, c, 1024 + h * MV:1024 + (h + 1) * MV], numt[:, a, :], mst[:, a, 7:8], None,
                                ALU.mult).then_inc(m_read, 1)

            units = MH * TB
            m_mask(0)
            m_weigh(0)
            for u in range(units):
                if u + 1 < units:
                    m_mask(u + 1)
                    m_weigh(u + 1)
                m_out(u)
            dve.wait_ge(mo_sig, 1)
            dve.wait_ge(m_read, units)
            for b in range(TB):
                for g in range(2):
                    sl = scr2[:, b, 1024 + g * 512:1024 + (g + 1) * 512]
                    last = V.tensor_tensor(sl, sl, vN2[:, 4 + g, b, :], ALU.mult)
            last.then_inc(cells, 1)
            dve.wait_ge(head_sq, 1)
            sq = region(0, 4096).rearrange("p (b d) -> p b d", b=TB)
            for b in range(TB):
                V.tensor_reduce(hss[:, b, 0:8], sq[:, b, 0:1024].rearrange("p (h e) -> p h e", h=FH), AX.X, ALU.add)
                last = V.tensor_reduce(hss[:, b, 8:12], sq[:, b, 1024:2048].rearrange("p (h e) -> p h e", h=MH), AX.X,
                                       ALU.add)
            step(last)
            V.tensor_scalar(hss[:, :, 0:8], hss[:, :, 0:8], 1.0 / DH, EPS, ALU.mult, ALU.add)
            V.tensor_scalar(hss[:, :, 8:12], hss[:, :, 8:12], 1.0 / MV, EPS, ALU.mult, ALU.add).then_inc(head_ms, 1)
            dve.wait_ge(head_rt, 1)
            step(V.reciprocal(hrt, hrt))
            for b in range(TB):
                fa = scr2[:, b, 0:1024].rearrange("p (h e) -> p h e", h=FH)
                ce = scr2[:, b, 1024:2048].rearrange("p (h e) -> p h e", h=MH)
                V.tensor_tensor(fa, fa, bc(hrt[:, b, 0:8].unsqueeze(2), [P, FH, DH]), ALU.mult)
                V.tensor_tensor(ce, ce, bc(hrt[:, b, 8:12].unsqueeze(2), [P, MH, MV]), ALU.mult).then_inc(xn_ready, 1)
            read_turned(2, "mixnorm")
            residual("out2", x2_ready)

            norm(3, "norm3", 3)
            evac_t("wq", 0)
            for f in range(8):
                b, j = divmod(f, 4)
                dve.wait_ge(qs_copied, f + 1)
                for hp in range(4 * j, 4 * j + 4):
                    sc, wk = scores[:, b, hp, :], work[:, b, hp, :]
                    tv, ti = topv[:, b, hp, :], topi[:, b, hp, :]
                    step(V.max(tv[:, 0:8], sc))
                    V.max_index(ti[:, 0:8], tv[:, 0:8], sc)
                    step(V.match_replace(wk, tv[:, 0:8], sc, LOWEST))
                    step(V.max(tv[:, 8:16], wk))
                    last = V.max_index(ti[:, 8:16], tv[:, 8:16], wk)
            step(last)
            step(V.tensor_copy(topf, topi))
            for b in range(TB):
                tv4 = topv[:, b].rearrange("p (h s) k -> p h s k", s=2)
                c4 = cand[:, b].rearrange("p h (i j) -> p h i j", i=TOPK)
                step(V.tensor_tensor(c4, bc(tv4[:, :, 0, :].unsqueeze(3), [P, PH, TOPK, TOPK]),
                                     bc(tv4[:, :, 1, :].unsqueeze(2), [P, PH, TOPK, TOPK]), ALU.add))
                for h in range(PH):
                    cd, wk = cand[:, b, h, :], cwork[:, b, h, :]
                    tv, ti = finv[:, b, h, :], fini[:, b, h, :]
                    step(V.max(tv[:, 0:8], cd))
                    V.max_index(ti[:, 0:8], tv[:, 0:8], cd)
                    step(V.match_replace(wk, tv[:, 0:8], cd, LOWEST))
                    step(V.max(tv[:, 8:16], wk))
                    last = V.max_index(ti[:, 8:16], tv[:, 8:16], wk)
                step(last)
                pos = fini[:, b].rearrange("p h k -> p (h k)")
                V.tensor_scalar(fab_u[:, 0, b, :], pos, 4, None, ALU.logical_shift_right)
                step(V.tensor_scalar(fab_u[:, 1, b, :], pos, 15, None, ALU.bitwise_and))
                for s in range(2):
                    last = V.tensor_copy(fab[:, s, b].rearrange("p h k -> p (h k)"), fab_u[:, s, b, :])
                step(last)
                step(V.tensor_copy(zs[:, b, :], finv[:, b, :, 0]))
                V.tensor_tensor(finv[:, b], finv[:, b], bc(zs[:, b, :].unsqueeze(2), [P, PH, TOPK]),
                                ALU.subtract).then_inc(gate_arg, 1)
                tf4 = topf[:, b].rearrange("p (h s) k -> p h s k", s=2)
                for s in range(2):
                    step(V.tensor_tensor(onehot, bc(fab[:, s, b].unsqueeze(3), [P, PH, TOPK, TOPK]),
                                         bc(prm("iota", 0, TOPK).unsqueeze(1).unsqueeze(1), [P, PH, TOPK, TOPK]),
                                         ALU.is_equal))
                    step(V.tensor_tensor(onehot, onehot, bc(tf4[:, :, s, :].unsqueeze(2), [P, PH, TOPK, TOPK]),
                                         ALU.mult))
                    step(V.tensor_reduce(chosen[:, b, s, :].rearrange("p (h k) -> p h k", h=PH), onehot, AX.X, ALU.add))
                dve.wait_ge(gate_exp, b + 1)
                step(V.tensor_reduce(zs[:, b, :], finv[:, b], AX.X, ALU.add))
                step(V.reciprocal(zs[:, b, :], zs[:, b, :]))
                V.tensor_tensor(chosen[:, b, 2, :].rearrange("p (h k) -> p h k", h=PH), finv[:, b],
                                bc(zs[:, b, :].unsqueeze(2), [P, PH, TOPK]), ALU.mult).then_inc(chosen_ready, 1)
            dve.wait_ge(chosenT_copied, TB)
            with dve.Fori(0, T // 8) as i:
                for q in range(4):
                    dve.wait_ge(pair_free, i * 4 + q + 1)
                    for t in range(2):
                        def col(s):
                            return idxT[:, s, bass.ds(i * 8 + 2 * q + t, 1)]
                        V.tensor_scalar(pairs[:, q % 2, t, 0, :], prm("iota"), col(1), None, ALU.is_equal)
                        last = V.tensor_scalar(pairs[:, q % 2, t, 1, :], prm("iota"), col(0), col(2),
                                               ALU.is_equal, ALU.mult)
                    last.then_inc(pair_ready, 1)
            dve.wait_ge(g_evac, 2 + T // 4)
            g0, n = G0["peer_u"]
            with dve.Fori(0, n) as i:
                for b in range(2):
                    dve.wait_ge(bank_free[b], i + B0["peer_u"][b] + 1)
                    gsl = R[:, bass.ds(i * (4 * T) + 2 * b * T, 2 * T)]
                    V.tensor_tensor(gsl, gsl, gelu_u[:, b, :], ALU.mult).then_inc(gated[b], 1)
            for b in range(2):
                dve.wait_ge(gated[b], n + 1)
            V.memset(gelu_u[:, 0, :], 0.0).then_inc(zeros_ready, 1)
            dve.wait_ge(y_done, 1)
            for b in range(0, 8, 2):
                V.tensor_copy(hT[:, 2 * b:2 * b + 2, :], bank[b][:].rearrange("p (c t) -> p c t", c=2)).then_inc(yT_dve, 1)
            for f in range(8):
                b, j = divmod(f, 4)
                dve.wait_ge(y_turned, f + 1)
                xs = xres[:, b, j * 512:(j + 1) * 512]
                V.tensor_tensor(xs, bank[f][:], xs, ALU.add).then_inc(x3_ready, 1)
            root_mean_square(4)
            dve.wait_ge(fnw_in, 16)
            for b in range(TB):
                V.scalar_tensor_tensor(out=R[:, b * D:(b + 1) * D], in0=xres[:, b, :], scalar=rstd[:, b:b + 1],
                                       in1=ring[0][:], op0=ALU.mult, op1=ALU.mult).then_inc(result, 1)


PARAMS.append(("cone", 1))


def cols_t(w):
    k, n = w.shape
    return w.reshape(k // P, P, n // P, P).transpose(2, 1, 0, 3).reshape(n // P, P, k)


def cols_n(w):
    n = w.shape[1]
    return w.reshape(4, 4, P, n // 512, 512).transpose(3, 0, 2, 1, 4).reshape(n // 512 * 4, P, SLOT)


def on_partitions(v):
    return v.reshape(-1, P).T


def layout(i):
    f = np.float32
    cut = np.cumsum([0, POOL_W, POOL_W, 2048, 512, 512, 512, 512, 512, 512, 2048, 48])
    w1 = i["w_in"][0]
    part = [w1[:, a:b] for a, b in zip(cut[:-1], cut[1:])]
    u, gp, q, kcr, vcr, ks, vs, kw, vw, gn, gb = part
    cut2 = np.cumsum([0, 1024, 1024, 1024, 8, 512, 512, 1024, 4, 4, 1024])
    fq, fk, fv, ff, mq, mk, mv, mi, mf, mo = [i["w_in_2"][0][:, a:b] for a, b in zip(cut2[:-1], cut2[1:])]

    def cmp_w1(w):
        return w[0].reshape(RING, 8, P, CH).transpose(0, 2, 1, 3).reshape(RING, P, SLOT)

    pool_out = cols_t(i["w_pool_out"][0]).reshape(8, 2, P, 1024).transpose(0, 2, 1, 3).reshape(8, P, SLOT)
    stream = np.concatenate([
        *(cols_t(w) for w in (u, gp, kcr, vcr, ks, kw, q, gn)), cols_n(vs), cols_n(vw),
        cmp_w1(i["cmp_w1_k"]), cmp_w1(i["cmp_w1_v"]), cols_t(i["w_merge"][0]), pool_out,
        cols_t(i["w_nsa_out"][0]), cols_n(i["w_out"][0]),
        *(cols_t(w) for w in (fq, fk, mq, mk)), *(cols_n(w) for w in (fv, mv, mo)),
        cols_n(i["w_out_2"][0]), cols_t(i["peer_w_q_2"][0]),
        i["peer_u_2"][0].reshape(NK, P, KC, P).transpose(0, 3, 2, 1).reshape(NK, P, SLOT),
        i["peer_v_2"][0].reshape(NK, P, SLOT)])

    t = np.arange(T)
    inv = (f(10000.0) ** (-np.arange(64, dtype=f) / f(64))).astype(f)

    def rot(pos):
        ang = (pos.astype(f)[None, :] * inv[:, None]).astype(f)
        c, s = np.cos(ang), np.sin(ang)
        return np.concatenate([c, c]).astype(f), np.concatenate([-s, s]).astype(f)

    cos, sin = rot(t)
    ccos, csin = (np.tile(a, (1, HKV)) for a in rot(np.arange(NCMP) * CS + CB - 1))
    tri = np.where(np.arange(P)[None, :] <= np.arange(P)[:, None], 0, NEG)
    valid = (np.arange(NCMP) * CS + CB - 1)[None, :] <= t[:, None]
    per_block = lambda a: a.reshape(TB, P, NCMP).transpose(1, 0, 2).reshape(P, TB * NCMP)
    table = {
        "ident": np.eye(P), "mask": np.concatenate([np.zeros((P, P)), tri], 1), "cos": cos, "sin": sin,
        "ccos": ccos, "csin": csin, "cmask": per_block(np.where(valid | ~valid.any(1, keepdims=True), 0, NEG)), "cvalid": per_block(valid),
        "iota": np.tile(np.arange(P), (P, 1)), "cone": np.ones((P, 1)),
        "norm1": on_partitions(i["norm_w"][0]), "norm2": on_partitions(i["norm1_w_2"][0]),
        "norm3": on_partitions(i["norm2_w_2"][0]),
        "mixnorm": on_partitions(np.concatenate([i["fox_out_norm_w_2"][0], i["mlstm_out_norm_w_2"][0]])),
        "pscale": on_partitions(i["pool_scale"][0]), "bmerge": on_partitions(i["b_merge"][0]),
        "pek": i["cmp_pe_k"][0].T, "pev": i["cmp_pe_v"][0].T,
        "convw": i["mlstm_conv_w_2"][0].reshape(4, 8, P).transpose(2, 1, 0).reshape(P, 32),
        "convb": on_partitions(i["mlstm_conv_b_2"][0]),
        "fbias": i["fox_f_bias_2"][0][:, None], "ibias": i["mlstm_i_bias_2"][0][:, None],
        "mfbias": i["mlstm_f_bias_2"][0][:, None],
        "keysT": i["peer_keys_2"][0].transpose(2, 0, 1).reshape(P, 2 * NK),
        "wrows": np.concatenate([ff, mi, mf], 1).reshape(KC, P, 16).transpose(1, 0, 2).reshape(P, KC * 16),
    }
    cnt = np.minimum(t[None, :] + 1, np.array(WINDOWS)[:, None]).astype(f)
    gb3 = gb.reshape(D, HQ, 3)[:, :, [1, 2, 0]].reshape(KC, P, 48)
    table1 = {
        "mixw": i["pool_mix"][0].reshape(NG, 2, P, 256).transpose(2, 0, 1, 3).reshape(P, 2048),
        "invcnt": np.tile((f(1) / cnt).reshape(1, NG * T), (P, 1)),
        "wgbr": gb3.transpose(1, 0, 2).reshape(P, KC * 48),
        "w2k": i["cmp_w2_k"][0].reshape(2, P, DH).transpose(1, 0, 2).reshape(P, 2 * DH),
        "w2v": i["cmp_w2_v"][0].reshape(2, P, DH).transpose(1, 0, 2).reshape(P, 2 * DH),
    }

    def packed(names, values):
        off, n = offsets(names)
        a = np.zeros((P, n), f)
        for name, (o, w) in off.items():
            v = values[name]
            assert v.shape[1] == w, name
            a[:v.shape[0], o:o + w] = v
        return a

    return {"x": i["x"], "stream": stream, "params": packed(PARAMS, table), "stage1": packed(STAGE1, table1),
            "fnw1": i["final_norm_w"], "fnw": i["final_norm_w_2"]}


def kernel(**inputs):
    import concourse.bacc as bacc
    from concourse.bass_utils import run_bass_kernel_spmd

    arrays = {n: np.ascontiguousarray(a) for n, a in layout({k: np.asarray(v) for k, v in inputs.items()}).items()}
    nc = bacc.Bacc("TRN2", target_bir_lowering=False, num_devices=1)
    args = [nc.dram_tensor(n, a.shape, F32, kind="ExternalInput").ap() for n, a in arrays.items()]
    out = nc.dram_tensor("out", (1, T, D), F32, kind="ExternalOutput").ap()
    build_two_blocks(nc, *args, out)
    r = run_bass_kernel_spmd(nc, [arrays], core_ids=[0])
    return r.results[0]["out"]
```

```python
from contextlib import ExitStack

import numpy as np

import concourse.bass as bass
from concourse import mybir

ALU = mybir.AluOpType
ACT = mybir.ActivationFunctionType
AX = mybir.AxisListType
F32 = mybir.dt.float32
F32R = mybir.dt.float32r
U32 = mybir.dt.uint32

P = 128
T = 256
TB = T // P
D = 2048
KC = D // P
EPS = 1e-6
NEG = -1e30
LOWEST = -3.0e38
RING = 4
SLOT = 2048

POOL_W = 1024
WINDOWS = (2, 4, 8, 16)
NG = len(WINDOWS)
HQ, HKV, DH = 16, 4, 128
GQ = HQ // HKV
CB, CS, CH = 32, 16, 256
NCMP = (T - CB) // CS + 1
NC4 = HKV * NCMP
FH = 8
MH, MV = 4, 256
PH, NK, TOPK = 8, 128, 16
HK = PH * TOPK
NE_BLOCKS = NK

SCALE = float(DH) ** -0.5

PHASES = [("in_t", 16), ("in_n", 2), ("cmp", 2), ("merge", 8), ("pool_out", 2), ("nsa_out", 4),
          ("out1", 4), ("in2_t", 6), ("in2_n", 6), ("out2", 4), ("wq", 4),
          ("peer_u0", 16), ("peer_v0", 16), ("peer_u1", 16), ("peer_v1", 16)]
RAW = ("cmp", "pool_out", "nsa_out", "out1")
HALF = NK // 2
GROUPS = sum(n for _, n in PHASES)

PARAMS = [("ident", 128), ("mask", 256), ("cos", 256), ("sin", 256), ("ccos", NC4), ("csin", NC4),
          ("cmask", TB * NCMP), ("cvalid", TB * NCMP), ("iota", 128),
          ("norm1", KC), ("norm2", KC), ("norm3", KC), ("mixnorm", KC), ("pscale", 8), ("bmerge", 32),
          ("pek", CB), ("pev", CB), ("convw", 32), ("convb", 8), ("fbias", 1), ("ibias", 1), ("mfbias", 1),
          ("keysT", 2 * NK), ("wrows", KC * 16)]
STAGE1 = [("invcnt", NG * 16), ("wgbr", KC * 48), ("w2k", 2 * DH), ("w2v", 2 * DH)]
R_WORDS = 25088


def offsets(table):
    at, out = 0, {}
    for name, width in table:
        out[name] = (at, width)
        at += width
    return out, at


def first_groups():
    at, out = 0, {}
    for name, n in PHASES:
        out[name] = (at, n)
        at += n
    return out


def split_groups():
    at, out = 0, {}
    for name, n in PHASES:
        out[name] = at
        at += 0 if name in RAW else n
    return out


def fills_per_bank(name, n):
    if name in ("in_t", "merge", "nsa_out", "in2_t", "wq", "peer_u0", "peer_u1"):
        return (n, n, 0, 0)
    if name in ("in_n", "out1", "in2_n", "out2"):
        return (n // 2,) * 4
    if name == "pool_out":
        return (n,) * 4
    return (0,) * 4


def earlier_fills():
    at, out = [1] * 4, {}
    for name, n in PHASES:
        out[name] = tuple(at)
        at = [a + f for a, f in zip(at, fills_per_bank(name, n))]
    return out


def build_two_blocks(nc, x, stream, params, stage1, mixw_in, fnw1, fnw, gates_dram, out):
    PO, n_params = offsets(PARAMS)
    S1, n_stage1 = offsets(STAGE1)
    G0 = first_groups()
    B0 = earlier_fills()
    S0 = split_groups()

    with ExitStack() as ctx:
        def sb(name, shape, dt=F32):
            return ctx.enter_context(nc.sbuf_tensor(name, shape, dt))

        def sem(name):
            return ctx.enter_context(nc.semaphore(name))

        bank = [ctx.enter_context(nc.psum_tensor(f"bank{b}", [P, 512], F32)) for b in range(8)]

        raw = [sb(f"raw{s}", [P, SLOT]) for s in range(2)]
        whi = [sb(f"whi{s}", [P, SLOT], F32R) for s in range(2)]
        wlo = [sb(f"wlo{s}", [P, SLOT], F32R) for s in range(2)]
        xres = sb("xres", [P, TB, D])
        hTh = sb("hTh", [P, KC, T], F32R)
        hTl = sb("hTl", [P, KC, T], F32R)
        ghi = sb("ghi", [P, 2, T], F32R)
        glo = sb("glo", [P, 2, T], F32R)
        par = sb("par", [P, n_params])
        R = sb("R", [P, R_WORDS])
        st = sb("st", [P, 320])

        def prm(name, a=0, b=None):
            o, w = PO[name]
            return par[:, o + a:o + (w if b is None else b)]

        def prm_rows(name, n):
            o, _ = PO[name]
            return par[0:n, o:o + 1]

        def region(a, n):
            return R[:, a:a + n]

        ident = prm("ident")
        tri = prm("mask", 128, 256)

        pT = region(0, 64 * T).rearrange("p (j t) -> p j t", t=T)
        U0, GP0, KCR0, VCR0, KS0, KW0, Q0, GN0 = 0, 8, 16, 20, 24, 28, 32, 48
        kb_at = (16384, 18304)
        kb = [region(a, CB * NC4).rearrange("p (l c) -> p l c", l=CB) for a in kb_at]
        PAD = 16
        W = T + PAD
        pool_buf = [region(16384 + a * 2 * W, 2 * W).rearrange("p (c t) -> p c t", c=2) for a in range(2)]
        vN1_at = 20224
        vN1 = region(vN1_at, 2048).rearrange("p (g b c) -> p g b c", g=2, b=TB)
        fnw1_sb = region(vN1_at, D)
        rot_buf = region(24064, 1024)
        mixw_sb = region(16 * T, 2048)
        stage1_at = 22272
        tmp_at = 24064
        turned_tmp = region(tmp_at, 1024).rearrange("p (a k) -> p a k", a=2)
        scr_of = [region(a, 4096) for a in (12288, 12288, 17408, 17408)]
        scr = scr_of[2]
        scr2 = scr.rearrange("p (b d) -> p b d", b=TB)
        SP = region(17552, 1024).rearrange("p (a k) -> p a k", a=2)
        PT = region(18576, 1024).rearrange("p (a k) -> p a k", a=2)

        def s1(name):
            o, w = S1[name]
            return region(stage1_at + o, w)
        k0 = kb_at[0]
        vcs = R[0:NCMP, k0:k0 + 512]
        kcT = region(k0 + 512, NC4)
        kcS = region(k0 + 576, NC4)
        PcT = R[0:NCMP, k0 + 640:k0 + 896].rearrange("p (a q) -> p a q", a=2)
        Pc = region(k0 + 896, 32).rearrange("p (a k) -> p a k", a=2)
        hdn = region(k0 + 928, 4 * NC4).rearrange("p (v f c) -> p v f c", v=2, f=2)
        assert k0 + 928 + 4 * NC4 <= 17552 and stage1_at + n_stage1 <= tmp_at
        gate0 = pT[:, 16:32, :]
        gate1 = pT[:, 32:48, :]

        FQ0, FK0, MQ0, MK0 = 0, 8, 16, 20
        vN2 = region(6144, 6144).rearrange("p (g b c) -> p g b c", g=6, b=TB)
        conv = region(12288, 2048).rearrange("p (j t) -> p j t", t=T)
        SP2 = region(4096, 1024).rearrange("p (a k) -> p a k", a=2)
        PT2 = region(5120, 1024).rearrange("p (a k) -> p a k", a=2)
        rows = region(14336, 3072).rearrange("p (j t) -> p j t", t=T)
        knat = region(21504, 512).rearrange("p (h d) -> p h d", h=MH)
        av = region(22016, 264)
        CN = region(22280, 4 * 264).rearrange("p (h e) -> p h e", h=MH)
        Dm = region(23336, 256).rearrange("p (a s) -> p a s", a=2)
        Sm = region(23592, 256).rearrange("p (a s) -> p a s", a=2)
        SmT = region(23848, 256).rearrange("p (a s) -> p a s", a=2)
        numt = region(24104, 512).rearrange("p (a e) -> p a e", a=2)
        smalls = region(24616, 32).rearrange("p (b c) -> p b c", b=TB)
        natc = region(24648, 64)

        qT3 = region(0, 4096).rearrange("p (j t) -> p j t", t=T)
        scores = region(4096, 4096).rearrange("p (b j n) -> p b j n", b=TB, j=2 * PH)
        work = region(8192, 4096).rearrange("p (b j n) -> p b j n", b=TB, j=2 * PH)
        topv = region(12288, 512).rearrange("p (b j k) -> p b j k", b=TB, j=2 * PH)
        topi = region(12800, 512).bitcast(U32).rearrange("p (b j k) -> p b j k", b=TB, j=2 * PH)
        topf = region(13312, 512).rearrange("p (b j k) -> p b j k", b=TB, j=2 * PH)
        cand = region(4096, 4096).rearrange("p (b h c) -> p b h c", b=TB, h=PH)
        cwork = region(8192, 4096).rearrange("p (b h c) -> p b h c", b=TB, h=PH)
        finv = region(13824, 256).rearrange("p (b h k) -> p b h k", b=TB, h=PH)
        fini = region(14080, 256).bitcast(U32).rearrange("p (b h k) -> p b h k", b=TB, h=PH)
        fab_u = region(14336, 512).bitcast(U32).rearrange("p (s b c) -> p s b c", s=2, b=TB)
        fab = region(14848, 512).rearrange("p (s b h k) -> p s b h k", s=2, b=TB, h=PH)
        onehot = region(15360, 2048).rearrange("p (h k j) -> p h k j", h=PH, k=TOPK)
        chosen = region(17408, 768).rearrange("p (b s c) -> p b s c", b=TB, s=3)
        idxT = region(18432, 768).rearrange("p (s t) -> p s t", s=3)
        pairs = region(19200, 1024).rearrange("p (a b c k) -> p a b c k", a=2, b=2, c=2)
        gelu_u = region(20224, 1024).rearrange("p (a k) -> p a k", a=2)
        staged = region(21248, 512).rearrange("p (a k) -> p a k", a=2)
        G = region(0, HALF * T).rearrange("p (g j t) -> p g j t", g=T // 4, t=4)

        ssq, msq, rt, rstd = st[:, 0:2], st[:, 2:4], st[:, 4:6], st[:, 6:8]
        gates = st[:, 8:104].rearrange("p (b c) -> p b c", b=TB)
        mx = st[:, 104:112].rearrange("p (a c) -> p a c", a=2)
        ngm = st[:, 112:120].rearrange("p (a c) -> p a c", a=2)
        sums = st[:, 120:128].rearrange("p (a c) -> p a c", a=2)
        rz = st[:, 128:136].rearrange("p (a c) -> p a c", a=2)
        gz = st[:, 136:144].rearrange("p (a c) -> p a c", a=2)
        mst = st[:, 144:160].rearrange("p (a c) -> p a c", a=2)
        hss = st[:, 160:184].rearrange("p (b c) -> p b c", b=TB)
        hrt = st[:, 184:208].rearrange("p (b c) -> p b c", b=TB)
        zs = st[:, 208:224].rearrange("p (b h) -> p b h", b=TB)
        rowst = st[0:8, 224:232]

        slot_full = [sem(f"slot_full{s}") for s in range(2)]
        raw_free = [sem(f"raw_free{s}") for s in range(2)]
        hi_ready = [sem(f"hi_ready{s}") for s in range(2)]
        slot_used = [sem(f"slot_used{s}") for s in range(2)]
        hTh_part, hTl_part = sem("hTh_part"), sem("hTl_part")
        mixw_loaded, gates_in, v_read = sem("mixw_loaded"), sem("gates_in"), sem("v_read")
        staged_out = [sem("staged_out0"), sem("staged_out1")]
        bank_free = [sem(f"bank_free{b}") for b in range(4)]
        x_in, params_in, stage1_in, fnw_in, out_done = (sem(n) for n in (
            "x_in", "params_in", "stage1_in", "fnw_in", "out_done"))
        sq_done, ms_ready, rt_done, xn_ready, turned, hT_part = (sem(n) for n in (
            "sq_done", "ms_ready", "rt_done", "xn_ready", "turned", "hT_part"))
        (gbr_ready, gates_ready, pooled, z_ready, y_pool, silu_done, swapped, roped, kb_ready, hid_ready,
         hid_silu, kc_ready, kc_copied, kc_roped, vc_ready, vc_copied) = (sem(n) for n in (
             "gbr_ready", "gates_ready", "pooled", "z_ready", "y_pool", "silu_done", "swapped", "roped",
             "kb_ready", "hid_ready", "hid_silu", "kc_ready", "kc_copied", "kc_roped", "vc_ready", "vc_copied"))
        (scores_ready, scores_read, max_ready, exp_done, probs_ready, probsT_ready, probsT_copied, o_done,
         o_read) = (sem(n) for n in (
             "scores_ready", "scores_read", "max_ready", "exp_done", "probs_ready", "probsT_ready",
             "probsT_copied", "o_done", "o_read"))
        merged_ready, x1_ready, x1_normed, x2_ready, fnw1_in = (sem(n) for n in (
            "merged_ready", "x1_ready", "x1_normed", "x2_ready", "fnw1_in"))
        (sm_ready, sm_copied, rowsT_ready, row_e, row_l, row_y, rows_ready, nat_ready, nat_copied, a_ready,
         conv_done, conv_silu, q_ready, knat_ready, knat_copied, av_ready, C_ready, C_copied) = (sem(n) for n in (
             "sm_ready", "sm_copied", "rowsT_ready", "row_e", "row_l", "row_y", "rows_ready", "nat_ready",
             "nat_copied", "a_ready", "conv_done", "conv_silu", "q_ready", "knat_ready", "knat_copied",
             "av_ready", "C_ready", "C_copied"))
        (f_scores, f_read, f_max, f_exp, f_T, f_copied, f_o, f_oread) = (sem(n) for n in (
            "f_scores", "f_read", "f_max", "f_exp", "f_T", "f_copied", "f_o", "f_oread"))
        (m_scores, m_max, m_exp, m_sm, m_T, m_copied, m_num, m_read) = (sem(n) for n in (
            "m_scores", "m_max", "m_exp", "m_sm", "m_T", "m_copied", "m_num", "m_read"))
        mo_sig, cells, head_sq, head_ms, head_rt = (sem(n) for n in (
            "mo_sig", "cells", "head_sq", "head_ms", "head_rt"))
        (qs_ready, qs_copied, gate_arg, gate_exp, chosen_ready, chosenT, chosenT_copied, pair_ready, pair_free,
         g_evac) = (sem(n) for n in (
             "qs_ready", "qs_copied", "gate_arg", "gate_exp", "chosen_ready", "chosenT", "chosenT_copied",
             "pair_ready", "pair_free", "g_evac"))
        gated = [sem("gated0"), sem("gated1")]
        x3_ready, result = sem("x3_ready"), sem("result")
        dve_step, act_step, pool_step = sem("dve_step"), sem("act_step"), sem("pool_step")

        def stepper(eng, s):
            n = [0]

            def step(ins):
                n[0] += 1
                ins.then_inc(s, 1)
                eng.wait_ge(s, n[0])
            return step

        def loaded(name, i, s):
            return i * 32 + 16 * (2 * G0[name][0] + s // 2 + 1)

        def consumed(name, i, s):
            return i * 2 + 2 * G0[name][0] + s // 2 + 1

        def rounded(name, i, s):
            return i * 2 + 2 * S0[name] + s // 2 + 1

        def multiplied(name, i, s):
            return i * 2 + 2 * S0[name] + s // 2 + 2

        def gate_block(j, n):
            return G[:, :, bass.ds(j, n), :]

        def bc(ap, shape):
            return ap.to_broadcast(shape)

        block = ctx.enter_context(nc.Block())

        @block.sync
        def _(sp):
            sp.dma_start(xres[:], x.rearrange("o (b p) d -> p (o b) d", p=P)).then_inc(x_in, 16)
            sp.dma_start(par[:], params).then_inc(params_in, 16)
            for s in range(2):
                sp.dma_start(raw[s][:], stream[s]).then_inc(slot_full[s], 16)
            sp.dma_start(region(stage1_at, n_stage1), stage1).then_inc(stage1_in, 16)
            for s in range(2, RING):
                sp.wait_ge(raw_free[s % 2], 1)
                sp.dma_start(raw[s % 2][:], stream[s]).then_inc(slot_full[s % 2], 16)
            with sp.Fori(1, GROUPS) as g:
                for s in range(RING):
                    sp.wait_ge(raw_free[s % 2], g * 2 + s // 2)
                    sp.dma_start(raw[s % 2][:], stream[g * RING + s]).then_inc(slot_full[s % 2], 16)
            sp.wait_ge(raw_free[0], 2 * GROUPS)
            sp.dma_start(raw[0][:], fnw.partition_broadcast(P)).then_inc(fnw_in, 16)
            sp.wait_ge(result, TB)
            sp.dma_start(out.rearrange("o (b p) d -> p (o b) d", p=P),
                         R[:, 0:TB * D].rearrange("p (b d) -> p b d", b=TB)).then_inc(out_done, 16)
            sp.wait_ge(out_done, 16)

        @block.tensor
        def _(pe):
            mm = nc.tensor.matmul

            def turn_norm(n):
                for b in range(TB):
                    pe.wait_ge(xn_ready, TB * n + b + 1)
                    for j in range(4):
                        if b > 0:
                            pe.wait_ge(hT_part, 8 * n + 4 * (b - 1) + j + 1)
                        for c in range(4):
                            last = nc.tensor.transpose(bank[4 + j][:, c * P:(c + 1) * P],
                                                       scr_of[n][:, b * D + (4 * j + c) * P:b * D + (4 * j + c + 1) * P], ident)
                        last.then_inc(turned, 1)

            def phase_t(name):
                with pe.Fori(0, G0[name][1]) as i:
                    for s in range(RING):
                        b, t = s // 2, s % 2
                        if t == 0:
                            pe.wait_ge(bank_free[b], i + B0[name][b])
                        pe.wait_ge(raw_free[t], consumed(name, i, s))
                        for k in range(KC):
                            ks = slice(k * P, (k + 1) * P)
                            for n, (w, x_) in enumerate(((whi, hTh), (whi, hTl), (wlo, hTh))):
                                last = mm(bank[b][:, t * T:(t + 1) * T], w[t][:, ks], x_[:, k, :],
                                          start=(k == 0 and n == 0), stop=(k == KC - 1 and n == 2))
                        last.then_inc(slot_used[t], 1)

            def phase_t_raw(name, rhs):
                with pe.Fori(0, G0[name][1]) as i:
                    for s in range(RING):
                        b, t = s // 2, s % 2
                        if t == 0:
                            pe.wait_ge(bank_free[b], i + B0[name][b])
                        pe.wait_ge(slot_full[t], loaded(name, i, s))
                        for k in range(KC):
                            last = mm(bank[b][:, t * T:(t + 1) * T], raw[t][:, k * P:(k + 1) * P],
                                      rhs[:, k, :], start=(k == 0), stop=(k == KC - 1))
                        last.then_inc(raw_free[t], 1)

            def phase_n(name):
                with pe.Fori(0, G0[name][1] // 2) as i:
                    for h in range(2):
                        for b in range(TB):
                            pe.wait_ge(bank_free[2 * h + b], i + B0[name][2 * h + b])
                        for s in range(RING):
                            t = s % 2
                            pe.wait_ge(raw_free[t], i * 4 + consumed(name, h, s))
                            for kk in range(4):
                                k = 4 * s + kk
                                for b in range(TB):
                                    ts_ = slice(b * P, (b + 1) * P)
                                    for n, (x_, w) in enumerate(((hTh, whi), (hTh, wlo), (hTl, whi))):
                                        last = mm(bank[2 * h + b][:], x_[:, k, ts_], w[t][:, kk * 512:(kk + 1) * 512],
                                                  start=(k == 0 and n == 0), stop=(k == KC - 1 and n == 2))
                            last.then_inc(slot_used[t], 1)

            def phase_n_raw(name, lhs):
                with pe.Fori(0, G0[name][1] // 2) as i:
                    for h in range(2):
                        for b in range(TB):
                            pe.wait_ge(bank_free[2 * h + b], i + B0[name][2 * h + b])
                        for s in range(RING):
                            t = s % 2
                            pe.wait_ge(slot_full[t], i * 64 + loaded(name, h, s))
                            for kk in range(4):
                                k = 4 * s + kk
                                for b in range(TB):
                                    last = mm(bank[2 * h + b][:], lhs[:, k, b * P:(b + 1) * P],
                                              raw[t][:, kk * 512:(kk + 1) * 512], start=(k == 0), stop=(k == KC - 1))
                            last.then_inc(raw_free[t], 1)

            def small_product(dst, b, w):
                for k in range(KC):
                    for n, x_ in enumerate((hTh, hTl)):
                        last = mm(dst, x_[:, k, b * P:(b + 1) * P].bitcast(F32), w[:, k, :],
                                  start=(k == 0 and n == 0), stop=(k == KC - 1 and n == 1))
                return last

            for s_ in (*bank_free, *gated, *slot_used):
                pe.sem_inc(s_, 1)
            pe.wait_ge(params_in, 16)
            turn_norm(0)
            pe.wait_ge(hTl_part, 8)
            phase_t("in_t")
            phase_n("in_n")
            pe.wait_ge(stage1_in, 16)
            wg = s1("wgbr").rearrange("p (k c) -> p k c", k=KC)
            for b in range(TB):
                last = small_product(bank[4 + b][:, 0:48], b, wg)
            last.then_inc(gbr_ready, 1)
            for v in range(2):
                pe.wait_ge(kb_ready, v + 1)
                if v == 0:
                    pe.wait_ge(gates_ready, 1)
                for s in range(RING):
                    pe.wait_ge(slot_full[s % 2], loaded("cmp", v, s))
                    for ll in range(8):
                        l = 8 * s + ll
                        for f in range(2):
                            last = mm(bank[4 + 2 * v + f][:, 0:NC4], raw[s % 2][:, ll * CH + f * P:ll * CH + (f + 1) * P],
                                      kb[v][:, l, :], start=(l == 0), stop=(l == CB - 1))
                    last.then_inc(raw_free[s % 2], 1)
            pe.wait_ge(hid_silu, 1)
            w2k = s1("w2k").rearrange("p (f e) -> p f e", f=2)
            w2v = s1("w2v").rearrange("p (f e) -> p f e", f=2)
            for f in range(2):
                last = mm(bank[4][:, 0:NC4], w2k[:, f, :], hdn[:, 0, f, :], start=(f == 0), stop=(f == 1))
            last.then_inc(kc_ready, 1)
            pe.wait_ge(hid_silu, 2)
            for h in range(HKV):
                for f in range(2):
                    last = mm(bank[5][0:NCMP, h * DH:(h + 1) * DH], hdn[:, 1, f, h * NCMP:(h + 1) * NCMP],
                              w2v[:, f, :], start=(f == 0), stop=(f == 1))
            last.then_inc(vc_ready, 1)

            def nsa_scores(u):
                h, qb = divmod(u, TB)
                a, kv, nk = u % 2, h // GQ, (qb + 1) * P
                if u >= 2:
                    pe.wait_ge(scores_read, u - 1)
                    pe.wait_ge(probsT_copied, u - 1)
                q = pT[:, Q0 + h, qb * P:(qb + 1) * P]
                mm(bank[4 + a][:, 0:nk], q, pT[:, KS0 + kv, 0:nk], start=True, stop=True)
                mm(bank[4 + a][:, T:T + nk], q, pT[:, KW0 + kv, 0:nk], start=True, stop=True)
                mm(bank[a][:, 0:NCMP], q, kcT[:, kv * NCMP:(kv + 1) * NCMP], start=True,
                   stop=True).then_inc(scores_ready, 1)

            def nsa_turn(u):
                qb, a = u % TB, u % 2
                nb = qb + 1
                pe.wait_ge(probs_ready, u + 1)
                if u >= 2:
                    pe.wait_ge(probsT_copied, u - 1)
                for br in range(2):
                    for k in range(nb):
                        j = br * nb + k
                        nc.tensor.transpose(bank[6 + a][:, j * P:(j + 1) * P],
                                            SP[:, a, br * T + k * P:br * T + (k + 1) * P], ident)
                nc.tensor.transpose(bank[a][0:NCMP, P:2 * P], Pc[:, a, 0:NCMP], ident).then_inc(probsT_ready, 1)

            def nsa_values(u):
                h, qb = divmod(u, TB)
                a, kv, nb = u % 2, h // GQ, qb + 1
                pe.wait_ge(probsT_copied, u + 1)
                if qb == 0 and h >= 2:
                    pe.wait_ge(o_read, h - 1)
                o = bank[2 + h % 2][:, qb * P:(qb + 1) * P]
                mm(o, vcs[:, kv * DH:(kv + 1) * DH], PcT[:, a, :], start=True, stop=False)
                for br in range(2):
                    for k in range(nb):
                        j = br * nb + k
                        last = mm(o, vN1[:, br, k, kv * DH:(kv + 1) * DH], PT[:, a, j * P:(j + 1) * P],
                                  start=False, stop=(j == 2 * nb - 1))
                last.then_inc(o_done, 1)

            units = HQ * TB
            pe.wait_ge(roped, 12)
            pe.wait_ge(kc_roped, 1)
            pe.wait_ge(vc_copied, 1)
            for b in range(4):
                pe.wait_ge(bank_free[b], B0["merge"][b])
            nsa_scores(0)
            nsa_scores(1)
            for u in range(units):
                nsa_turn(u)
                if u + 2 < units:
                    nsa_scores(u + 2)
                nsa_values(u)
            pe.wait_ge(pooled, NG)
            pe.wait_ge(probsT_copied, units)
            pe.wait_ge(mixw_loaded, 16)
            mixw = mixw_sb.rearrange("p (g c e) -> p g c e", g=NG, c=2)
            for g in range(NG):
                for e in range(2):
                    for c in range(2):
                        last = mm(bank[4 + g][:, e * T:(e + 1) * T], mixw[:, g, c, e * P:(e + 1) * P],
                                  pT[:, U0 + 2 * g + c, :], start=(c == 0), stop=(c == 1))
                last.then_inc(z_ready, 1)
            pe.wait_ge(o_read, HQ)
            phase_t("merge")
            pe.wait_ge(y_pool, NG)
            with pe.Fori(0, G0["pool_out"][1]) as i:
                for s in range(RING):
                    t = s % 2
                    pe.wait_ge(bank_free[s], i + B0["pool_out"][s])
                    pe.wait_ge(slot_full[t], loaded("pool_out", i, s))
                    for e in range(2):
                        for k in range(8):
                            last = mm(bank[s][:, e * T:(e + 1) * T], raw[t][:, (e * 8 + k) * P:(e * 8 + k + 1) * P],
                                      pT[:, U0 + k, :], start=(k == 0), stop=(k == 7))
                    last.then_inc(raw_free[t], 1)
            phase_t_raw("nsa_out", pT[:, GN0:GN0 + 16, :])
            pe.wait_ge(merged_ready, 2 * G0["nsa_out"][1])
            phase_n_raw("out1", gate0)

            turn_norm(1)
            pe.wait_ge(hTl_part, 16)
            wr = prm("wrows").rearrange("p (k c) -> p k c", k=KC)
            for b in range(TB):
                last = small_product(bank[4][:, b * 16:(b + 1) * 16], b, wr)
            last.then_inc(sm_ready, 1)
            pe.wait_ge(sm_copied, 1)
            for b in range(TB):
                for r, (c0, c1) in enumerate(((0, 8), (8, 12), (12, 16))):
                    last = nc.tensor.transpose(bank[5 + r][0:c1 - c0, b * P:(b + 1) * P], smalls[:, b, c0:c1], ident)
            last.then_inc(rowsT_ready, 1)
            phase_t("in2_t")
            phase_n("in2_n")
            pe.wait_ge(rows_ready, 1)
            for c in range(TB):
                nc.tensor.transpose(bank[4][:, 8 * c:8 * c + 8], rows[0:8, 6, c * P:(c + 1) * P], ident[0:8, 0:8])
                nc.tensor.transpose(bank[4][:, 16 + 4 * c:20 + 4 * c], rows[0:4, 8, c * P:(c + 1) * P],
                                    ident[0:4, 0:4])
                nc.tensor.transpose(bank[4][:, 24 + 4 * c:28 + 4 * c], rows[0:4, 10, c * P:(c + 1) * P],
                                    ident[0:4, 0:4])
            nc.tensor.transpose(bank[4][:, 32:36], rows[0:4, 11, 0:P], ident[0:4, 0:4]).then_inc(nat_ready, 1)
            pe.wait_ge(q_ready, 2)
            for h in range(MH):
                last = nc.tensor.transpose(bank[5][:, h * P:(h + 1) * P], conv[:, 4 + h, 0:P], ident)
            last.then_inc(knat_ready, 1)
            pe.wait_ge(knat_copied, 1)
            for h in range(MH):
                pe.wait_ge(av_ready, h + 1)
                mm(bank[6][:, 0:MV + 1], knat[:, h, :], av[:, 0:MV + 1], start=True, stop=True).then_inc(C_ready, 1)

            def fox_scores(u):
                h, qb = divmod(u, TB)
                a, nk = u % 2, (qb + 1) * P
                if u >= 2:
                    pe.wait_ge(f_read, u - 1)
                mm(bank[4 + a][:, 0:nk], pT[:, FQ0 + h, qb * P:(qb + 1) * P], pT[:, FK0 + h, 0:nk],
                   start=True, stop=False)
                mm(bank[4 + a][:, 0:nk], bc(ident[0:8, h:h + 1], [8, P]), rows[0:8, 7, 0:nk],
                   start=False, stop=True).then_inc(f_scores, 1)

            def fox_turn(u):
                qb, a = u % TB, u % 2
                pe.wait_ge(f_exp, u + 1)
                if u >= 2:
                    pe.wait_ge(f_copied, u - 1)
                for k in range(qb + 1):
                    last = nc.tensor.transpose(bank[6 + a][:, k * P:(k + 1) * P], SP2[:, a, k * P:(k + 1) * P], ident)
                last.then_inc(f_T, 1)

            def fox_values(u):
                h, qb = divmod(u, TB)
                a = u % 2
                pe.wait_ge(f_copied, u + 1)
                if u >= 2:
                    pe.wait_ge(f_oread, u - 1)
                for k in range(qb + 1):
                    last = mm(bank[2 + a][:, 0:DH], PT2[:, a, k * P:(k + 1) * P],
                              vN2[:, h // 4, k, (h % 4) * DH:(h % 4 + 1) * DH], start=(k == 0), stop=(k == qb))
                last.then_inc(f_o, 1)

            units = FH * TB
            pe.wait_ge(nat_copied, 1)
            pe.wait_ge(C_copied, MH)
            for b in range(4):
                pe.wait_ge(bank_free[b], B0["out2"][b])
            fox_scores(0)
            fox_scores(1)
            for u in range(units):
                fox_turn(u)
                if u + 2 < units:
                    fox_scores(u + 2)
                fox_values(u)
            pe.wait_ge(f_copied, units)
            pe.wait_ge(f_oread, units)

            def m_sc(u):
                c, h = divmod(u, MH)
                a = u % 2
                if u >= 2:
                    pe.wait_ge(m_sm, u - 1)
                cs = slice(c * P, (c + 1) * P)
                mm(bank[4 + a][:, 0:P], conv[:, h, cs], conv[:, 4 + h, cs], start=True, stop=True)
                mm(bank[4 + a][:, P:2 * P], bc(ident[0:4, h:h + 1], [4, P]), rows[0:4, 9, cs],
                   start=True, stop=True).then_inc(m_scores, 1)

            def m_turn(u):
                a = u % 2
                pe.wait_ge(m_sm, u + 1)
                if u >= 2:
                    pe.wait_ge(m_copied, u - 1)
                nc.tensor.transpose(bank[6 + a][:, 0:P], Sm[:, a, :], ident).then_inc(m_T, 1)

            def m_values(u):
                c, h = divmod(u, MH)
                a = u % 2
                pe.wait_ge(m_copied, u + 1)
                if u >= 2:
                    pe.wait_ge(m_read, u - 1)
                if c == 1:
                    mm(bank[a][:, 0:MV + 1], conv[:, h, P:2 * P], CN[:, h, 0:MV + 1], start=True, stop=True)
                mm(bank[2 + a][:, 0:MV], SmT[:, a, :], vN2[:, 2 + h // 2, c, (h % 2) * MV:(h % 2 + 1) * MV],
                   start=True, stop=True).then_inc(m_num, 1)

            units = MH * TB
            m_sc(0)
            m_sc(1)
            for u in range(units):
                m_turn(u)
                if u + 2 < units:
                    m_sc(u + 2)
                m_values(u)
            turn_norm(2)
            pe.wait_ge(hTl_part, 24)
            phase_n("out2")
            turn_norm(3)
            pe.wait_ge(hTl_part, 32)
            phase_t("wq")
            for b in range(2):
                pe.wait_ge(bank_free[b], B0["peer_u0"][b])
            keysT = prm("keysT").rearrange("p (s n) -> p s n", s=2)
            for f in range(TB * 4):
                b, j = divmod(f, 4)
                if f >= 4:
                    pe.wait_ge(qs_copied, f - 3)
                for c in range(4):
                    hp = 4 * j + c
                    last = mm(bank[4 + j][:, c * NK:(c + 1) * NK], qT3[:, hp, b * P:(b + 1) * P],
                              keysT[:, hp % 2, :], start=True, stop=True)
                last.then_inc(qs_ready, 1)
            for b in range(TB):
                pe.wait_ge(chosen_ready, b + 1)
                for s in range(3):
                    last = nc.tensor.transpose(bank[4 + b][:, s * P:(s + 1) * P], chosen[:, b, s, :], ident)
                last.then_inc(chosenT, 1)
            pe.wait_ge(chosenT_copied, TB)
            pe.sem_inc(pair_free, 2)
            with pe.Fori(0, T // 8) as i:
                for q in range(4):
                    if q % 2 == 0:
                        pe.wait_ge(g_evac, i * 2 + q // 2 + 1)
                    pe.wait_ge(pair_ready, i * 4 + q + 1)
                    for t in range(2):
                        c = (q % 2) * 2 + t
                        last = mm(bank[4 + q // 2][:, c * P:(c + 1) * P], pairs[:, q % 2, t, 0, :],
                                  pairs[:, q % 2, t, 1, :], start=True, stop=True)
                    last.then_inc(pair_free, 1)
            def expert_values(name, i, first, last_group):
                for s in range(RING):
                    t = s % 2
                    pe.wait_ge(raw_free[t], consumed(name, i, s))
                    for b in range(TB):
                        ts_ = slice(b * P, (b + 1) * P)
                        for n, (x_, w) in enumerate(((ghi, whi), (ghi, wlo), (glo, whi))):
                            for c in range(4):
                                last = mm(bank[4 * b + c][:], x_[:, t, ts_], w[t][:, c * 512:(c + 1) * 512],
                                          start=(first and s == 0 and n == 0),
                                          stop=(last_group and s == RING - 1 and n == 2))
                    last.then_inc(slot_used[t], 1)

            for half in range(2):
                if half:
                    pe.wait_ge(v_read, 2)
                phase_t(f"peer_u{half}")
                pe.wait_ge(g_evac, 2 + T // 4)
                if half:
                    pe.wait_ge(v_read, 8)
                for b in range(2):
                    pe.wait_ge(bank_free[b], B0[f"peer_v{half}"][b])
                name = f"peer_v{half}"
                n = G0[name][1]
                expert_values(name, 0, True, False)
                with pe.Fori(1, n - 1) as i:
                    expert_values(name, i, False, False)
                expert_values(name, n - 1, False, True)

        @block.scalar
        def _(act):
            step = stepper(act, act_step)
            A = nc.scalar.activation

            def split(name, i, s):
                t = s % 2
                act.wait_ge(slot_full[t], loaded(name, i, s))
                act.wait_ge(slot_used[t], rounded(name, i, s))
                if name.startswith("peer_v"):
                    A(ghi[:, t, :].rearrange("p (g o t) -> p g o t", o=1, t=4), gate_block(i * 4 + s, 1), ACT.Copy)
                A(whi[t][:], raw[t][:], ACT.Copy).then_inc(hi_ready[t], 1)

            def phase(name, evac0, evac1):
                n = G0[name][1]
                split(name, 0, 0)
                with act.Fori(0, n - 1) as i:
                    for s in range(1, RING):
                        split(name, i, s)
                    evac0(i)
                    split(name, i + 1, 0)
                    evac1(i)
                for s in range(1, RING):
                    split(name, n - 1, s)
                evac0(n - 1)
                evac1(n - 1)

            def keep(i):
                pass

            def high_parts(n):
                for b in range(TB):
                    for j in range(4):
                        f = 4 * b + j
                        act.wait_ge(hT_part, 8 * n + f + 1)
                        A(hTh[:, 4 * j:4 * j + 4, b * P:(b + 1) * P],
                          turned_tmp[:, f % 2, :].rearrange("p (c t) -> p c t", c=4), ACT.Copy).then_inc(hTh_part, 1)

            def squares(n):
                for b in range(TB):
                    A(scr_of[(0, 0, 1, 3)[n]][:, b * D:(b + 1) * D], xres[:, b, :], ACT.Square, accum_out=ssq[:, b:b + 1]).then_inc(sq_done, 1)
                act.wait_ge(ms_ready, n + 1)
                A(rt, msq, ACT.Sqrt).then_inc(rt_done, 1)

            def evac_t(name):
                def evac1(i):
                    act.wait_ge(slot_used[1], multiplied(name, i, 3))
                    A(R[:, bass.ds(i * (4 * T) + 2 * T, 2 * T)], bank[1][:], ACT.Copy).then_inc(bank_free[1], 1)
                phase(name, keep, evac1)

            def phase_n(name, dst):
                def evac(g):
                    act.wait_ge(slot_used[1], multiplied(name, g, 3))
                    A(dst[:, g, 0, :], bank[2 * (g % 2)][:], ACT.Copy).then_inc(bank_free[2 * (g % 2)], 1)
                n = G0[name][1]
                for g in range(n):
                    split(name, g, 0)
                    if g and dst is not None:
                        evac(g - 1)
                    for s in range(1, RING):
                        split(name, g, s)
                if dst is not None:
                    evac(n - 1)

            act.wait_ge(x_in, 16)
            squares(0)
            high_parts(0)
            evac_t("in_t")
            phase_n("in_n", vN1)
            act.wait_ge(gbr_ready, 1)
            for b in range(TB):
                last = A(gates[:, b, :], bank[4 + b][:, 0:48], ACT.Sigmoid)
            last.then_inc(gates_ready, 1)
            act.wait_ge(bank_free[0], B0["in_n"][0])
            A(pT[:, GP0:GP0 + 8, :], pT[:, GP0:GP0 + 8, :], ACT.Silu).then_inc(silu_done, 1)
            A(pT[:, GN0:GN0 + 16, :], pT[:, GN0:GN0 + 16, :], ACT.Silu).then_inc(silu_done, 1)
            for j in range(12):
                if j >= 2:
                    act.wait_ge(roped, j - 1)
                buf = rot_buf[:, (j % 2) * 512:(j % 2 + 1) * 512].rearrange("p (j t) -> p j t", t=T)
                src = pT[:, KS0 + 2 * j:KS0 + 2 * j + 2, :]
                A(buf[0:64], src[64:128], ACT.Copy)
                A(buf[64:128], src[0:64], ACT.Copy).then_inc(swapped, 1)
            act.wait_ge(kb_ready, 2)
            act.dma_start(mixw_sb, mixw_in).then_inc(mixw_loaded, 16)
            for v in range(2):
                act.wait_ge(raw_free[1], consumed("cmp", v, 3))
                for f in range(2):
                    last = A(hdn[:, v, f, :], bank[4 + 2 * v + f][:, 0:NC4], ACT.Silu)
                last.then_inc(hid_silu, 1)
            act.wait_ge(kc_ready, 1)
            A(kcT, bank[4][:, 0:NC4], ACT.Copy)
            A(kcS[0:64], bank[4][64:128, 0:NC4], ACT.Copy)
            A(kcS[64:128], bank[4][0:64, 0:NC4], ACT.Copy).then_inc(kc_copied, 1)
            act.wait_ge(vc_ready, 1)
            A(vcs, bank[5][0:NCMP, :], ACT.Copy).then_inc(vc_copied, 1)

            def nsa_exp(u):
                a, nk = u % 2, (u % TB + 1) * P
                act.wait_ge(max_ready, u + 1)
                for br in range(2):
                    sl = SP[:, a, br * T:br * T + nk]
                    A(sl, sl, ACT.Exp, bias=ngm[:, a, br:br + 1], scale=SCALE, accum_out=sums[:, a, br:br + 1])
                A(Pc[:, a, 0:NCMP], Pc[:, a, 0:NCMP], ACT.Exp, bias=ngm[:, a, 2:3], scale=SCALE,
                  accum_out=sums[:, a, 2:3]).then_inc(exp_done, 1)

            def nsa_copy(u):
                a, n = u % 2, 2 * (u % TB + 1) * P
                act.wait_ge(probsT_ready, u + 1)
                if u >= 2:
                    act.wait_ge(o_done, u - 1)
                A(PT[:, a, 0:n], bank[6 + a][:, 0:n], ACT.Copy)
                A(PcT[:, a, :], bank[a][0:NCMP, P:2 * P], ACT.Copy).then_inc(probsT_copied, 1)

            units = HQ * TB
            nsa_exp(0)
            for u in range(units):
                if u + 1 < units:
                    nsa_exp(u + 1)
                nsa_copy(u)
            act.wait_ge(o_done, units)
            act.dma_start(fnw1_sb, fnw1.partition_broadcast(P)).then_inc(fnw1_in, 16)
            bm = PO["bmerge"][0]

            def merge_gate(b):
                def evac(i):
                    act.wait_ge(slot_used[1], multiplied("merge", i, 2 * b + 1))
                    for e in range(2):
                        last = A(R[:, bass.ds(i * (4 * T) + (16 + 2 * b + e) * T, T)], bank[b][:, e * T:(e + 1) * T],
                                 ACT.Sigmoid, bias=par[:, bass.ds(i * 4 + bm + 2 * b + e, 1)])
                    last.then_inc(bank_free[b], 1)
                return evac
            phase("merge", merge_gate(0), merge_gate(1))

            act.wait_ge(x1_ready, 8)
            squares(1)
            act.wait_ge(x1_normed, TB)
            squares(2)
            high_parts(1)
            act.wait_ge(sm_ready, 1)
            A(smalls, bank[4][:, 0:32].rearrange("p (b c) -> p b c", b=TB), ACT.Copy).then_inc(sm_copied, 1)
            act.wait_ge(row_y, 1)
            A(rows[0:8, 4, :], rows[0:8, 4, :], ACT.Exp).then_inc(act_step, 1)
            A(rows[0:4, 5, :], rows[0:4, 5, :], ACT.Exp).then_inc(act_step, 1)
            act.wait_ge(act_step, 2)
            A(rows[0:8, 4, :], rows[0:8, 4, :], ACT.Ln, bias=1.0)
            A(rows[0:4, 5, :], rows[0:4, 5, :], ACT.Ln, bias=1.0).then_inc(row_l, 1)
            act.wait_ge(a_ready, 1)
            A(rows[0:4, 11, 0:P], rows[0:4, 9, 0:P], ACT.Exp, bias=rowst[0:4, 1:2]).then_inc(rows_ready, 1)
            evac_t("in2_t")
            phase_n("in2_n", vN2)
            act.wait_ge(conv_done, 8)
            A(conv, conv, ACT.Silu).then_inc(conv_silu, 1)
            act.wait_ge(nat_ready, 1)
            A(natc[:, 0:36], bank[4][:, 0:36], ACT.Copy).then_inc(nat_copied, 1)
            act.wait_ge(knat_ready, 1)
            A(knat, bank[5][:].rearrange("p (h d) -> p h d", h=MH), ACT.Copy).then_inc(knat_copied, 1)
            for b in range(4):
                act.wait_ge(bank_free[b], B0["out2"][b])
            A(vN2[:, 4:6], vN2[:, 4:6], ACT.Sigmoid).then_inc(mo_sig, 1)

            def fox_exp(u):
                a, nk = u % 2, (u % TB + 1) * P
                act.wait_ge(f_max, u + 1)
                A(SP2[:, a, 0:nk], SP2[:, a, 0:nk], ACT.Exp, bias=ngm[:, a, 0:1],
                  accum_out=sums[:, a, 0:1]).then_inc(f_exp, 1)

            def fox_copy(u):
                a, n = u % 2, (u % TB + 1) * P
                act.wait_ge(f_T, u + 1)
                if u >= 2:
                    act.wait_ge(f_o, u - 1)
                A(PT2[:, a, 0:n], bank[6 + a][:, 0:n], ACT.Copy).then_inc(f_copied, 1)

            units = FH * TB
            fox_exp(0)
            for u in range(units):
                if u + 1 < units:
                    fox_exp(u + 1)
                fox_copy(u)

            def m_exps(u):
                a = u % 2
                act.wait_ge(m_max, u + 1)
                A(Dm[:, a, :], Dm[:, a, :], ACT.Exp, bias=mst[:, a, 1:2])
                A(mst[:, a, 3:5], mst[:, a, 1:3], ACT.Exp).then_inc(m_exp, 1)

            def m_copy(u):
                a = u % 2
                act.wait_ge(m_T, u + 1)
                if u >= 2:
                    act.wait_ge(m_num, u - 1)
                A(SmT[:, a, :], bank[6 + a][:, 0:P], ACT.Copy).then_inc(m_copied, 1)

            units = MH * TB
            m_exps(0)
            for u in range(units):
                if u + 1 < units:
                    m_exps(u + 1)
                m_copy(u)
            act.wait_ge(cells, 1)
            A(region(0, 4096), scr, ACT.Square).then_inc(head_sq, 1)
            act.wait_ge(head_ms, 1)
            A(hrt, hss, ACT.Sqrt).then_inc(head_rt, 1)
            high_parts(2)
            phase_n("out2", None)
            act.wait_ge(x2_ready, 8)
            squares(3)
            high_parts(3)
            evac_t("wq")
            for f in range(8):
                b, j = divmod(f, 4)
                act.wait_ge(qs_ready, f + 1)
                A(scores[:, b, 4 * j:4 * j + 4, :], bank[4 + j][:].rearrange("p (c n) -> p c n", c=4),
                  ACT.Copy).then_inc(qs_copied, 1)
            for b in range(TB):
                act.wait_ge(gate_arg, b + 1)
                A(finv[:, b], finv[:, b], ACT.Exp).then_inc(gate_exp, 1)
            for b in range(TB):
                act.wait_ge(chosenT, b + 1)
                A(idxT[:, :, b * P:(b + 1) * P], bank[4 + b][:, 0:3 * P].rearrange("p (s t) -> p s t", s=3),
                  ACT.Copy).then_inc(chosenT_copied, 1)
            act.sem_inc(g_evac, 2)
            for q in range(2):
                act.sem_inc(staged_out[q], 16)
            with act.Fori(0, T // 8) as i:
                for q in range(2):
                    src = bank[4 + q][:].rearrange("p (t n) -> p n t", t=4)
                    act.wait_ge(pair_free, i * 4 + 2 * q + 4)
                    A(G[:, bass.ds(i * 2 + q, 1), :, :].rearrange("p g j t -> p (g j) t"), src[:, 0:HALF, :], ACT.Copy)
                    act.wait_ge(staged_out[q], i * 16 + 16)
                    A(staged[:, q, :].rearrange("p (j t) -> p j t", t=4), src[:, HALF:NK, :], ACT.Copy).then_inc(g_evac, 1)
                    act.wait_ge(g_evac, i * 2 + q + 3)
                    act.dma_start(gates_dram[i * 2 + q], staged[:, q, :]).then_inc(staged_out[q], 16)

            def gelu(name, b):
                base = 1 + (0 if name == "peer_u0" else G0["peer_u0"][1])

                def evac(i):
                    act.wait_ge(slot_used[1], multiplied(name, i, 2 * b + 1))
                    act.wait_ge(gated[b], i + base)
                    A(gelu_u[:, b, :], bank[b][:], ACT.Gelu).then_inc(bank_free[b], 1)
                return evac

            for half in range(2):
                name = f"peer_u{half}"
                phase(name, gelu(name, 0), gelu(name, 1))
                name = f"peer_v{half}"
                for b in range(2):
                    act.wait_ge(gated[b], 1 + (half + 1) * G0["peer_u0"][1])
                with act.Fori(0, G0[name][1]) as i:
                    for s in range(RING):
                        split(name, i, s)
                if half == 0:
                    act.wait_ge(raw_free[1], consumed(name, G0[name][1] - 1, 3))
                    for q in range(2):
                        act.wait_ge(staged_out[q], 16 + 16 * (T // 8))
                    act.dma_start(region(0, HALF * T).rearrange("p (g c) -> p g c", g=T // 4),
                                  gates_dram.rearrange("g p c -> p g c")).then_inc(gates_in, 16)
            act.wait_ge(x3_ready, 8)
            for b in range(TB):
                A(R[:, b * D:(b + 1) * D], xres[:, b, :], ACT.Square, accum_out=ssq[:, b:b + 1]).then_inc(sq_done, 1)
            act.wait_ge(ms_ready, 5)
            A(rt, msq, ACT.Sqrt).then_inc(rt_done, 1)

        @block.gpsimd
        def _(pool):
            step = stepper(pool, pool_step)
            bufs = pool_buf
            inv = s1("invcnt").rearrange("p (g t) -> p g t", g=NG)
            pool.wait_ge(stage1_in, 16)
            step(nc.gpsimd.memset(region(kb_at[0], 4 * W), 0.0))
            for b in range(2):
                pool.wait_ge(bank_free[b], B0["in_t"][b] + 2)
            for g, w in enumerate(WINDOWS):
                u = pT[:, U0 + 2 * g:U0 + 2 * g + 2, :]
                step(nc.gpsimd.tensor_copy(bufs[0][:, :, PAD:], u))
                a, s = 0, 1
                while s < w:
                    step(nc.gpsimd.tensor_tensor(bufs[1 - a][:, :, PAD:], bufs[a][:, :, PAD:],
                                                 bufs[a][:, :, PAD - s:PAD - s + T], ALU.add))
                    a, s = 1 - a, 2 * s
                step(nc.gpsimd.tensor_scalar(bufs[1 - a][:, :, PAD:], bufs[a][:, :, PAD:], 1.0 / w, None, ALU.mult))
                step(nc.gpsimd.tensor_tensor(bufs[1 - a][:, :, PAD:PAD + 16], bufs[a][:, :, PAD:PAD + 16],
                                             bc(inv[:, g:g + 1, :], [P, 2, 16]), ALU.mult))
                nc.gpsimd.tensor_tensor(u, bufs[1 - a][:, :, PAD:], u, ALU.subtract).then_inc(pooled, 1)
                pool.wait_ge(pooled, g + 1)

        @block.vector
        def _(dve):
            step = stepper(dve, dve_step)
            V = nc.vector

            def root_mean_square(m):
                dve.wait_ge(sq_done, TB * (m + 1))
                V.tensor_scalar(msq, ssq, 1.0 / D, EPS, ALU.mult, ALU.add).then_inc(ms_ready, 1)
                dve.wait_ge(rt_done, m + 1)
                step(V.reciprocal(rstd, rt))

            def norm(n, weight, m):
                root_mean_square(m)
                for b in range(TB):
                    V.tensor_scalar(scr_of[n][:, b * D:(b + 1) * D], xres[:, b, :], rstd[:, b:b + 1], None,
                                    ALU.mult).then_inc(xn_ready, 1)
                read_turned(n, weight)

            def read_turned(n, weight):
                def low_part(f):
                    b, j = divmod(f, 4)
                    at = (slice(None), slice(4 * j, 4 * j + 4), slice(b * P, (b + 1) * P))
                    dve.wait_ge(hTh_part, 8 * n + f + 1)
                    V.tensor_tensor(hTl[at], turned_tmp[:, f % 2, :].rearrange("p (c t) -> p c t", c=4),
                                    hTh[at].bitcast(F32), ALU.subtract).then_inc(hTl_part, 1)

                for f in range(8):
                    b, j = divmod(f, 4)
                    dve.wait_ge(turned, 8 * n + f + 1)
                    if f >= 2:
                        dve.wait_ge(hTl_part, 8 * n + f - 1)
                    V.tensor_tensor(turned_tmp[:, f % 2, :].rearrange("p (c t) -> p c t", c=4),
                                    bank[4 + j][:].rearrange("p (c t) -> p c t", c=4),
                                    bc(prm(weight, 4 * j, 4 * j + 4).unsqueeze(2), [P, 4, P]),
                                    ALU.mult).then_inc(hT_part, 1)
                    if f:
                        low_part(f - 1)
                low_part(7)

            def split(name, i, s):
                t = s % 2
                dve.wait_ge(hi_ready[t], rounded(name, i, s))
                if name.startswith("peer_v"):
                    V.tensor_tensor(glo[:, t, :].rearrange("p (g o t) -> p g o t", o=1, t=4), gate_block(i * 4 + s, 1),
                                    ghi[:, t, :].bitcast(F32).rearrange("p (g o t) -> p g o t", o=1, t=4),
                                    ALU.subtract)
                V.tensor_tensor(wlo[t][:], raw[t][:], whi[t][:].bitcast(F32), ALU.subtract).then_inc(raw_free[t], 1)

            def phase(name, evac0, evac1, after_first=None):
                n = G0[name][1]
                split(name, 0, 0)
                if after_first is not None:
                    after_first()
                with dve.Fori(0, n - 1) as i:
                    for s in range(1, RING):
                        split(name, i, s)
                    evac0(i)
                    split(name, i + 1, 0)
                    evac1(i)
                for s in range(1, RING):
                    split(name, n - 1, s)
                evac0(n - 1)
                evac1(n - 1)

            def keep(i):
                pass

            def evac_t(name):
                def evac0(i):
                    dve.wait_ge(slot_used[1], multiplied(name, i, 1))
                    V.tensor_copy(R[:, bass.ds(i * (4 * T), 2 * T)], bank[0][:]).then_inc(bank_free[0], 1)
                phase(name, evac0, keep)

            def phase_n(name, evac):
                n = G0[name][1]
                for g in range(n):
                    split(name, g, 0)
                    if g:
                        evac(g - 1)
                    for s in range(1, RING):
                        split(name, g, s)
                evac(n - 1)

            def evac_n(name, dst):
                def evac(g):
                    dve.wait_ge(slot_used[1], multiplied(name, g, 3))
                    V.tensor_copy(dst[:, g, 1, :], bank[2 * (g % 2) + 1][:]).then_inc(bank_free[2 * (g % 2) + 1], 1)
                phase_n(name, evac)

            def residual(g, ready):
                for b in range(TB):
                    xs = xres[:, b, g * 512:(g + 1) * 512]
                    step(V.tensor_tensor(xs, bank[2 * (g % 2) + b][:], xs, ALU.add))
                    dve.sem_inc(bank_free[2 * (g % 2) + b], 1)
                    dve.sem_inc(ready, 1)

            dve.wait_ge(params_in, 16)
            dve.wait_ge(x_in, 16)
            norm(0, "norm1", 0)
            evac_t("in_t")
            evac_n("in_n", vN1)
            dve.wait_ge(pooled, NG)
            dve.wait_ge(bank_free[1], B0["in_n"][1])
            for v, (src, pe_name) in enumerate(((KCR0, "pek"), (VCR0, "pev"))):
                kv_rows = pT[:, src:src + 4, :].rearrange("p h (m r) -> p h m r", r=CS)
                for a in range(2):
                    for h in range(HKV):
                        last = V.tensor_tensor(
                            kb[v][:, a * CS:(a + 1) * CS, h * NCMP:(h + 1) * NCMP].rearrange("p r n -> p n r"),
                            kv_rows[:, h, a:a + NCMP, :],
                            bc(prm(pe_name, a * CS, (a + 1) * CS).unsqueeze(1), [P, NCMP, CS]), ALU.add)
                last.then_inc(kb_ready, 1)
            for j in range(12):
                dve.wait_ge(swapped, j + 1)
                buf = rot_buf[:, (j % 2) * 512:(j % 2 + 1) * 512].rearrange("p (j t) -> p j t", t=T)
                xb = pT[:, KS0 + 2 * j:KS0 + 2 * j + 2, :]
                V.tensor_tensor(buf, buf, bc(prm("sin").unsqueeze(1), [P, 2, T]), ALU.mult)
                step(V.tensor_tensor(xb, xb, bc(prm("cos").unsqueeze(1), [P, 2, T]), ALU.mult))
                V.tensor_tensor(xb, xb, buf, ALU.add).then_inc(roped, 1)
            dve.wait_ge(kc_copied, 1)
            step(V.tensor_tensor(kcS, kcS, prm("csin"), ALU.mult))
            step(V.tensor_tensor(kcT, kcT, prm("ccos"), ALU.mult))
            V.tensor_tensor(kcT, kcT, kcS, ALU.add).then_inc(kc_roped, 1)

            def nsa_mask(u):
                qb, a = u % TB, u % 2
                nk = (qb + 1) * P
                dve.wait_ge(scores_ready, u + 1)
                if u >= 2:
                    dve.wait_ge(probsT_ready, u - 1)
                s3 = SP[:, a, :].rearrange("p (r k) -> p r k", r=2)[:, :, 0:nk]
                m3 = prm("mask", 256 - nk, 256)
                V.tensor_tensor(s3, bank[4 + a][:].rearrange("p (r k) -> p r k", r=2)[:, :, 0:nk],
                                bc(m3.unsqueeze(1), [P, 2, nk]), ALU.add)
                step(V.tensor_tensor(Pc[:, a, 0:NCMP], bank[a][:, 0:NCMP],
                                     prm("cmask", qb * NCMP, (qb + 1) * NCMP), ALU.add))
                V.tensor_reduce(mx[:, a, 0:2], s3, AX.X, ALU.max).then_inc(scores_read, 1)
                step(V.tensor_reduce(mx[:, a, 2:3], Pc[:, a, 0:NCMP], AX.X, ALU.max))
                V.tensor_scalar(ngm[:, a, 0:3], mx[:, a, 0:3], -SCALE, None, ALU.mult).then_inc(max_ready, 1)

            def nsa_scale(u):
                h, qb = divmod(u, TB)
                a, nk = u % 2, (qb + 1) * P
                dve.wait_ge(exp_done, u + 1)
                step(V.reciprocal(rz[:, a, 0:3], sums[:, a, 0:3]))
                step(V.tensor_tensor(gz[:, a, 0:3], rz[:, a, 0:3], gates_for(h, qb), ALU.mult))
                for br in range(2):
                    sl = SP[:, a, br * T:br * T + nk]
                    V.tensor_scalar(sl, sl, gz[:, a, br:br + 1], None, ALU.mult)
                V.scalar_tensor_tensor(out=Pc[:, a, 0:NCMP], in0=Pc[:, a, 0:NCMP], scalar=gz[:, a, 2:3],
                                       in1=prm("cvalid", qb * NCMP, (qb + 1) * NCMP),
                                       op0=ALU.mult, op1=ALU.mult).then_inc(probs_ready, 1)

            def gates_for(h, qb):
                return gates[:, qb, 3 * h:3 * h + 3]

            def nsa_out(h):
                dve.wait_ge(o_done, 2 * h + 2)
                g = pT[:, GN0 + h, :]
                V.tensor_tensor(g, bank[2 + h % 2][:, 0:T], g, ALU.mult).then_inc(o_read, 1)

            units = HQ * TB
            dve.wait_ge(gates_ready, 1)
            dve.wait_ge(silu_done, 2)
            nsa_mask(0)
            for u in range(units):
                if u + 1 < units:
                    nsa_mask(u + 1)
                nsa_scale(u)
                if u % 2 == 1 and u >= 3:
                    nsa_out(u // 2 - 1)
            nsa_out(HQ - 1)
            for g in range(NG):
                dve.wait_ge(z_ready, g + 1)
                for e in range(2):
                    c = 2 * g + e
                    last = V.scalar_tensor_tensor(out=pT[:, U0 + c, :], in0=bank[4 + g][:, e * T:(e + 1) * T],
                                                  scalar=prm("pscale", c, c + 1), in1=pT[:, GP0 + c, :],
                                                  op0=ALU.mult, op1=ALU.mult)
                last.then_inc(y_pool, 1)
            phase("merge", keep, keep)
            for b in range(2):
                dve.wait_ge(bank_free[b], B0["pool_out"][b])
            with dve.Fori(0, G0["pool_out"][1]) as i:
                for s in range(RING):
                    dve.wait_ge(raw_free[s % 2], consumed("pool_out", i, s))
                    gsl = R[:, bass.ds(i * (8 * T) + (16 + 2 * s) * T, 2 * T)]
                    V.tensor_tensor(gsl, bank[s][:], gsl, ALU.mult).then_inc(bank_free[s], 1)
            for s in range(RING):
                dve.wait_ge(bank_free[s], B0["nsa_out"][s])
            with dve.Fori(0, G0["nsa_out"][1]) as i:
                for b in range(2):
                    dve.wait_ge(raw_free[1], consumed("nsa_out", i, 2 * b + 1))
                    g1 = R[:, bass.ds(i * (4 * T) + (32 + 2 * b) * T, 2 * T)]
                    gm = R[:, bass.ds(i * (4 * T) + (16 + 2 * b) * T, 2 * T)]
                    V.tensor_tensor(g1, bank[b][:], g1, ALU.mult).then_inc(bank_free[b], 1)
                    dve.wait_ge(bank_free[b], i + B0["nsa_out"][b] + 1)
                    V.tensor_tensor(gm, gm, g1, ALU.add).then_inc(merged_ready, 1)
            for g in range(G0["out1"][1]):
                dve.wait_ge(raw_free[1], consumed("out1", g, 3))
                residual(g, x1_ready)
            root_mean_square(1)
            dve.wait_ge(fnw1_in, 16)
            for b in range(TB):
                V.scalar_tensor_tensor(out=xres[:, b, :], in0=xres[:, b, :], scalar=rstd[:, b:b + 1],
                                       in1=fnw1_sb, op0=ALU.mult, op1=ALU.mult).then_inc(x1_normed, 1)

            norm(1, "norm2", 2)
            dve.wait_ge(rowsT_ready, 1)
            V.tensor_scalar(rows[0:8, 0, :], bank[5][0:8, 0:T], prm_rows("fbias", 8), None, ALU.add)
            V.tensor_scalar(rows[0:4, 1, :], bank[6][0:4, 0:T], prm_rows("ibias", 4), None, ALU.add)
            step(V.tensor_scalar(rows[0:4, 2, :], bank[7][0:4, 0:T], prm_rows("mfbias", 4), None, ALU.add))
            step(V.tensor_scalar(rows[0:8, 4, :], rows[0:8, 0, :], -1.0, None, ALU.mult))
            step(V.tensor_scalar(rows[0:4, 5, :], rows[0:4, 2, :], -1.0, None, ALU.mult))
            V.tensor_tensor(rows[0:8, 4, :], rows[0:8, 4, :], rows[0:8, 0, :], ALU.min)
            V.tensor_tensor(rows[0:4, 5, :], rows[0:4, 5, :], rows[0:4, 2, :], ALU.min).then_inc(row_y, 1)
            V.tensor_scalar(rows[0:8, 0, :], rows[0:8, 0, :], 0.0, None, ALU.min)
            step(V.tensor_scalar(rows[0:4, 2, :], rows[0:4, 2, :], 0.0, None, ALU.min))
            dve.wait_ge(row_l, 1)
            V.tensor_tensor(rows[0:8, 0, :], rows[0:8, 0, :], rows[0:8, 4, :], ALU.subtract)
            step(V.tensor_tensor(rows[0:4, 2, :], rows[0:4, 2, :], rows[0:4, 5, :], ALU.subtract))
            ones8 = bc(prm_rows("cone", 8), [8, T])
            V.tensor_tensor_scan(rows[0:8, 6, :], ones8, rows[0:8, 0, :], 0.0, ALU.mult, ALU.add)
            for c in range(TB):
                cs = slice(c * P, (c + 1) * P)
                last = V.tensor_tensor_scan(rows[0:4, 8, cs], bc(prm_rows("cone", 4), [4, P]), rows[0:4, 2, cs], 0.0,
                                            ALU.mult, ALU.add)
            step(last)
            V.tensor_scalar(rows[0:8, 7, :], rows[0:8, 6, :], -1.0, None, ALU.mult)
            step(V.tensor_tensor(rows[0:4, 9, :], rows[0:4, 1, :], rows[0:4, 8, :], ALU.subtract))
            bl = rows[0:4, 8, P - 1:P]
            step(V.tensor_reduce(rowst[0:4, 0:1], rows[0:4, 9, 0:P], AX.X, ALU.max))
            step(V.tensor_tensor(rowst[0:4, 0:1], rowst[0:4, 0:1], bl, ALU.add))
            step(V.tensor_tensor(rowst[0:4, 2:3], rowst[0:4, 0:1], bl, ALU.max))
            V.tensor_copy(rows[0:4, 10, 0:P], rows[0:4, 8, 0:P])
            V.tensor_scalar(rows[0:4, 10, P:T], rows[0:4, 8, P:T], rowst[0:4, 2:3], None, ALU.add)
            V.tensor_tensor(rowst[0:4, 1:2], bl, rowst[0:4, 2:3], ALU.subtract).then_inc(a_ready, 1)
            evac_t("in2_t")
            evac_n("in2_n", vN2)
            dve.wait_ge(bank_free[1], B0["in2_n"][1])
            for j in range(8):
                src, y = pT[:, MQ0 + j, :], conv[:, j, :]
                cw = prm("convw", 4 * j, 4 * j + 4)
                step(V.tensor_scalar(y, src, cw[:, 3:4], prm("convb", j, j + 1), ALU.mult, ALU.add))
                for tap in range(3):
                    sh = 3 - tap
                    last = V.scalar_tensor_tensor(out=y[:, sh:T], in0=src[:, 0:T - sh], scalar=cw[:, tap:tap + 1],
                                                  in1=y[:, sh:T], op0=ALU.mult, op1=ALU.add)
                    if tap < 2:
                        step(last)
                last.then_inc(conv_done, 1)
            V.tensor_scalar(pT[:, FQ0:FQ0 + 8, :], pT[:, FQ0:FQ0 + 8, :], SCALE, None, ALU.mult).then_inc(q_ready, 1)
            dve.wait_ge(conv_silu, 1)
            V.tensor_scalar(conv[:, 4:8, :], conv[:, 4:8, :], SCALE, None, ALU.mult).then_inc(q_ready, 1)
            dve.wait_ge(nat_copied, 1)
            dve.wait_ge(bank_free[0], B0["out2"][0])
            dve.wait_ge(bank_free[2], B0["out2"][2])
            for h in range(MH):
                a_col = natc[:, 32 + h:33 + h]
                if h >= 1:
                    dve.wait_ge(C_ready, h)
                V.tensor_scalar(av[:, 0:MV], vN2[:, 2 + h // 2, 0, (h % 2) * MV:(h % 2 + 1) * MV], a_col, None, ALU.mult)
                V.tensor_copy(av[:, MV:MV + 1], a_col).then_inc(av_ready, 1)
                dve.wait_ge(C_ready, h + 1)
                V.tensor_copy(CN[:, h, 0:MV + 1], bank[6][:, 0:MV + 1]).then_inc(C_copied, 1)

            def fox_mask(u):
                h, qb = divmod(u, TB)
                a, nk = u % 2, (qb + 1) * P
                dve.wait_ge(f_scores, u + 1)
                if u >= 2:
                    dve.wait_ge(f_T, u - 1)
                V.scalar_tensor_tensor(out=SP2[:, a, 0:nk], in0=bank[4 + a][:, 0:nk],
                                       scalar=natc[:, 8 * qb + h:8 * qb + h + 1], in1=prm("mask", 256 - nk, 256),
                                       op0=ALU.add, op1=ALU.add).then_inc(f_read, 1)
                dve.wait_ge(f_read, u + 1)
                step(V.tensor_reduce(mx[:, a, 0:1], SP2[:, a, 0:nk], AX.X, ALU.max))
                V.tensor_scalar(ngm[:, a, 0:1], mx[:, a, 0:1], -1.0, None, ALU.mult).then_inc(f_max, 1)

            def fox_out(u):
                h, qb = divmod(u, TB)
                a = u % 2
                dve.wait_ge(f_exp, u + 1)
                step(V.reciprocal(rz[:, a, 0:1], sums[:, a, 0:1]))
                dve.wait_ge(f_o, u + 1)
                V.tensor_scalar(scr2[:, qb, h * DH:(h + 1) * DH], bank[2 + a][:, 0:DH], rz[:, a, 0:1], None,
                                ALU.mult).then_inc(f_oread, 1)

            units = FH * TB
            fox_mask(0)
            for u in range(units):
                if u + 1 < units:
                    if u >= 1:
                        fox_out(u - 1)
                    fox_mask(u + 1)
            fox_out(units - 2)
            fox_out(units - 1)

            def m_mask(u):
                c, h = divmod(u, MH)
                a = u % 2
                dve.wait_ge(m_scores, u + 1)
                g_col = natc[:, 24 + 4 * c + h:25 + 4 * c + h]
                step(V.scalar_tensor_tensor(out=Dm[:, a, :], in0=bank[4 + a][:, P:2 * P],
                                            scalar=natc[:, 16 + 4 * c + h:17 + 4 * c + h], in1=tri,
                                            op0=ALU.add, op1=ALU.add))
                step(V.tensor_reduce(mst[:, a, 0:1], Dm[:, a, :], AX.X, ALU.max))
                step(V.tensor_tensor(mst[:, a, 0:1], mst[:, a, 0:1], g_col, ALU.max))
                V.tensor_scalar(mst[:, a, 1:2], mst[:, a, 0:1], -1.0, None, ALU.mult)
                V.tensor_tensor(mst[:, a, 2:3], g_col, mst[:, a, 0:1], ALU.subtract).then_inc(m_max, 1)

            def m_weigh(u):
                a = u % 2
                dve.wait_ge(m_exp, u + 1)
                if u >= 2:
                    dve.wait_ge(m_T, u - 1)
                V.tensor_tensor_reduce(Sm[:, a, :], bank[4 + a][:, 0:P], Dm[:, a, :], 1.0, 0.0, ALU.mult, ALU.add,
                                       mst[:, a, 5:6]).then_inc(m_sm, 1)

            def m_out(u):
                c, h = divmod(u, MH)
                a = u % 2
                dve.wait_ge(m_num, u + 1)
                dve.wait_ge(m_sm, u + 1)
                if c == 1:
                    step(V.tensor_scalar(numt[:, a, :], bank[a][:, 0:MV], mst[:, a, 4:5], None, ALU.mult))
                    V.scalar_tensor_tensor(out=mst[:, a, 5:6], in0=bank[a][:, MV:MV + 1], scalar=mst[:, a, 4:5],
                                           in1=mst[:, a, 5:6], op0=ALU.mult, op1=ALU.add)
                    step(V.tensor_tensor(numt[:, a, :], bank[2 + a][:, 0:MV], numt[:, a, :], ALU.add))
                else:
                    step(V.tensor_copy(numt[:, a, :], bank[2 + a][:, 0:MV]))
                step(V.tensor_scalar(mst[:, a, 6:7], mst[:, a, 5:6], -1.0, None, ALU.mult))
                step(V.tensor_tensor(mst[:, a, 6:7], mst[:, a, 6:7], mst[:, a, 5:6], ALU.max))
                step(V.tensor_tensor(mst[:, a, 6:7], mst[:, a, 6:7], mst[:, a, 3:4], ALU.max))
                step(V.reciprocal(mst[:, a, 7:8], mst[:, a, 6:7]))
                V.tensor_scalar(scr2[:, c, 1024 + h * MV:1024 + (h + 1) * MV], numt[:, a, :], mst[:, a, 7:8], None,
                                ALU.mult).then_inc(m_read, 1)

            units = MH * TB
            m_mask(0)
            m_weigh(0)
            for u in range(units):
                if u + 1 < units:
                    m_mask(u + 1)
                    m_weigh(u + 1)
                m_out(u)
            dve.wait_ge(mo_sig, 1)
            dve.wait_ge(m_read, units)
            for b in range(TB):
                for g in range(2):
                    sl = scr2[:, b, 1024 + g * 512:1024 + (g + 1) * 512]
                    last = V.tensor_tensor(sl, sl, vN2[:, 4 + g, b, :], ALU.mult)
            last.then_inc(cells, 1)
            dve.wait_ge(head_sq, 1)
            sq = region(0, 4096).rearrange("p (b d) -> p b d", b=TB)
            for b in range(TB):
                V.tensor_reduce(hss[:, b, 0:8], sq[:, b, 0:1024].rearrange("p (h e) -> p h e", h=FH), AX.X, ALU.add)
                last = V.tensor_reduce(hss[:, b, 8:12], sq[:, b, 1024:2048].rearrange("p (h e) -> p h e", h=MH), AX.X,
                                       ALU.add)
            step(last)
            V.tensor_scalar(hss[:, :, 0:8], hss[:, :, 0:8], 1.0 / DH, EPS, ALU.mult, ALU.add)
            V.tensor_scalar(hss[:, :, 8:12], hss[:, :, 8:12], 1.0 / MV, EPS, ALU.mult, ALU.add).then_inc(head_ms, 1)
            dve.wait_ge(head_rt, 1)
            step(V.reciprocal(hrt, hrt))
            for b in range(TB):
                fa = scr2[:, b, 0:1024].rearrange("p (h e) -> p h e", h=FH)
                ce = scr2[:, b, 1024:2048].rearrange("p (h e) -> p h e", h=MH)
                V.tensor_tensor(fa, fa, bc(hrt[:, b, 0:8].unsqueeze(2), [P, FH, DH]), ALU.mult)
                V.tensor_tensor(ce, ce, bc(hrt[:, b, 8:12].unsqueeze(2), [P, MH, MV]), ALU.mult).then_inc(xn_ready, 1)
            read_turned(2, "mixnorm")

            def add_out2(g):
                dve.wait_ge(slot_used[1], multiplied("out2", g, 3))
                residual(g, x2_ready)
            phase_n("out2", add_out2)

            norm(3, "norm3", 3)
            evac_t("wq")
            for f in range(8):
                b, j = divmod(f, 4)
                dve.wait_ge(qs_copied, f + 1)
                for hp in range(4 * j, 4 * j + 4):
                    sc, wk = scores[:, b, hp, :], work[:, b, hp, :]
                    tv, ti = topv[:, b, hp, :], topi[:, b, hp, :]
                    step(V.max(tv[:, 0:8], sc))
                    V.max_index(ti[:, 0:8], tv[:, 0:8], sc)
                    step(V.match_replace(wk, tv[:, 0:8], sc, LOWEST))
                    step(V.max(tv[:, 8:16], wk))
                    last = V.max_index(ti[:, 8:16], tv[:, 8:16], wk)
            step(last)
            step(V.tensor_copy(topf, topi))
            for b in range(TB):
                tv4 = topv[:, b].rearrange("p (h s) k -> p h s k", s=2)
                c4 = cand[:, b].rearrange("p h (i j) -> p h i j", i=TOPK)
                step(V.tensor_tensor(c4, bc(tv4[:, :, 0, :].unsqueeze(3), [P, PH, TOPK, TOPK]),
                                     bc(tv4[:, :, 1, :].unsqueeze(2), [P, PH, TOPK, TOPK]), ALU.add))
                for h in range(PH):
                    cd, wk = cand[:, b, h, :], cwork[:, b, h, :]
                    tv, ti = finv[:, b, h, :], fini[:, b, h, :]
                    step(V.max(tv[:, 0:8], cd))
                    V.max_index(ti[:, 0:8], tv[:, 0:8], cd)
                    step(V.match_replace(wk, tv[:, 0:8], cd, LOWEST))
                    step(V.max(tv[:, 8:16], wk))
                    last = V.max_index(ti[:, 8:16], tv[:, 8:16], wk)
                step(last)
                pos = fini[:, b].rearrange("p h k -> p (h k)")
                V.tensor_scalar(fab_u[:, 0, b, :], pos, 4, None, ALU.logical_shift_right)
                step(V.tensor_scalar(fab_u[:, 1, b, :], pos, 15, None, ALU.bitwise_and))
                for s in range(2):
                    last = V.tensor_copy(fab[:, s, b].rearrange("p h k -> p (h k)"), fab_u[:, s, b, :])
                step(last)
                step(V.tensor_copy(zs[:, b, :], finv[:, b, :, 0]))
                V.tensor_tensor(finv[:, b], finv[:, b], bc(zs[:, b, :].unsqueeze(2), [P, PH, TOPK]),
                                ALU.subtract).then_inc(gate_arg, 1)
                tf4 = topf[:, b].rearrange("p (h s) k -> p h s k", s=2)
                for s in range(2):
                    step(V.tensor_tensor(onehot, bc(fab[:, s, b].unsqueeze(3), [P, PH, TOPK, TOPK]),
                                         bc(prm("iota", 0, TOPK).unsqueeze(1).unsqueeze(1), [P, PH, TOPK, TOPK]),
                                         ALU.is_equal))
                    step(V.tensor_tensor(onehot, onehot, bc(tf4[:, :, s, :].unsqueeze(2), [P, PH, TOPK, TOPK]),
                                         ALU.mult))
                    step(V.tensor_reduce(chosen[:, b, s, :].rearrange("p (h k) -> p h k", h=PH), onehot, AX.X, ALU.add))
                dve.wait_ge(gate_exp, b + 1)
                step(V.tensor_reduce(zs[:, b, :], finv[:, b], AX.X, ALU.add))
                step(V.reciprocal(zs[:, b, :], zs[:, b, :]))
                V.tensor_tensor(chosen[:, b, 2, :].rearrange("p (h k) -> p h k", h=PH), finv[:, b],
                                bc(zs[:, b, :].unsqueeze(2), [P, PH, TOPK]), ALU.mult).then_inc(chosen_ready, 1)
            dve.wait_ge(chosenT_copied, TB)
            with dve.Fori(0, T // 8) as i:
                for q in range(4):
                    dve.wait_ge(pair_free, i * 4 + q + 1)
                    for t in range(2):
                        def col(s):
                            return idxT[:, s, bass.ds(i * 8 + 2 * q + t, 1)]
                        V.tensor_scalar(pairs[:, q % 2, t, 0, :], prm("iota"), col(1), None, ALU.is_equal)
                        last = V.tensor_scalar(pairs[:, q % 2, t, 1, :], prm("iota"), col(0), col(2),
                                               ALU.is_equal, ALU.mult)
                    last.then_inc(pair_ready, 1)
            dve.wait_ge(g_evac, 2 + T // 4)

            def gate(name, b):
                def evac(i):
                    dve.wait_ge(bank_free[b], i + B0[name][b] + 1)
                    gb = gate_block(i * 4 + 2 * b, 2)
                    V.tensor_tensor(gb, gb, gelu_u[:, b, :].rearrange("p (j g t) -> p g j t", j=2, t=4),
                                    ALU.mult).then_inc(gated[b], 1)
                return evac

            def add_experts(half, ready):
                name = f"peer_v{half}"
                dve.wait_ge(slot_used[1], multiplied(name, G0[name][1] - 1, 3))
                for c in range(8):
                    xs = xres[:, c // 4, (c % 4) * 512:(c % 4 + 1) * 512]
                    V.tensor_tensor(xs, bank[c][:], xs, ALU.add).then_inc(ready, 1)

            def between_halves():
                add_experts(0, v_read)
                dve.wait_ge(gates_in, 16)

            for half in range(2):
                name = f"peer_u{half}"
                phase(name, gate(name, 0), gate(name, 1), between_halves if half else None)
                for b in range(2):
                    dve.wait_ge(gated[b], 1 + (half + 1) * G0["peer_u0"][1])
                with dve.Fori(0, G0["peer_v0"][1]) as i:
                    for s in range(RING):
                        split(f"peer_v{half}", i, s)
            add_experts(1, x3_ready)
            root_mean_square(4)
            dve.wait_ge(fnw_in, 16)
            for b in range(TB):
                V.scalar_tensor_tensor(out=R[:, b * D:(b + 1) * D], in0=xres[:, b, :], scalar=rstd[:, b:b + 1],
                                       in1=raw[0][:], op0=ALU.mult, op1=ALU.mult).then_inc(result, 1)


PARAMS.append(("cone", 1))


def cols_t(w):
    k, n = w.shape
    return w.reshape(k // P, P, n // P, P).transpose(2, 1, 0, 3).reshape(n // P, P, k)


def cols_n(w):
    n = w.shape[1]
    return w.reshape(4, 4, P, n // 512, 512).transpose(3, 0, 2, 1, 4).reshape(n // 512 * 4, P, SLOT)


def on_partitions(v):
    return v.reshape(-1, P).T


def layout(i):
    f = np.float32
    cut = np.cumsum([0, POOL_W, POOL_W, 2048, 512, 512, 512, 512, 512, 512, 2048, 48])
    w1 = i["w_in"][0]
    part = [w1[:, a:b] for a, b in zip(cut[:-1], cut[1:])]
    u, gp, q, kcr, vcr, ks, vs, kw, vw, gn, gb = part
    cut2 = np.cumsum([0, 1024, 1024, 1024, 8, 512, 512, 1024, 4, 4, 1024])
    fq, fk, fv, ff, mq, mk, mv, mi, mf, mo = [i["w_in_2"][0][:, a:b] for a, b in zip(cut2[:-1], cut2[1:])]

    def cmp_w1(w):
        return w[0].reshape(RING, 8, P, CH).transpose(0, 2, 1, 3).reshape(RING, P, SLOT)

    pool_out = cols_t(i["w_pool_out"][0]).reshape(8, 2, P, 1024).transpose(0, 2, 1, 3).reshape(8, P, SLOT)
    peer_u = i["peer_u_2"][0].reshape(NK, P, KC, P).transpose(0, 3, 2, 1).reshape(NK, P, SLOT)
    peer_v = i["peer_v_2"][0].reshape(NK, P, SLOT)
    stream = np.concatenate([
        *(cols_t(w) for w in (u, gp, kcr, vcr, ks, kw, q, gn)), cols_n(vs), cols_n(vw),
        cmp_w1(i["cmp_w1_k"]), cmp_w1(i["cmp_w1_v"]), cols_t(i["w_merge"][0]), pool_out,
        cols_t(i["w_nsa_out"][0]), cols_n(i["w_out"][0]),
        *(cols_t(w) for w in (fq, fk, mq, mk)), *(cols_n(w) for w in (fv, mv, mo)),
        cols_n(i["w_out_2"][0]), cols_t(i["peer_w_q_2"][0]),
        *(w[half * HALF:(half + 1) * HALF] for half in range(2) for w in (peer_u, peer_v))])

    t = np.arange(T)
    inv = (f(10000.0) ** (-np.arange(64, dtype=f) / f(64))).astype(f)

    def rot(pos):
        ang = (pos.astype(f)[None, :] * inv[:, None]).astype(f)
        c, s = np.cos(ang), np.sin(ang)
        return np.concatenate([c, c]).astype(f), np.concatenate([-s, s]).astype(f)

    cos, sin = rot(t)
    ccos, csin = (np.tile(a, (1, HKV)) for a in rot(np.arange(NCMP) * CS + CB - 1))
    tri = np.where(np.arange(P)[None, :] <= np.arange(P)[:, None], 0, NEG)
    valid = (np.arange(NCMP) * CS + CB - 1)[None, :] <= t[:, None]
    per_block = lambda a: a.reshape(TB, P, NCMP).transpose(1, 0, 2).reshape(P, TB * NCMP)
    table = {
        "ident": np.eye(P), "mask": np.concatenate([np.zeros((P, P)), tri], 1), "cos": cos, "sin": sin,
        "ccos": ccos, "csin": csin, "cmask": per_block(np.where(valid | ~valid.any(1, keepdims=True), 0, NEG)), "cvalid": per_block(valid),
        "iota": np.tile(np.arange(P), (P, 1)), "cone": np.ones((P, 1)),
        "norm1": on_partitions(i["norm_w"][0]), "norm2": on_partitions(i["norm1_w_2"][0]),
        "norm3": on_partitions(i["norm2_w_2"][0]),
        "mixnorm": on_partitions(np.concatenate([i["fox_out_norm_w_2"][0], i["mlstm_out_norm_w_2"][0]])),
        "pscale": on_partitions(i["pool_scale"][0]), "bmerge": on_partitions(i["b_merge"][0]),
        "pek": i["cmp_pe_k"][0].T, "pev": i["cmp_pe_v"][0].T,
        "convw": i["mlstm_conv_w_2"][0].reshape(4, 8, P).transpose(2, 1, 0).reshape(P, 32),
        "convb": on_partitions(i["mlstm_conv_b_2"][0]),
        "fbias": i["fox_f_bias_2"][0][:, None], "ibias": i["mlstm_i_bias_2"][0][:, None],
        "mfbias": i["mlstm_f_bias_2"][0][:, None],
        "keysT": i["peer_keys_2"][0].transpose(2, 0, 1).reshape(P, 2 * NK),
        "wrows": np.concatenate([ff, mi, mf], 1).reshape(KC, P, 16).transpose(1, 0, 2).reshape(P, KC * 16),
    }
    cnt = np.minimum(t[None, :] + 1, np.array(WINDOWS)[:, None]).astype(f)
    gb3 = gb.reshape(D, HQ, 3)[:, :, [1, 2, 0]].reshape(KC, P, 48)
    table1 = {
        "invcnt": np.tile((f(1) / cnt[:, :16]).reshape(1, NG * 16), (P, 1)),
        "wgbr": gb3.transpose(1, 0, 2).reshape(P, KC * 48),
        "w2k": i["cmp_w2_k"][0].reshape(2, P, DH).transpose(1, 0, 2).reshape(P, 2 * DH),
        "w2v": i["cmp_w2_v"][0].reshape(2, P, DH).transpose(1, 0, 2).reshape(P, 2 * DH),
    }

    def packed(names, values):
        off, n = offsets(names)
        a = np.zeros((P, n), f)
        for name, (o, w) in off.items():
            v = values[name]
            assert v.shape[1] == w, name
            a[:v.shape[0], o:o + w] = v
        return a

    return {"x": i["x"], "stream": stream, "params": packed(PARAMS, table), "stage1": packed(STAGE1, table1),
            "mixw": i["pool_mix"][0].reshape(NG, 2, P, 256).transpose(2, 0, 1, 3).reshape(P, 2048), "fnw1": i["final_norm_w"], "fnw": i["final_norm_w_2"]}


def kernel(**inputs):
    import concourse.bacc as bacc
    from concourse.bass_utils import run_bass_kernel_spmd

    arrays = {n: np.ascontiguousarray(a) for n, a in layout({k: np.asarray(v) for k, v in inputs.items()}).items()}
    nc = bacc.Bacc("TRN2", target_bir_lowering=False, num_devices=1)
    args = [nc.dram_tensor(n, a.shape, F32, kind="ExternalInput").ap() for n, a in arrays.items()]
    out = nc.dram_tensor("out", (1, T, D), F32, kind="ExternalOutput").ap()
    gates_dram = nc.dram_tensor("gates_dram", (T // 4, P, HALF * 4), F32, kind="Internal").ap()
    build_two_blocks(nc, *args, gates_dram, out)
    r = run_bass_kernel_spmd(nc, [arrays], core_ids=[0])
    return r.results[0]["out"]
```

```python
from contextlib import ExitStack

import numpy as np

import concourse.bass as bass
from concourse import mybir

ALU = mybir.AluOpType
ACT = mybir.ActivationFunctionType
AX = mybir.AxisListType
F32 = mybir.dt.float32
F32R = mybir.dt.float32r
U32 = mybir.dt.uint32

P = 128
T = 256
TB = T // P
D = 2048
KC = D // P
EPS = 1e-6
NEG = -1e30
LOWEST = -3.0e38
RING = 4
SLOT = 2048

POOL_W = 1024
WINDOWS = (2, 4, 8, 16)
NG = len(WINDOWS)
HQ, HKV, DH = 16, 4, 128
GQ = HQ // HKV
CB, CS, CH = 32, 16, 256
NCMP = (T - CB) // CS + 1
NC4 = HKV * NCMP
FH = 8
MH, MV = 4, 256
PH, NK, TOPK = 8, 128, 16
HK = PH * TOPK
NE_BLOCKS = NK

SCALE = float(DH) ** -0.5

PHASES = [("in_t", 16), ("in_n", 2), ("narrow1", 0.5), ("cmp", 2), ("merge", 8), ("pool_out", 2), ("nsa_out", 4),
          ("out1", 4), ("in2_t", 6), ("narrow2", 0.5), ("in2_n", 6), ("out2", 4), ("wq", 4),
          ("peer_u0", 16), ("peer_v0", 16), ("peer_u1", 16), ("peer_v1", 16)]
RAW = ("cmp", "pool_out")
HALF = NK // 2
CHOOSE_G, MAKE_G = 10, 4
EARLY = RING * CHOOSE_G
TRACK = 8
PAIRS = int(2 * sum(n for _, n in PHASES))
MERGE_ORDER = (0, 1, 4, 5, 6, 7, 2, 3)
MERGE_EARLY = 5
MERGE_AT = [n * HQ * TB // (RING * MERGE_EARLY) for n in range(RING * MERGE_EARLY)]
ROW_AT = (0, 32, 64)

PARAMS = [("ident", 128), ("mask", 256), ("cos", 256), ("sin", 256), ("ccos", NC4), ("csin", NC4),
          ("cmask", TB * NCMP), ("cvalid", TB * NCMP), ("iota", 128),
          ("norm1", KC), ("norm2", KC), ("norm3", KC), ("mixnorm", KC), ("pscale", 8), ("bmerge", 32),
          ("pek", CB), ("pev", CB), ("convw", 32), ("convb", 8), ("fbias", 1), ("ibias", 1), ("mfbias", 1),
          ("keysT", 2 * NK), ("cone", 1)]
STAGE1 = [("invcnt", NG * 16), ("w2k", 2 * DH), ("w2v", 2 * DH)]
R_WORDS = 25088


def offsets(table):
    at, out = 0, {}
    for name, width in table:
        out[name] = (at, width)
        at += width
    return out, at


def first_pairs():
    at, out = 0, {}
    for name, n in PHASES:
        out[name] = (at, n)
        at += int(2 * n)
    return out


def split_pairs():
    at, out = 0, {}
    for name, n in PHASES:
        out[name] = at
        at += 0 if name in RAW else int(2 * n)
    return out


def fills_per_bank(name, n):
    if name in ("in_t", "merge", "nsa_out", "in2_t", "wq", "peer_u0", "peer_u1"):
        return (n, n, 0, 0)
    if name in ("in_n", "out1", "in2_n", "out2"):
        return (n // 2,) * 4
    if name == "pool_out":
        return (n,) * 4
    return (0,) * 4


def earlier_fills():
    at, out = [1] * 4, {}
    for name, n in PHASES:
        out[name] = tuple(at)
        at = [a + f for a, f in zip(at, fills_per_bank(name, n))]
    return out


def build_two_blocks(nc, x, stream, params, stage1, mixw_in, fnw1, fnw, gates_dram, out):
    PO, n_params = offsets(PARAMS)
    S1, n_stage1 = offsets(STAGE1)
    G0 = first_pairs()
    B0 = earlier_fills()
    S0 = split_pairs()

    with ExitStack() as ctx:
        def sb(name, shape, dt=F32):
            return ctx.enter_context(nc.sbuf_tensor(name, shape, dt))

        def sem(name):
            return ctx.enter_context(nc.semaphore(name))

        bank = [ctx.enter_context(nc.psum_tensor(f"bank{b}", [P, 512], F32)) for b in range(8)]

        raw = [sb(f"raw{s}", [P, SLOT]) for s in range(2)]
        whi = [sb(f"whi{s}", [P, SLOT], F32R) for s in range(2)]
        wlo = [sb(f"wlo{s}", [P, SLOT], F32R) for s in range(2)]
        xres = sb("xres", [P, TB, D])
        hTh = sb("hTh", [P, KC, T], F32R)
        hTl = sb("hTl", [P, KC, T], F32R)
        ghi = sb("ghi", [P, 2, T], F32R)
        glo = sb("glo", [P, 2, T], F32R)
        par = sb("par", [P, n_params])
        R = sb("R", [P, R_WORDS])
        st = sb("st", [P, 320])

        def prm(name, a=0, b=None):
            o, w = PO[name]
            return par[:, o + a:o + (w if b is None else b)]

        def prm_rows(name, n):
            o, _ = PO[name]
            return par[0:n, o:o + 1]

        def region(a, n):
            return R[:, a:a + n]

        ident = prm("ident")
        tri = prm("mask", 128, 256)

        pT = region(0, 64 * T).rearrange("p (j t) -> p j t", t=T)
        U0, GP0, KCR0, VCR0, KS0, KW0, Q0, GN0 = 0, 8, 16, 20, 24, 28, 32, 48
        kb_at = (16384, 18304)
        kb = [region(a, CB * NC4).rearrange("p (l c) -> p l c", l=CB) for a in kb_at]
        PAD = 16
        W = T + PAD
        pool_buf = [region(16384 + a * 2 * W, 2 * W).rearrange("p (c t) -> p c t", c=2) for a in range(2)]
        vN1_at = 20224
        vN1 = region(vN1_at, 2048).rearrange("p (g b c) -> p g b c", g=2, b=TB)
        fnw1_sb = region(vN1_at, D)
        rot_buf = region(24064, 1024)
        gbr_rows = R[0:48, 23000:23000 + T]
        mixw_sb = region(23040, 2048)
        stage1_at = 22272
        tmp_at = 24064
        turned_tmp = region(tmp_at, 1024).rearrange("p (a k) -> p a k", a=2)
        scr_of = [region(a, 4096) for a in (12288, 12288, 17408, 17408)]
        scr = scr_of[2]
        scr2 = scr.rearrange("p (b d) -> p b d", b=TB)
        SP = region(17552, 1024).rearrange("p (a k) -> p a k", a=2)
        PT = region(18576, 1024).rearrange("p (a k) -> p a k", a=2)

        def s1(name):
            o, w = S1[name]
            return region(stage1_at + o, w)
        k0 = kb_at[0]
        vcs = R[0:NCMP, k0:k0 + 512]
        kcT = region(k0 + 512, NC4)
        kcS = region(k0 + 576, NC4)
        PcT = R[0:NCMP, k0 + 640:k0 + 896].rearrange("p (a q) -> p a q", a=2)
        Pc = region(k0 + 896, 32).rearrange("p (a k) -> p a k", a=2)
        hdn = region(k0 + 928, 4 * NC4).rearrange("p (v f c) -> p v f c", v=2, f=2)
        assert k0 + 928 + 4 * NC4 <= 17552 and stage1_at + n_stage1 <= tmp_at
        gate0 = pT[:, 16:32, :]
        gate1 = pT[:, 32:48, :]

        FQ0, FK0, MQ0, MK0 = 0, 8, 16, 20
        vN2 = region(6144, 6144).rearrange("p (g b c) -> p g b c", g=6, b=TB)
        conv = region(12288, 2048).rearrange("p (j t) -> p j t", t=T)
        SP2 = region(4096, 1024).rearrange("p (a k) -> p a k", a=2)
        PT2 = region(5120, 1024).rearrange("p (a k) -> p a k", a=2)
        rows = region(14336, 3072).rearrange("p (j t) -> p j t", t=T)
        knat = region(21504, 512).rearrange("p (h d) -> p h d", h=MH)
        av = region(22016, 264)
        CN = region(22280, 4 * 264).rearrange("p (h e) -> p h e", h=MH)
        Dm = region(23336, 256).rearrange("p (a s) -> p a s", a=2)
        Sm = region(23592, 256).rearrange("p (a s) -> p a s", a=2)
        SmT = region(23848, 256).rearrange("p (a s) -> p a s", a=2)
        numt = region(24104, 512).rearrange("p (a e) -> p a e", a=2)
        natc = region(24648, 64)

        qT3 = region(0, 4096).rearrange("p (j t) -> p j t", t=T)
        sc_at = HALF * T
        scores = region(sc_at, 4096).rearrange("p (u n) -> p u n", n=NK)
        cand = region(sc_at, 4096).rearrange("p (b h c) -> p b h c", b=TB, h=PH)
        onehots = region(sc_at, 4096).rearrange("p (b h k j) -> p b h k j", b=TB, h=PH, k=TOPK)
        topv = region(sc_at + 4096, 512).rearrange("p (u k) -> p u k", k=TOPK)
        topi = region(sc_at + 4608, 512).bitcast(U32).rearrange("p (u k) -> p u k", k=TOPK)
        topf = region(sc_at + 5120, 512).rearrange("p (u k) -> p u k", k=TOPK)
        finv = region(sc_at + 5632, 256).rearrange("p (b h k) -> p b h k", b=TB, h=PH)
        fini = region(sc_at + 5888, 256).bitcast(U32).rearrange("p (b h k) -> p b h k", b=TB, h=PH)
        fab_u = region(sc_at + 6144, 512).bitcast(U32).rearrange("p (s b c) -> p s b c", s=2, b=TB)
        fab = region(sc_at + 6656, 512).rearrange("p (s b h k) -> p s b h k", s=2, b=TB, h=PH)
        chosen = region(sc_at + 7168, 768).rearrange("p (b s c) -> p b s c", b=TB, s=3)
        idxT = region(sc_at, 768).rearrange("p (s t) -> p s t", s=3)
        first_hot = region(sc_at + 768, TRACK * NK).rearrange("p (t n) -> p t n", n=NK)
        second_hot = region(sc_at + 1792, TRACK * NK).rearrange("p (t n) -> p t n", n=NK)
        staged = region(sc_at + 2816, 512).rearrange("p (a k) -> p a k", a=2)
        late_acts = region(sc_at + 4608, RING * MAKE_G * T).rearrange("p (j t) -> p j t", t=T)
        gelu_u = region(sc_at, 1024).rearrange("p (a k) -> p a k", a=2)
        G = region(0, HALF * T).rearrange("p (g j t) -> p g j t", g=T // 4, t=4)

        ssq, msq, rt, rstd = st[:, 0:2], st[:, 2:4], st[:, 4:6], st[:, 6:8]
        gates = st[:, 8:104].rearrange("p (b c) -> p b c", b=TB)
        mx = st[:, 104:112].rearrange("p (a c) -> p a c", a=2)
        ngm = st[:, 112:120].rearrange("p (a c) -> p a c", a=2)
        sums = st[:, 120:128].rearrange("p (a c) -> p a c", a=2)
        rz = st[:, 128:136].rearrange("p (a c) -> p a c", a=2)
        gz = st[:, 136:144].rearrange("p (a c) -> p a c", a=2)
        mst = st[:, 144:160].rearrange("p (a c) -> p a c", a=2)
        hss = st[:, 160:184].rearrange("p (b c) -> p b c", b=TB)
        hrt = st[:, 184:208].rearrange("p (b c) -> p b c", b=TB)
        zs = st[:, 208:224].rearrange("p (b h) -> p b h", b=TB)
        rowst = st[0:8, 224:232]

        slot_full = [sem(f"slot_full{s}") for s in range(2)]
        raw_free = [sem(f"raw_free{s}") for s in range(2)]
        hi_ready = [sem(f"hi_ready{s}") for s in range(2)]
        slot_used = [sem(f"slot_used{s}") for s in range(2)]
        hTh_part, hTl_part = sem("hTh_part"), sem("hTl_part")
        mixw_loaded, gates_in, v_read = sem("mixw_loaded"), sem("gates_in"), sem("v_read")
        staged_out = [sem("staged_out0"), sem("staged_out1")]
        bank_free = [sem(f"bank_free{b}") for b in range(4)]
        x_in, params_in, stage1_in, fnw_in, out_done = (sem(n) for n in (
            "x_in", "params_in", "stage1_in", "fnw_in", "out_done"))
        sq_done, ms_ready, rt_done, xn_ready, turned, hT_part = (sem(n) for n in (
            "sq_done", "ms_ready", "rt_done", "xn_ready", "turned", "hT_part"))
        (gbr_ready, gbr_copied, gbr_turned, gates_ready, pooled, z_ready, y_pool, silu_done, swapped, roped, kb_ready, hid_ready,
         hid_silu, kc_ready, kc_copied, kc_roped, vc_ready, vc_copied) = (sem(n) for n in (
             "gbr_ready", "gbr_copied", "gbr_turned", "gates_ready", "pooled", "z_ready", "y_pool", "silu_done", "swapped", "roped",
             "kb_ready", "hid_ready", "hid_silu", "kc_ready", "kc_copied", "kc_roped", "vc_ready", "vc_copied"))
        (scores_ready, scores_read, max_ready, exp_done, probs_ready, probsT_ready, probsT_copied, o_done,
         o_read) = (sem(n) for n in (
             "scores_ready", "scores_read", "max_ready", "exp_done", "probs_ready", "probsT_ready",
             "probsT_copied", "o_done", "o_read"))
        merged_ready, x1_ready, x1_normed, x2_ready, fnw1_in = (sem(n) for n in (
            "merged_ready", "x1_ready", "x1_normed", "x2_ready", "fnw1_in"))
        branch_high, branch_split = sem("branch_high"), sem("branch_split")
        (rowsT_ready, row_e, row_l, row_y, rows_ready, nat_ready, nat_copied, a_ready,
         conv_done, conv_silu, q_ready, knat_ready, knat_copied, av_ready, C_ready, C_copied) = (sem(n) for n in (
             "rowsT_ready", "row_e", "row_l", "row_y", "rows_ready", "nat_ready",
             "nat_copied", "a_ready", "conv_done", "conv_silu", "q_ready", "knat_ready", "knat_copied",
             "av_ready", "C_ready", "C_copied"))
        (f_scores, f_read, f_max, f_exp, f_T, f_copied, f_o, f_oread) = (sem(n) for n in (
            "f_scores", "f_read", "f_max", "f_exp", "f_T", "f_copied", "f_o", "f_oread"))
        (m_scores, m_max, m_exp, m_sm, m_T, m_copied, m_num, m_read) = (sem(n) for n in (
            "m_scores", "m_max", "m_exp", "m_sm", "m_T", "m_copied", "m_num", "m_read"))
        mo_sig, cells, head_sq, head_ms, head_rt = (sem(n) for n in (
            "mo_sig", "cells", "head_sq", "head_ms", "head_rt"))
        (qs_ready, qs_copied, gate_arg, gate_exp, chosen_ready, chosenT, chosenT_copied) = (
            sem(n) for n in ("qs_ready", "qs_copied", "gate_arg", "gate_exp", "chosen_ready",
                             "chosenT", "chosenT_copied"))
        hot_ready, hot_used = sem("hot_ready"), sem("hot_used")
        g_kept, g_weighted = sem("g_kept"), sem("g_weighted")
        gated = [sem("gated0"), sem("gated1")]
        x3_ready, result = sem("x3_ready"), sem("result")
        dve_step, act_step, pool_step = sem("dve_step"), sem("act_step"), sem("pool_step")

        def stepper(eng, s):
            n = [0]

            def step(ins):
                n[0] += 1
                ins.then_inc(s, 1)
                eng.wait_ge(s, n[0])
            return step

        def loaded(name, i, s):
            return i * 32 + 16 * (G0[name][0] + s // 2 + 1)

        def consumed(name, i, s):
            return i * 2 + (G0[name][0] + s // 2 + 1)

        def rounded(name, i, s):
            return i * 2 + (S0[name] + s // 2 + 1)

        def multiplied(name, i, s):
            return i * 2 + (S0[name] + s // 2 + 2)

        def gate_block(j, n):
            return G[:, :, bass.ds(j, n), :]

        def bc(ap, shape):
            return ap.to_broadcast(shape)

        block = ctx.enter_context(nc.Block())

        @block.sync
        def _(sp):
            sp.dma_start(xres[:], x.rearrange("o (b p) d -> p (o b) d", p=P)).then_inc(x_in, 16)
            sp.dma_start(par[:], params).then_inc(params_in, 16)
            for s in range(2):
                sp.dma_start(raw[s][:], stream[s]).then_inc(slot_full[s], 16)
            sp.dma_start(region(stage1_at, n_stage1), stage1).then_inc(stage1_in, 16)
            with sp.Fori(1, PAIRS) as g:
                for s in range(2):
                    sp.wait_ge(raw_free[s], g)
                    sp.dma_start(raw[s][:], stream[g * 2 + s]).then_inc(slot_full[s], 16)
            sp.wait_ge(raw_free[0], PAIRS)
            sp.dma_start(raw[0][:], fnw.partition_broadcast(P)).then_inc(fnw_in, 16)
            sp.wait_ge(result, TB)
            sp.dma_start(out.rearrange("o (b p) d -> p (o b) d", p=P),
                         R[:, 0:TB * D].rearrange("p (b d) -> p b d", b=TB)).then_inc(out_done, 16)
            sp.wait_ge(out_done, 16)

        @block.tensor
        def _(pe):
            mm = nc.tensor.matmul

            def turn_norm(n):
                for b in range(TB):
                    pe.wait_ge(xn_ready, TB * n + b + 1)
                    for j in range(4):
                        if b > 0:
                            pe.wait_ge(hT_part, 8 * n + 4 * (b - 1) + j + 1)
                        for c in range(4):
                            last = nc.tensor.transpose(bank[4 + j][:, c * P:(c + 1) * P],
                                                       scr_of[n][:, b * D + (4 * j + c) * P:b * D + (4 * j + c + 1) * P], ident)
                        last.then_inc(turned, 1)

            def t_slot(name, i, s, between=None):
                b, t = s // 2, s % 2
                if t == 0:
                    pe.wait_ge(bank_free[b], i + B0[name][b])
                pe.wait_ge(raw_free[t], consumed(name, i, s))
                for k in range(KC):
                    ks = slice(k * P, (k + 1) * P)
                    for n, (w, x_) in enumerate(((whi, hTh), (whi, hTl), (wlo, hTh))):
                        last = mm(bank[b][:, t * T:(t + 1) * T], w[t][:, ks], x_[:, k, :],
                                  start=(k == 0 and n == 0), stop=(k == KC - 1 and n == 2))
                    if k == KC - 1:
                        last.then_inc(slot_used[t], 1)
                    if between is not None:
                        between(k)

            def phase_t(name, lo=0, hi=None, between=None):
                with pe.Fori(0, (G0[name][1] if hi is None else hi) - lo) as i:
                    for s in range(RING):
                        t_slot(name, i + lo, s, None if between is None else lambda k: between(i, s, k))

            def phase_n(name):
                with pe.Fori(0, G0[name][1] // 2) as i:
                    for h in range(2):
                        for b in range(TB):
                            pe.wait_ge(bank_free[2 * h + b], i + B0[name][2 * h + b])
                        for s in range(RING):
                            t = s % 2
                            pe.wait_ge(raw_free[t], i * 4 + consumed(name, h, s))
                            for kk in range(4):
                                k = 4 * s + kk
                                for b in range(TB):
                                    ts_ = slice(b * P, (b + 1) * P)
                                    for n, (x_, w) in enumerate(((hTh, whi), (hTh, wlo), (hTl, whi))):
                                        last = mm(bank[2 * h + b][:], x_[:, k, ts_], w[t][:, kk * 512:(kk + 1) * 512],
                                                  start=(k == 0 and n == 0), stop=(k == KC - 1 and n == 2))
                            last.then_inc(slot_used[t], 1)

            def narrow(name, dst, n, ready):
                pe.wait_ge(raw_free[0], consumed(name, 0, 0))
                for k in range(KC):
                    for m, (w, x_) in enumerate(((whi, hTh), (whi, hTl), (wlo, hTh))):
                        last = mm(dst, w[0][:, k * P:k * P + n], x_[:, k, :],
                                  start=(k == 0 and m == 0), stop=(k == KC - 1 and m == 2))
                last.then_inc(slot_used[0], 1)
                pe.wait_ge(raw_free[1], consumed(name, 0, 1))
                pe.sem_inc(slot_used[1], 1)
                pe.wait_ge(slot_used[0], multiplied(name, 0, 0))
                pe.sem_inc(ready, 1)

            for s_ in (*bank_free, *gated, *slot_used):
                pe.sem_inc(s_, 1)
            pe.wait_ge(params_in, 16)
            turn_norm(0)
            pe.wait_ge(hTl_part, 8)
            phase_t("in_t")
            phase_n("in_n")
            narrow("narrow1", bank[6][0:48, 0:T], 48, gbr_ready)
            pe.wait_ge(gbr_copied, 1)
            pe.wait_ge(stage1_in, 16)
            for b in range(TB):
                last = nc.tensor.transpose(bank[4 + b][:, 0:48], gbr_rows[:, b * P:(b + 1) * P], ident[0:48, 0:48])
            last.then_inc(gbr_turned, 1)
            for v in range(2):
                pe.wait_ge(kb_ready, v + 1)
                if v == 0:
                    pe.wait_ge(gates_ready, 1)
                for s in range(RING):
                    pe.wait_ge(slot_full[s % 2], loaded("cmp", v, s))
                    for ll in range(8):
                        l = 8 * s + ll
                        for f in range(2):
                            last = mm(bank[4 + 2 * v + f][:, 0:NC4], raw[s % 2][:, ll * CH + f * P:ll * CH + (f + 1) * P],
                                      kb[v][:, l, :], start=(l == 0), stop=(l == CB - 1))
                    last.then_inc(raw_free[s % 2], 1)
            pe.wait_ge(hid_silu, 1)
            w2k = s1("w2k").rearrange("p (f e) -> p f e", f=2)
            w2v = s1("w2v").rearrange("p (f e) -> p f e", f=2)
            for f in range(2):
                last = mm(bank[4][:, 0:NC4], w2k[:, f, :], hdn[:, 0, f, :], start=(f == 0), stop=(f == 1))
            last.then_inc(kc_ready, 1)
            pe.wait_ge(hid_silu, 2)
            for h in range(HKV):
                for f in range(2):
                    last = mm(bank[5][0:NCMP, h * DH:(h + 1) * DH], hdn[:, 1, f, h * NCMP:(h + 1) * NCMP],
                              w2v[:, f, :], start=(f == 0), stop=(f == 1))
            last.then_inc(vc_ready, 1)

            def nsa_scores(u):
                h, qb = divmod(u, TB)
                a, kv, nk = u % 2, h // GQ, (qb + 1) * P
                if u >= 2:
                    pe.wait_ge(scores_read, u - 1)
                    pe.wait_ge(probsT_copied, u - 1)
                q = pT[:, Q0 + h, qb * P:(qb + 1) * P]
                mm(bank[4 + a][:, 0:nk], q, pT[:, KS0 + kv, 0:nk], start=True, stop=True)
                mm(bank[4 + a][:, T:T + nk], q, pT[:, KW0 + kv, 0:nk], start=True, stop=True)
                mm(bank[6 + a][:, 0:NCMP], q, kcT[:, kv * NCMP:(kv + 1) * NCMP], start=True,
                   stop=True).then_inc(scores_ready, 1)

            def nsa_turn(u):
                qb, a = u % TB, u % 2
                nb = qb + 1
                pe.wait_ge(probs_ready, u + 1)
                if u >= 2:
                    pe.wait_ge(probsT_copied, u - 1)
                for br in range(2):
                    for k in range(nb):
                        j = br * nb + k
                        nc.tensor.transpose(bank[6 + a][:, j * P:(j + 1) * P],
                                            SP[:, a, br * T + k * P:br * T + (k + 1) * P], ident)
                nc.tensor.transpose(bank[4 + a][0:NCMP, 0:P], Pc[:, a, 0:NCMP], ident).then_inc(probsT_ready, 1)

            def nsa_values(u):
                h, qb = divmod(u, TB)
                a, kv, nb = u % 2, h // GQ, qb + 1
                pe.wait_ge(probsT_copied, u + 1)
                if qb == 0 and h >= 2:
                    pe.wait_ge(o_read, h - 1)
                o = bank[2 + h % 2][:, qb * P:(qb + 1) * P]
                mm(o, vcs[:, kv * DH:(kv + 1) * DH], PcT[:, a, :], start=True, stop=False)
                for br in range(2):
                    for k in range(nb):
                        j = br * nb + k
                        last = mm(o, vN1[:, br, k, kv * DH:(kv + 1) * DH], PT[:, a, j * P:(j + 1) * P],
                                  start=False, stop=(j == 2 * nb - 1))
                last.then_inc(o_done, 1)

            units = HQ * TB
            pe.wait_ge(roped, 12)
            pe.wait_ge(kc_roped, 1)
            pe.wait_ge(vc_copied, 1)
            for b in range(4):
                pe.wait_ge(bank_free[b], B0["merge"][b])
            nsa_scores(0)
            nsa_scores(1)
            for u in range(units):
                nsa_turn(u)
                if u + 2 < units:
                    nsa_scores(u + 2)
                if u in MERGE_AT:
                    t_slot("merge", *divmod(MERGE_AT.index(u), RING))
                nsa_values(u)
            pe.wait_ge(pooled, NG)
            pe.wait_ge(probsT_copied, units)
            pe.wait_ge(mixw_loaded, 16)
            mixw = mixw_sb.rearrange("p (g c e) -> p g c e", g=NG, c=2)
            for g in range(NG):
                for e in range(2):
                    for c in range(2):
                        last = mm(bank[4 + g][:, e * T:(e + 1) * T], mixw[:, g, c, e * P:(e + 1) * P],
                                  pT[:, U0 + 2 * g + c, :], start=(c == 0), stop=(c == 1))
                last.then_inc(z_ready, 1)
            pe.wait_ge(o_read, HQ)
            phase_t("merge", MERGE_EARLY)
            pe.wait_ge(y_pool, NG)
            with pe.Fori(0, G0["pool_out"][1]) as i:
                for s in range(RING):
                    t = s % 2
                    pe.wait_ge(bank_free[s], i + B0["pool_out"][s])
                    pe.wait_ge(slot_full[t], loaded("pool_out", i, s))
                    for e in range(2):
                        for k in range(8):
                            last = mm(bank[s][:, e * T:(e + 1) * T], raw[t][:, (e * 8 + k) * P:(e * 8 + k + 1) * P],
                                      pT[:, U0 + k, :], start=(k == 0), stop=(k == 7))
                    last.then_inc(raw_free[t], 1)
            pe.wait_ge(branch_split, 8)
            phase_t("nsa_out")
            pe.wait_ge(branch_split, 16)
            phase_n("out1")

            turn_norm(1)
            pe.wait_ge(hTl_part, 16)
            phase_t("in2_t")
            narrow("narrow2", bank[5][0:ROW_AT[2] + MH, 0:T], ROW_AT[2] + MH, rowsT_ready)
            phase_n("in2_n")
            pe.wait_ge(rows_ready, 1)
            for c in range(TB):
                nc.tensor.transpose(bank[4][:, 8 * c:8 * c + 8], rows[0:8, 6, c * P:(c + 1) * P], ident[0:8, 0:8])
                nc.tensor.transpose(bank[4][:, 16 + 4 * c:20 + 4 * c], rows[0:4, 8, c * P:(c + 1) * P],
                                    ident[0:4, 0:4])
                nc.tensor.transpose(bank[4][:, 24 + 4 * c:28 + 4 * c], rows[0:4, 10, c * P:(c + 1) * P],
                                    ident[0:4, 0:4])
            nc.tensor.transpose(bank[4][:, 32:36], rows[0:4, 11, 0:P], ident[0:4, 0:4]).then_inc(nat_ready, 1)
            pe.wait_ge(q_ready, 2)
            for h in range(MH):
                last = nc.tensor.transpose(bank[5][:, h * P:(h + 1) * P], conv[:, 4 + h, 0:P], ident)
            last.then_inc(knat_ready, 1)
            pe.wait_ge(knat_copied, 1)
            for h in range(MH):
                pe.wait_ge(av_ready, h + 1)
                mm(bank[6][:, 0:MV + 1], knat[:, h, :], av[:, 0:MV + 1], start=True, stop=True).then_inc(C_ready, 1)

            def fox_scores(u):
                h, qb = divmod(u, TB)
                a, nk = u % 2, (qb + 1) * P
                if u >= 2:
                    pe.wait_ge(f_read, u - 1)
                mm(bank[4 + a][:, 0:nk], pT[:, FQ0 + h, qb * P:(qb + 1) * P], pT[:, FK0 + h, 0:nk],
                   start=True, stop=False)
                mm(bank[4 + a][:, 0:nk], bc(ident[0:8, h:h + 1], [8, P]), rows[0:8, 7, 0:nk],
                   start=False, stop=True).then_inc(f_scores, 1)

            def fox_turn(u):
                qb, a = u % TB, u % 2
                pe.wait_ge(f_exp, u + 1)
                if u >= 2:
                    pe.wait_ge(f_copied, u - 1)
                for k in range(qb + 1):
                    last = nc.tensor.transpose(bank[6 + a][:, k * P:(k + 1) * P], SP2[:, a, k * P:(k + 1) * P], ident)
                last.then_inc(f_T, 1)

            def fox_values(u):
                h, qb = divmod(u, TB)
                a = u % 2
                pe.wait_ge(f_copied, u + 1)
                if u >= 2:
                    pe.wait_ge(f_oread, u - 1)
                for k in range(qb + 1):
                    last = mm(bank[2 + a][:, 0:DH], PT2[:, a, k * P:(k + 1) * P],
                              vN2[:, h // 4, k, (h % 4) * DH:(h % 4 + 1) * DH], start=(k == 0), stop=(k == qb))
                last.then_inc(f_o, 1)

            units = FH * TB
            pe.wait_ge(nat_copied, 1)
            pe.wait_ge(C_copied, MH)
            for b in range(4):
                pe.wait_ge(bank_free[b], B0["out2"][b])
            fox_scores(0)
            fox_scores(1)
            for u in range(units):
                fox_turn(u)
                if u + 2 < units:
                    fox_scores(u + 2)
                fox_values(u)
            pe.wait_ge(f_copied, units)
            pe.wait_ge(f_oread, units)

            def m_sc(u):
                c, h = divmod(u, MH)
                a = u % 2
                if u >= 2:
                    pe.wait_ge(m_sm, u - 1)
                cs = slice(c * P, (c + 1) * P)
                mm(bank[4 + a][:, 0:P], conv[:, h, cs], conv[:, 4 + h, cs], start=True, stop=True)
                mm(bank[4 + a][:, P:2 * P], bc(ident[0:4, h:h + 1], [4, P]), rows[0:4, 9, cs],
                   start=True, stop=True).then_inc(m_scores, 1)

            def m_turn(u):
                a = u % 2
                pe.wait_ge(m_sm, u + 1)
                if u >= 2:
                    pe.wait_ge(m_copied, u - 1)
                nc.tensor.transpose(bank[6 + a][:, 0:P], Sm[:, a, :], ident).then_inc(m_T, 1)

            def m_values(u):
                c, h = divmod(u, MH)
                a = u % 2
                pe.wait_ge(m_copied, u + 1)
                if u >= 2:
                    pe.wait_ge(m_read, u - 1)
                if c == 1:
                    mm(bank[a][:, 0:MV + 1], conv[:, h, P:2 * P], CN[:, h, 0:MV + 1], start=True, stop=True)
                mm(bank[2 + a][:, 0:MV], SmT[:, a, :], vN2[:, 2 + h // 2, c, (h % 2) * MV:(h % 2 + 1) * MV],
                   start=True, stop=True).then_inc(m_num, 1)

            units = MH * TB
            m_sc(0)
            m_sc(1)
            for u in range(units):
                m_turn(u)
                if u + 2 < units:
                    m_sc(u + 2)
                m_values(u)
            turn_norm(2)
            pe.wait_ge(hTl_part, 24)
            phase_n("out2")
            turn_norm(3)
            pe.wait_ge(hTl_part, 32)
            phase_t("wq")
            for b in range(2):
                pe.wait_ge(bank_free[b], B0["peer_u0"][b])
            keysT = prm("keysT").rearrange("p (s n) -> p s n", s=2)
            for f in range(TB * 4):
                b, j = divmod(f, 4)
                if f >= 4:
                    pe.wait_ge(qs_copied, f - 3)
                for c in range(4):
                    hp = 4 * j + c
                    last = mm(bank[4 + j][:, c * NK:(c + 1) * NK], qT3[:, hp, b * P:(b + 1) * P],
                              keysT[:, hp % 2, :], start=True, stop=True)
                last.then_inc(qs_ready, 1)
            phase_t("peer_u0", 0, CHOOSE_G)
            for b in range(TB):
                pe.wait_ge(chosen_ready, b + 1)
                for s in range(3):
                    last = nc.tensor.transpose(bank[4 + b][:, s * P:(s + 1) * P], chosen[:, b, s, :], ident)
                last.then_inc(chosenT, 1)
            pe.wait_ge(chosenT_copied, 1)
            pe.sem_inc(hot_used, TRACK // 2)

            def token_gates(i, s, k):
                if k % 4 == 0:
                    m = i * 16 + 4 * s + k // 4
                    pe.wait_ge(g_kept, m + 1)
                    pe.wait_ge(g_weighted, m + 1)
                if k % 2 == 0:
                    n = i * 32 + 8 * s + k // 2
                    pe.wait_ge(hot_ready, n + 1)
                c = k % 4
                last = mm(bank[4 + k // 4][:, c * P:(c + 1) * P], second_hot[:, k % TRACK, :],
                          first_hot[:, k % TRACK, :], start=True, stop=True)
                if k % 2 == 1:
                    last.then_inc(hot_used, 1)
            phase_t("peer_u0", CHOOSE_G, CHOOSE_G + MAKE_G, token_gates)
            phase_t("peer_u0", CHOOSE_G + MAKE_G)
            def expert_values(name, i, first, last_group):
                for s in range(RING):
                    t = s % 2
                    pe.wait_ge(raw_free[t], consumed(name, i, s))
                    for b in range(TB):
                        ts_ = slice(b * P, (b + 1) * P)
                        for n, (x_, w) in enumerate(((ghi, whi), (ghi, wlo), (glo, whi))):
                            for c in range(4):
                                last = mm(bank[4 * b + c][:], x_[:, t, ts_], w[t][:, c * 512:(c + 1) * 512],
                                          start=(first and s == 0 and n == 0),
                                          stop=(last_group and s == RING - 1 and n == 2))
                    last.then_inc(slot_used[t], 1)

            for half in range(2):
                if half:
                    pe.wait_ge(v_read, 2)
                    phase_t("peer_u1")
                    pe.wait_ge(v_read, 8)
                else:
                    pe.wait_ge(g_kept, 4 + T // 4)
                    pe.wait_ge(g_weighted, 4 + T // 4)
                for b in range(2):
                    pe.wait_ge(bank_free[b], B0[f"peer_v{half}"][b])
                name = f"peer_v{half}"
                n = G0[name][1]
                expert_values(name, 0, True, False)
                with pe.Fori(1, n - 1) as i:
                    expert_values(name, i, False, False)
                expert_values(name, n - 1, False, True)

        @block.scalar
        def _(act):
            step = stepper(act, act_step)
            A = nc.scalar.activation

            def split(name, i, s):
                t = s % 2
                act.wait_ge(slot_full[t], loaded(name, i, s))
                act.wait_ge(slot_used[t], rounded(name, i, s))
                if name.startswith("peer_v"):
                    A(ghi[:, t, :].rearrange("p (g o t) -> p g o t", o=1, t=4), gate_block(i * 4 + s, 1), ACT.Copy)
                A(whi[t][:], raw[t][:], ACT.Copy).then_inc(hi_ready[t], 1)

            def phase(name, after, lo=0, hi=None, started=False, ahead=False):
                n = (G0[name][1] if hi is None else hi) - lo
                if not started:
                    split(name, lo, 0)
                if n > 1:
                    with act.Fori(0, n - 1) as i:
                        for s in range(RING):
                            split(name, i + (lo + (s + 1) // RING), (s + 1) % RING)
                            after(i, s)
                for s in range(RING):
                    if s + 1 < RING:
                        split(name, lo + n - 1, s + 1)
                    elif ahead:
                        split(name, lo + n, 0)
                    after(n - 1, s)

            def high_parts(n):
                for b in range(TB):
                    for j in range(4):
                        f = 4 * b + j
                        act.wait_ge(hT_part, 8 * n + f + 1)
                        A(hTh[:, 4 * j:4 * j + 4, b * P:(b + 1) * P],
                          turned_tmp[:, f % 2, :].rearrange("p (c t) -> p c t", c=4), ACT.Copy).then_inc(hTh_part, 1)

            def squares(n):
                unused = scr_of[(0, 0, 1, 3)[n]]
                for b in range(TB):
                    A(unused[:, b * D:(b + 1) * D], xres[:, b, :], ACT.Square,
                      accum_out=ssq[:, b:b + 1]).then_inc(sq_done, 1)
                act.wait_ge(ms_ready, n + 1)
                A(rt, msq, ACT.Sqrt).then_inc(rt_done, 1)

            def keep(i, s):
                pass

            def evac_t(name):
                def evac(i, s):
                    if s == 3:
                        act.wait_ge(slot_used[1], multiplied(name, i, 3))
                        A(R[:, bass.ds(i * (4 * T) + 2 * T, 2 * T)], bank[1][:], ACT.Copy).then_inc(bank_free[1], 1)
                phase(name, evac)

            def phase_n(name, dst, between=None):
                def evac(g):
                    act.wait_ge(slot_used[1], multiplied(name, g, 3))
                    A(dst[:, g, 0, :], bank[2 * (g % 2)][:], ACT.Copy).then_inc(bank_free[2 * (g % 2)], 1)
                n = G0[name][1]
                for g in range(n):
                    split(name, g, 0)
                    if g and dst is not None:
                        evac(g - 1)
                    for s in range(1, RING):
                        split(name, g, s)
                        if s == 1 and between is not None:
                            between(g)
                if dst is not None:
                    evac(n - 1)

            act.wait_ge(x_in, 16)
            squares(0)
            high_parts(0)
            evac_t("in_t")
            phase_n("in_n", vN1)
            split("narrow1", 0, 0)
            split("narrow1", 0, 1)
            act.wait_ge(gbr_ready, 1)
            A(gbr_rows, bank[6][0:48, 0:T], ACT.Copy).then_inc(gbr_copied, 1)
            act.wait_ge(gbr_turned, 1)
            for b in range(TB):
                last = A(gates[:, b, :], bank[4 + b][:, 0:48], ACT.Sigmoid)
            last.then_inc(gates_ready, 1)
            act.wait_ge(bank_free[0], B0["in_n"][0])
            A(pT[:, GP0:GP0 + 8, :], pT[:, GP0:GP0 + 8, :], ACT.Silu).then_inc(silu_done, 1)
            A(pT[:, GN0:GN0 + 16, :], pT[:, GN0:GN0 + 16, :], ACT.Silu).then_inc(silu_done, 1)
            for j in range(12):
                if j >= 2:
                    act.wait_ge(roped, j - 1)
                buf = rot_buf[:, (j % 2) * 512:(j % 2 + 1) * 512].rearrange("p (j t) -> p j t", t=T)
                src = pT[:, KS0 + 2 * j:KS0 + 2 * j + 2, :]
                A(buf[0:64], src[64:128], ACT.Copy)
                A(buf[64:128], src[0:64], ACT.Copy).then_inc(swapped, 1)
            for v in range(2):
                act.wait_ge(raw_free[1], consumed("cmp", v, 3))
                for f in range(2):
                    last = A(hdn[:, v, f, :], bank[4 + 2 * v + f][:, 0:NC4], ACT.Silu)
                last.then_inc(hid_silu, 1)
            act.wait_ge(kc_ready, 1)
            A(kcT, bank[4][:, 0:NC4], ACT.Copy)
            A(kcS[0:64], bank[4][64:128, 0:NC4], ACT.Copy)
            A(kcS[64:128], bank[4][0:64, 0:NC4], ACT.Copy).then_inc(kc_copied, 1)
            act.wait_ge(vc_ready, 1)
            A(vcs, bank[5][0:NCMP, :], ACT.Copy).then_inc(vc_copied, 1)

            def nsa_exp(u):
                a, nk = u % 2, (u % TB + 1) * P
                act.wait_ge(max_ready, u + 1)
                for br in range(2):
                    sl = SP[:, a, br * T:br * T + nk]
                    A(sl, sl, ACT.Exp, bias=ngm[:, a, br:br + 1], scale=SCALE, accum_out=sums[:, a, br:br + 1])
                A(Pc[:, a, 0:NCMP], Pc[:, a, 0:NCMP], ACT.Exp, bias=ngm[:, a, 2:3], scale=SCALE,
                  accum_out=sums[:, a, 2:3]).then_inc(exp_done, 1)

            def nsa_copy(u):
                a, n = u % 2, 2 * (u % TB + 1) * P
                act.wait_ge(probsT_ready, u + 1)
                if u >= 2:
                    act.wait_ge(o_done, u - 1)
                A(PT[:, a, 0:n], bank[6 + a][:, 0:n], ACT.Copy)
                A(PcT[:, a, :], bank[4 + a][0:NCMP, 0:P], ACT.Copy).then_inc(probsT_copied, 1)

            bm = PO["bmerge"][0]

            def merge_gate(b, i, place):
                act.wait_ge(slot_used[1], multiplied("merge", i, 2 * b + 1))
                for e in range(2):
                    at = place * 4 + (2 * b + e)
                    last = A(R[:, bass.ds(at * T + 16 * T, T)], bank[b][:, e * T:(e + 1) * T], ACT.Sigmoid,
                             bias=par[:, bass.ds(at + bm, 1)])
                last.then_inc(bank_free[b], 1)

            act.wait_ge(roped, 12)
            act.dma_start(mixw_sb, mixw_in).then_inc(mixw_loaded, 16)
            units = HQ * TB
            split("merge", 0, 0)
            nsa_exp(0)
            for u in range(units):
                if u + 1 < units:
                    nsa_exp(u + 1)
                nsa_copy(u)
                if u in MERGE_AT:
                    split("merge", *divmod(MERGE_AT.index(u) + 1, RING))
                if u - 1 in MERGE_AT and MERGE_AT.index(u - 1) % 2 == 1:
                    i, s = divmod(MERGE_AT.index(u - 1), RING)
                    merge_gate(s // 2, i, MERGE_ORDER[i])
            if MERGE_AT[-1] == units - 1:
                merge_gate(1, MERGE_EARLY - 1, MERGE_ORDER[MERGE_EARLY - 1])
            act.wait_ge(o_done, units)
            act.dma_start(fnw1_sb, fnw1.partition_broadcast(P)).then_inc(fnw1_in, 16)

            def merge_gates(lo):
                def after(i, s):
                    if s >= 2:
                        merge_gate(s - 2, i + lo, i + MERGE_ORDER[lo])
                return after
            phase("merge", merge_gates(MERGE_EARLY), MERGE_EARLY, 6, started=True, ahead=True)
            phase("merge", merge_gates(6), 6, started=True)

            def branch_high_parts(src):
                for j in range(8):
                    A(hTh[:, 2 * j:2 * j + 2, :], src[:, 2 * j:2 * j + 2, :], ACT.Copy).then_inc(branch_high, 1)
            branch_high_parts(pT[:, GN0:GN0 + 16, :])
            phase("nsa_out", keep)
            act.wait_ge(slot_used[1], multiplied("nsa_out", G0["nsa_out"][1] - 1, 3))
            for j in range(4):
                act.wait_ge(merged_ready, 2 * (j + 1))
                for e in range(2):
                    jj = 2 * j + e
                    A(hTh[:, 2 * jj:2 * jj + 2, :], gate0[:, 2 * jj:2 * jj + 2, :], ACT.Copy).then_inc(branch_high, 1)
            phase_n("out1", None)

            act.wait_ge(x1_ready, 8)
            squares(1)
            act.wait_ge(x1_normed, TB)
            squares(2)
            high_parts(1)
            evac_t("in2_t")
            split("narrow2", 0, 0)
            split("narrow2", 0, 1)

            def gate_rows(g):
                if g == 1:
                    act.wait_ge(row_y, 1)
                    A(rows[0:8, 4, :], rows[0:8, 4, :], ACT.Exp).then_inc(act_step, 1)
                    A(rows[0:4, 5, :], rows[0:4, 5, :], ACT.Exp).then_inc(act_step, 1)
                    act.wait_ge(act_step, 2)
                    A(rows[0:8, 4, :], rows[0:8, 4, :], ACT.Ln, bias=1.0)
                    A(rows[0:4, 5, :], rows[0:4, 5, :], ACT.Ln, bias=1.0).then_inc(row_l, 1)
                elif g == 5:
                    act.wait_ge(a_ready, 1)
                    A(rows[0:4, 11, 0:P], rows[0:4, 9, 0:P], ACT.Exp, bias=rowst[0:4, 1:2]).then_inc(rows_ready, 1)
            phase_n("in2_n", vN2, gate_rows)
            act.wait_ge(conv_done, 8)
            A(conv, conv, ACT.Silu).then_inc(conv_silu, 1)
            act.wait_ge(nat_ready, 1)
            A(natc[:, 0:36], bank[4][:, 0:36], ACT.Copy).then_inc(nat_copied, 1)
            act.wait_ge(knat_ready, 1)
            A(knat, bank[5][:].rearrange("p (h d) -> p h d", h=MH), ACT.Copy).then_inc(knat_copied, 1)
            for b in range(4):
                act.wait_ge(bank_free[b], B0["out2"][b])
            A(vN2[:, 4:6], vN2[:, 4:6], ACT.Sigmoid).then_inc(mo_sig, 1)

            def fox_exp(u):
                a, nk = u % 2, (u % TB + 1) * P
                act.wait_ge(f_max, u + 1)
                A(SP2[:, a, 0:nk], SP2[:, a, 0:nk], ACT.Exp, bias=ngm[:, a, 0:1],
                  accum_out=sums[:, a, 0:1]).then_inc(f_exp, 1)

            def fox_copy(u):
                a, n = u % 2, (u % TB + 1) * P
                act.wait_ge(f_T, u + 1)
                if u >= 2:
                    act.wait_ge(f_o, u - 1)
                A(PT2[:, a, 0:n], bank[6 + a][:, 0:n], ACT.Copy).then_inc(f_copied, 1)

            units = FH * TB
            fox_exp(0)
            for u in range(units):
                if u + 1 < units:
                    fox_exp(u + 1)
                fox_copy(u)

            def m_exps(u):
                a = u % 2
                act.wait_ge(m_max, u + 1)
                A(Dm[:, a, :], Dm[:, a, :], ACT.Exp, bias=mst[:, a, 1:2])
                A(mst[:, a, 3:5], mst[:, a, 1:3], ACT.Exp).then_inc(m_exp, 1)

            def m_copy(u):
                a = u % 2
                act.wait_ge(m_T, u + 1)
                if u >= 2:
                    act.wait_ge(m_num, u - 1)
                A(SmT[:, a, :], bank[6 + a][:, 0:P], ACT.Copy).then_inc(m_copied, 1)

            units = MH * TB
            m_exps(0)
            for u in range(units):
                if u + 1 < units:
                    m_exps(u + 1)
                m_copy(u)
            act.wait_ge(cells, 1)
            A(region(0, 4096), scr, ACT.Square).then_inc(head_sq, 1)
            act.wait_ge(head_ms, 1)
            A(hrt, hss, ACT.Sqrt).then_inc(head_rt, 1)
            high_parts(2)
            phase_n("out2", None)
            act.wait_ge(x2_ready, 8)
            squares(3)
            high_parts(3)
            evac_t("wq")
            split("peer_u0", 0, 0)
            for f in range(8):
                b, j = divmod(f, 4)
                act.wait_ge(qs_ready, f + 1)
                A(scores[:, 16 * b + 4 * j:16 * b + 4 * j + 4, :], bank[4 + j][:].rearrange("p (c n) -> p c n", c=4),
                  ACT.Copy).then_inc(qs_copied, 1)

            def gelu_to(dst, name, lo):
                def after(i, s):
                    if s >= 2:
                        b = s - 2
                        act.wait_ge(slot_used[1], multiplied(name, i + lo, 2 * b + 1))
                        to, view = dst(i, b)
                        A(to, bank[b][:].rearrange(view, j=2, t=4), ACT.Gelu).then_inc(bank_free[b], 1)
                return after

            def early(lo):
                return gelu_to(lambda i, b: (gate_block(i * 4 + (4 * lo + 2 * b), 2), "p (j g t) -> p g j t"),
                               "peer_u0", lo)

            steps = (0, CHOOSE_G - 4, CHOOSE_G - 1, CHOOSE_G)
            for n in range(3):
                phase("peer_u0", early(steps[n]), steps[n], steps[n + 1], started=True, ahead=True)
                if n < TB:
                    act.wait_ge(gate_arg, n + 1)
                    A(finv[:, n], finv[:, n], ACT.Exp).then_inc(gate_exp, 1)
            act.wait_ge(chosenT, TB)
            for b in range(TB):
                last = A(idxT[:, :, b * P:(b + 1) * P], bank[4 + b][:, 0:3 * P].rearrange("p (s t) -> p s t", s=3),
                         ACT.Copy)
            last.then_inc(chosenT_copied, 1)
            act.sem_inc(g_kept, 4)
            for q in range(2):
                act.sem_inc(staged_out[q], 16)
            late = gelu_to(lambda i, b: (late_acts[:, bass.ds(i * 4 + 2 * b, 2), :], "p (j g t) -> p j (g t)"),
                           "peer_u0", CHOOSE_G)

            def keep_gates(i, s):
                for q in range(4):
                    m = i * 16 + (4 * s + q)
                    src = bank[4 + q][:].rearrange("p (t n) -> p n t", t=4)
                    act.wait_ge(g_weighted, m + 5)
                    A(G[:, bass.ds(m, 1), EARLY:, :].rearrange("p g j t -> p (g j) t"), src[:, EARLY:HALF, :], ACT.Copy)
                    act.wait_ge(staged_out[q % 2], i * 128 + 16 * (2 * s + q // 2 + 1))
                    A(staged[:, q % 2, :].rearrange("p (j t) -> p j t", t=4), src[:, HALF:NK, :],
                      ACT.Copy).then_inc(g_kept, 1)
                    act.wait_ge(g_kept, m + 5)
                    act.dma_start(gates_dram[m], staged[:, q % 2, :]).then_inc(staged_out[q % 2], 16)
                late(i, s)
            phase("peer_u0", keep_gates, CHOOSE_G, CHOOSE_G + MAKE_G, started=True, ahead=True)

            def gelu(name, lo, base):
                def after(i, s):
                    if s >= 2:
                        b = s - 2
                        act.wait_ge(slot_used[1], multiplied(name, i + lo, 2 * b + 1))
                        act.wait_ge(gated[b], i + base)
                        A(gelu_u[:, b, :], bank[b][:], ACT.Gelu).then_inc(bank_free[b], 1)
                return after

            REST = G0["peer_u0"][1] - CHOOSE_G - MAKE_G
            act.wait_ge(hot_used, T // 2 + TRACK // 2)
            to_late = gelu_to(lambda i, b: (late_acts[:, bass.ds(i * 4 + 2 * b, 2), :], "p (j g t) -> p j (g t)"),
                              "peer_u1", 0)

            def load_gates(i, s):
                n = T // 4 // (RING * MAKE_G)
                act.dma_start(G[:, bass.ds(i * (RING * n) + s * n, n), :, :].rearrange("p g j t -> p g (j t)"),
                              gates_dram[bass.ds(i * (RING * n) + s * n, n)].rearrange("g p c -> p g c")
                              ).then_inc(gates_in, 16)
                to_late(i, s)
            for half in range(2):
                if half == 0:
                    phase("peer_u0", gelu("peer_u0", CHOOSE_G + MAKE_G, 1), CHOOSE_G + MAKE_G, started=True)
                else:
                    phase("peer_u1", load_gates, 0, MAKE_G, ahead=True)
                    phase("peer_u1", gelu("peer_u1", MAKE_G, 1 + REST), MAKE_G, started=True)
                name = f"peer_v{half}"
                for b in range(2):
                    act.wait_ge(gated[b], 1 + REST + half * (G0["peer_u1"][1] - MAKE_G))
                act.wait_ge(g_weighted, 4 + T // 4)
                with act.Fori(0, G0[name][1]) as i:
                    for s in range(RING):
                        split(name, i, s)
                if half == 0:
                    act.wait_ge(raw_free[1], consumed(name, G0[name][1] - 1, 3))
                    for q in range(2):
                        act.wait_ge(staged_out[q], 16 + 16 * (T // 8))
            act.wait_ge(x3_ready, 8)
            for b in range(TB):
                A(R[:, b * D:(b + 1) * D], xres[:, b, :], ACT.Square, accum_out=ssq[:, b:b + 1]).then_inc(sq_done, 1)
            act.wait_ge(ms_ready, 5)
            A(rt, msq, ACT.Sqrt).then_inc(rt_done, 1)

        @block.gpsimd
        def _(pool):
            step = stepper(pool, pool_step)
            bufs = pool_buf
            inv = s1("invcnt").rearrange("p (g t) -> p g t", g=NG)
            pool.wait_ge(stage1_in, 16)
            step(nc.gpsimd.memset(region(kb_at[0], 4 * W), 0.0))
            for b in range(2):
                pool.wait_ge(bank_free[b], B0["in_t"][b] + 2)
            for g, w in enumerate(WINDOWS):
                u = pT[:, U0 + 2 * g:U0 + 2 * g + 2, :]
                step(nc.gpsimd.tensor_copy(bufs[0][:, :, PAD:], u))
                a, s = 0, 1
                while s < w:
                    step(nc.gpsimd.tensor_tensor(bufs[1 - a][:, :, PAD:], bufs[a][:, :, PAD:],
                                                 bufs[a][:, :, PAD - s:PAD - s + T], ALU.add))
                    a, s = 1 - a, 2 * s
                step(nc.gpsimd.tensor_scalar(bufs[1 - a][:, :, PAD:], bufs[a][:, :, PAD:], 1.0 / w, None, ALU.mult))
                step(nc.gpsimd.tensor_tensor(bufs[1 - a][:, :, PAD:PAD + 16], bufs[a][:, :, PAD:PAD + 16],
                                             bc(inv[:, g:g + 1, :], [P, 2, 16]), ALU.mult))
                nc.gpsimd.tensor_tensor(u, bufs[1 - a][:, :, PAD:], u, ALU.subtract).then_inc(pooled, 1)
                pool.wait_ge(pooled, g + 1)

        @block.vector
        def _(dve):
            step = stepper(dve, dve_step)
            V = nc.vector

            def root_mean_square(m):
                dve.wait_ge(sq_done, TB * (m + 1))
                V.tensor_scalar(msq, ssq, 1.0 / D, EPS, ALU.mult, ALU.add).then_inc(ms_ready, 1)
                dve.wait_ge(rt_done, m + 1)
                step(V.reciprocal(rstd, rt))

            def norm(n, weight, m):
                root_mean_square(m)
                for b in range(TB):
                    V.tensor_scalar(scr_of[n][:, b * D:(b + 1) * D], xres[:, b, :], rstd[:, b:b + 1], None,
                                    ALU.mult).then_inc(xn_ready, 1)
                read_turned(n, weight)

            def read_turned(n, weight):
                def low_part(f):
                    b, j = divmod(f, 4)
                    at = (slice(None), slice(4 * j, 4 * j + 4), slice(b * P, (b + 1) * P))
                    dve.wait_ge(hTh_part, 8 * n + f + 1)
                    V.tensor_tensor(hTl[at], turned_tmp[:, f % 2, :].rearrange("p (c t) -> p c t", c=4),
                                    hTh[at].bitcast(F32), ALU.subtract).then_inc(hTl_part, 1)

                for f in range(8):
                    b, j = divmod(f, 4)
                    dve.wait_ge(turned, 8 * n + f + 1)
                    if f >= 2:
                        dve.wait_ge(hTl_part, 8 * n + f - 1)
                    V.tensor_tensor(turned_tmp[:, f % 2, :].rearrange("p (c t) -> p c t", c=4),
                                    bank[4 + j][:].rearrange("p (c t) -> p c t", c=4),
                                    bc(prm(weight, 4 * j, 4 * j + 4).unsqueeze(2), [P, 4, P]),
                                    ALU.mult).then_inc(hT_part, 1)
                    if f:
                        low_part(f - 1)
                low_part(7)

            def split(name, i, s):
                t = s % 2
                dve.wait_ge(hi_ready[t], rounded(name, i, s))
                if name.startswith("peer_v"):
                    V.tensor_tensor(glo[:, t, :].rearrange("p (g o t) -> p g o t", o=1, t=4), gate_block(i * 4 + s, 1),
                                    ghi[:, t, :].bitcast(F32).rearrange("p (g o t) -> p g o t", o=1, t=4),
                                    ALU.subtract)
                V.tensor_tensor(wlo[t][:], raw[t][:], whi[t][:].bitcast(F32), ALU.subtract).then_inc(raw_free[t], 1)

            def phase(name, after, lo=0, hi=None, started=False, ahead=False):
                n = (G0[name][1] if hi is None else hi) - lo
                if not started:
                    split(name, lo, 0)
                if n > 1:
                    with dve.Fori(0, n - 1) as i:
                        for s in range(RING):
                            split(name, i + (lo + (s + 1) // RING), (s + 1) % RING)
                            after(i, s)
                for s in range(RING):
                    if s + 1 < RING:
                        split(name, lo + n - 1, s + 1)
                    elif ahead:
                        split(name, lo + n, 0)
                    after(n - 1, s)

            def keep(i, s):
                pass

            def evac_t(name):
                def evac(i, s):
                    if s == 2:
                        dve.wait_ge(slot_used[1], multiplied(name, i, 1))
                        V.tensor_copy(R[:, bass.ds(i * (4 * T), 2 * T)], bank[0][:]).then_inc(bank_free[0], 1)
                phase(name, evac)

            def phase_n(name, evac, between=None):
                n = G0[name][1]
                for g in range(n):
                    split(name, g, 0)
                    if g:
                        evac(g - 1)
                    for s in range(1, RING):
                        split(name, g, s)
                        if between is not None:
                            between(g, s)
                evac(n - 1)

            def evac_n(name, dst, between=None):
                def evac(g):
                    dve.wait_ge(slot_used[1], multiplied(name, g, 3))
                    V.tensor_copy(dst[:, g, 1, :], bank[2 * (g % 2) + 1][:]).then_inc(bank_free[2 * (g % 2) + 1], 1)
                phase_n(name, evac, between)

            def residual(g, ready):
                for b in range(TB):
                    xs = xres[:, b, g * 512:(g + 1) * 512]
                    step(V.tensor_tensor(xs, bank[2 * (g % 2) + b][:], xs, ALU.add))
                    dve.sem_inc(bank_free[2 * (g % 2) + b], 1)
                    dve.sem_inc(ready, 1)

            dve.wait_ge(params_in, 16)
            dve.wait_ge(x_in, 16)
            norm(0, "norm1", 0)
            evac_t("in_t")
            evac_n("in_n", vN1)
            split("narrow1", 0, 0)
            split("narrow1", 0, 1)
            dve.wait_ge(pooled, NG)
            dve.wait_ge(bank_free[1], B0["in_n"][1])
            for v, (src, pe_name) in enumerate(((KCR0, "pek"), (VCR0, "pev"))):
                kv_rows = pT[:, src:src + 4, :].rearrange("p h (m r) -> p h m r", r=CS)
                for a in range(2):
                    for h in range(HKV):
                        last = V.tensor_tensor(
                            kb[v][:, a * CS:(a + 1) * CS, h * NCMP:(h + 1) * NCMP].rearrange("p r n -> p n r"),
                            kv_rows[:, h, a:a + NCMP, :],
                            bc(prm(pe_name, a * CS, (a + 1) * CS).unsqueeze(1), [P, NCMP, CS]), ALU.add)
                last.then_inc(kb_ready, 1)
            for j in range(12):
                dve.wait_ge(swapped, j + 1)
                buf = rot_buf[:, (j % 2) * 512:(j % 2 + 1) * 512].rearrange("p (j t) -> p j t", t=T)
                xb = pT[:, KS0 + 2 * j:KS0 + 2 * j + 2, :]
                V.tensor_tensor(buf, buf, bc(prm("sin").unsqueeze(1), [P, 2, T]), ALU.mult)
                step(V.tensor_tensor(xb, xb, bc(prm("cos").unsqueeze(1), [P, 2, T]), ALU.mult))
                V.tensor_tensor(xb, xb, buf, ALU.add).then_inc(roped, 1)
            dve.wait_ge(kc_copied, 1)
            step(V.tensor_tensor(kcS, kcS, prm("csin"), ALU.mult))
            step(V.tensor_tensor(kcT, kcT, prm("ccos"), ALU.mult))
            V.tensor_tensor(kcT, kcT, kcS, ALU.add).then_inc(kc_roped, 1)

            def nsa_mask(u):
                qb, a = u % TB, u % 2
                nk = (qb + 1) * P
                dve.wait_ge(scores_ready, u + 1)
                if u >= 2:
                    dve.wait_ge(probsT_ready, u - 1)
                s3 = SP[:, a, :].rearrange("p (r k) -> p r k", r=2)[:, :, 0:nk]
                m3 = prm("mask", 256 - nk, 256)
                V.tensor_tensor(s3, bank[4 + a][:].rearrange("p (r k) -> p r k", r=2)[:, :, 0:nk],
                                bc(m3.unsqueeze(1), [P, 2, nk]), ALU.add)
                step(V.tensor_tensor(Pc[:, a, 0:NCMP], bank[6 + a][:, 0:NCMP],
                                     prm("cmask", qb * NCMP, (qb + 1) * NCMP), ALU.add))
                V.tensor_reduce(mx[:, a, 0:2], s3, AX.X, ALU.max).then_inc(scores_read, 1)
                step(V.tensor_reduce(mx[:, a, 2:3], Pc[:, a, 0:NCMP], AX.X, ALU.max))
                V.tensor_scalar(ngm[:, a, 0:3], mx[:, a, 0:3], -SCALE, None, ALU.mult).then_inc(max_ready, 1)

            def nsa_scale(u):
                h, qb = divmod(u, TB)
                a, nk = u % 2, (qb + 1) * P
                dve.wait_ge(exp_done, u + 1)
                step(V.reciprocal(rz[:, a, 0:3], sums[:, a, 0:3]))
                step(V.tensor_tensor(gz[:, a, 0:3], rz[:, a, 0:3], gates_for(h, qb), ALU.mult))
                for br in range(2):
                    sl = SP[:, a, br * T:br * T + nk]
                    V.tensor_scalar(sl, sl, gz[:, a, br:br + 1], None, ALU.mult)
                V.scalar_tensor_tensor(out=Pc[:, a, 0:NCMP], in0=Pc[:, a, 0:NCMP], scalar=gz[:, a, 2:3],
                                       in1=prm("cvalid", qb * NCMP, (qb + 1) * NCMP),
                                       op0=ALU.mult, op1=ALU.mult).then_inc(probs_ready, 1)

            def gates_for(h, qb):
                return gates[:, qb, 3 * h:3 * h + 3]

            def nsa_out(h):
                dve.wait_ge(o_done, 2 * h + 2)
                g = pT[:, GN0 + h, :]
                V.tensor_tensor(g, bank[2 + h % 2][:, 0:T], g, ALU.mult).then_inc(o_read, 1)

            units = HQ * TB
            dve.wait_ge(gates_ready, 1)
            dve.wait_ge(silu_done, 2)
            split("merge", 0, 0)
            nsa_mask(0)
            for u in range(units):
                if u + 1 < units:
                    nsa_mask(u + 1)
                nsa_scale(u)
                if u in MERGE_AT:
                    split("merge", *divmod(MERGE_AT.index(u) + 1, RING))
                if u % 2 == 1 and u >= 3:
                    nsa_out(u // 2 - 1)
            nsa_out(HQ - 1)
            for g in range(NG):
                dve.wait_ge(z_ready, g + 1)
                for e in range(2):
                    c = 2 * g + e
                    last = V.scalar_tensor_tensor(out=pT[:, U0 + c, :], in0=bank[4 + g][:, e * T:(e + 1) * T],
                                                  scalar=prm("pscale", c, c + 1), in1=pT[:, GP0 + c, :],
                                                  op0=ALU.mult, op1=ALU.mult)
                last.then_inc(y_pool, 1)
            phase("merge", keep, MERGE_EARLY, started=True)
            for b in range(2):
                dve.wait_ge(bank_free[b], B0["pool_out"][b])

            def branch_low_parts(n, src):
                for j in range(8):
                    at = slice(2 * j, 2 * j + 2)
                    dve.wait_ge(branch_high, 8 * n + j + 1)
                    V.tensor_tensor(hTl[:, at, :], src[:, at, :], hTh[:, at, :].bitcast(F32),
                                    ALU.subtract).then_inc(branch_split, 1)
            branch_low_parts(0, pT[:, GN0:GN0 + 16, :])
            with dve.Fori(0, G0["pool_out"][1]) as i:
                for s in range(RING):
                    dve.wait_ge(raw_free[s % 2], consumed("pool_out", i, s))
                    gsl = R[:, bass.ds(i * (8 * T) + (16 + 2 * s) * T, 2 * T)]
                    V.tensor_tensor(gsl, bank[s][:], gsl, ALU.mult).then_inc(bank_free[s], 1)
            for s in range(RING):
                dve.wait_ge(bank_free[s], B0["nsa_out"][s])
            def merge_branches(i, s):
                if s >= 2:
                    b = s - 2
                    dve.wait_ge(slot_used[1], multiplied("nsa_out", i, 2 * b + 1))
                    g1 = R[:, bass.ds(i * (4 * T) + (32 + 2 * b) * T, 2 * T)]
                    gm = R[:, bass.ds(i * (4 * T) + (16 + 2 * b) * T, 2 * T)]
                    V.tensor_tensor(g1, bank[b][:], g1, ALU.mult).then_inc(bank_free[b], 1)
                    dve.wait_ge(bank_free[b], i + B0["nsa_out"][b] + 1)
                    V.tensor_tensor(gm, gm, g1, ALU.add).then_inc(merged_ready, 1)
            phase("nsa_out", merge_branches)
            branch_low_parts(1, gate0)

            def add_out1(g):
                dve.wait_ge(slot_used[1], multiplied("out1", g, 3))
                residual(g, x1_ready)
            phase_n("out1", add_out1)
            root_mean_square(1)
            dve.wait_ge(fnw1_in, 16)
            for b in range(TB):
                V.scalar_tensor_tensor(out=xres[:, b, :], in0=xres[:, b, :], scalar=rstd[:, b:b + 1],
                                       in1=fnw1_sb, op0=ALU.mult, op1=ALU.mult).then_inc(x1_normed, 1)

            norm(1, "norm2", 2)
            evac_t("in2_t")
            split("narrow2", 0, 0)
            split("narrow2", 0, 1)

            def convolve(j):
                src, y = pT[:, MQ0 + j, :], conv[:, j, :]
                cw = prm("convw", 4 * j, 4 * j + 4)
                step(V.tensor_scalar(y, src, cw[:, 3:4], prm("convb", j, j + 1), ALU.mult, ALU.add))
                for tap in range(3):
                    sh = 3 - tap
                    last = V.scalar_tensor_tensor(out=y[:, sh:T], in0=src[:, 0:T - sh], scalar=cw[:, tap:tap + 1],
                                                  in1=y[:, sh:T], op0=ALU.mult, op1=ALU.add)
                    if tap < 2:
                        step(last)
                last.then_inc(conv_done, 1)

            def gate_rows(g, s):
                bl = rows[0:4, 8, P - 1:P]
                if g in (1, 4, 5) and (g, s) != (5, 3):
                    convolve({1: 0, 4: 3, 5: 6}[g] + s - 1)
                if (g, s) == (0, 1):
                    dve.wait_ge(rowsT_ready, 1)
                    V.tensor_scalar(rows[0:8, 0, :], bank[5][0:FH, 0:T], prm_rows("fbias", 8), None, ALU.add)
                    V.tensor_scalar(rows[0:4, 1, :], bank[5][ROW_AT[1]:ROW_AT[1] + MH, 0:T], prm_rows("ibias", 4), None, ALU.add)
                    step(V.tensor_scalar(rows[0:4, 2, :], bank[5][ROW_AT[2]:ROW_AT[2] + MH, 0:T], prm_rows("mfbias", 4), None, ALU.add))
                elif (g, s) == (0, 2):
                    step(V.tensor_scalar(rows[0:8, 4, :], rows[0:8, 0, :], -1.0, None, ALU.mult))
                    step(V.tensor_scalar(rows[0:4, 5, :], rows[0:4, 2, :], -1.0, None, ALU.mult))
                elif (g, s) == (0, 3):
                    V.tensor_tensor(rows[0:8, 4, :], rows[0:8, 4, :], rows[0:8, 0, :], ALU.min)
                    V.tensor_tensor(rows[0:4, 5, :], rows[0:4, 5, :], rows[0:4, 2, :], ALU.min).then_inc(row_y, 1)
                    V.tensor_scalar(rows[0:8, 0, :], rows[0:8, 0, :], 0.0, None, ALU.min)
                    step(V.tensor_scalar(rows[0:4, 2, :], rows[0:4, 2, :], 0.0, None, ALU.min))
                elif (g, s) == (2, 1):
                    dve.wait_ge(row_l, 1)
                    V.tensor_tensor(rows[0:8, 0, :], rows[0:8, 0, :], rows[0:8, 4, :], ALU.subtract)
                    step(V.tensor_tensor(rows[0:4, 2, :], rows[0:4, 2, :], rows[0:4, 5, :], ALU.subtract))
                elif (g, s) == (2, 2):
                    V.tensor_tensor_scan(rows[0:8, 6, :], bc(prm_rows("cone", 8), [8, T]), rows[0:8, 0, :], 0.0,
                                         ALU.mult, ALU.add)
                    for c in range(TB):
                        cs = slice(c * P, (c + 1) * P)
                        last = V.tensor_tensor_scan(rows[0:4, 8, cs], bc(prm_rows("cone", 4), [4, P]),
                                                    rows[0:4, 2, cs], 0.0, ALU.mult, ALU.add)
                    step(last)
                elif (g, s) == (2, 3):
                    V.tensor_scalar(rows[0:8, 7, :], rows[0:8, 6, :], -1.0, None, ALU.mult)
                    step(V.tensor_tensor(rows[0:4, 9, :], rows[0:4, 1, :], rows[0:4, 8, :], ALU.subtract))
                elif (g, s) == (3, 1):
                    step(V.tensor_reduce(rowst[0:4, 0:1], rows[0:4, 9, 0:P], AX.X, ALU.max))
                    step(V.tensor_tensor(rowst[0:4, 0:1], rowst[0:4, 0:1], bl, ALU.add))
                    step(V.tensor_tensor(rowst[0:4, 2:3], rowst[0:4, 0:1], bl, ALU.max))
                elif (g, s) == (3, 2):
                    V.tensor_copy(rows[0:4, 10, 0:P], rows[0:4, 8, 0:P])
                    V.tensor_scalar(rows[0:4, 10, P:T], rows[0:4, 8, P:T], rowst[0:4, 2:3], None, ALU.add)
                    V.tensor_tensor(rowst[0:4, 1:2], bl, rowst[0:4, 2:3], ALU.subtract).then_inc(a_ready, 1)
            dve.wait_ge(bank_free[1], B0["in2_n"][1])
            evac_n("in2_n", vN2, gate_rows)
            V.tensor_scalar(pT[:, FQ0:FQ0 + 8, :], pT[:, FQ0:FQ0 + 8, :], SCALE, None, ALU.mult).then_inc(q_ready, 1)
            dve.wait_ge(conv_silu, 1)
            V.tensor_scalar(conv[:, 4:8, :], conv[:, 4:8, :], SCALE, None, ALU.mult).then_inc(q_ready, 1)
            dve.wait_ge(nat_copied, 1)
            dve.wait_ge(bank_free[0], B0["out2"][0])
            dve.wait_ge(bank_free[2], B0["out2"][2])
            for h in range(MH):
                a_col = natc[:, 32 + h:33 + h]
                if h >= 1:
                    dve.wait_ge(C_ready, h)
                V.tensor_scalar(av[:, 0:MV], vN2[:, 2 + h // 2, 0, (h % 2) * MV:(h % 2 + 1) * MV], a_col, None, ALU.mult)
                V.tensor_copy(av[:, MV:MV + 1], a_col).then_inc(av_ready, 1)
                dve.wait_ge(C_ready, h + 1)
                V.tensor_copy(CN[:, h, 0:MV + 1], bank[6][:, 0:MV + 1]).then_inc(C_copied, 1)

            def fox_mask(u):
                h, qb = divmod(u, TB)
                a, nk = u % 2, (qb + 1) * P
                dve.wait_ge(f_scores, u + 1)
                if u >= 2:
                    dve.wait_ge(f_T, u - 1)
                V.scalar_tensor_tensor(out=SP2[:, a, 0:nk], in0=bank[4 + a][:, 0:nk],
                                       scalar=natc[:, 8 * qb + h:8 * qb + h + 1], in1=prm("mask", 256 - nk, 256),
                                       op0=ALU.add, op1=ALU.add).then_inc(f_read, 1)
                dve.wait_ge(f_read, u + 1)
                step(V.tensor_reduce(mx[:, a, 0:1], SP2[:, a, 0:nk], AX.X, ALU.max))
                V.tensor_scalar(ngm[:, a, 0:1], mx[:, a, 0:1], -1.0, None, ALU.mult).then_inc(f_max, 1)

            def fox_out(u):
                h, qb = divmod(u, TB)
                a = u % 2
                dve.wait_ge(f_exp, u + 1)
                step(V.reciprocal(rz[:, a, 0:1], sums[:, a, 0:1]))
                dve.wait_ge(f_o, u + 1)
                V.tensor_scalar(scr2[:, qb, h * DH:(h + 1) * DH], bank[2 + a][:, 0:DH], rz[:, a, 0:1], None,
                                ALU.mult).then_inc(f_oread, 1)

            units = FH * TB
            fox_mask(0)
            for u in range(units):
                if u + 1 < units:
                    if u >= 1:
                        fox_out(u - 1)
                    fox_mask(u + 1)
            fox_out(units - 2)
            fox_out(units - 1)

            def m_mask(u):
                c, h = divmod(u, MH)
                a = u % 2
                dve.wait_ge(m_scores, u + 1)
                g_col = natc[:, 24 + 4 * c + h:25 + 4 * c + h]
                step(V.scalar_tensor_tensor(out=Dm[:, a, :], in0=bank[4 + a][:, P:2 * P],
                                            scalar=natc[:, 16 + 4 * c + h:17 + 4 * c + h], in1=tri,
                                            op0=ALU.add, op1=ALU.add))
                step(V.tensor_reduce(mst[:, a, 0:1], Dm[:, a, :], AX.X, ALU.max))
                step(V.tensor_tensor(mst[:, a, 0:1], mst[:, a, 0:1], g_col, ALU.max))
                V.tensor_scalar(mst[:, a, 1:2], mst[:, a, 0:1], -1.0, None, ALU.mult)
                V.tensor_tensor(mst[:, a, 2:3], g_col, mst[:, a, 0:1], ALU.subtract).then_inc(m_max, 1)

            def m_weigh(u):
                a = u % 2
                dve.wait_ge(m_exp, u + 1)
                if u >= 2:
                    dve.wait_ge(m_T, u - 1)
                V.tensor_tensor_reduce(Sm[:, a, :], bank[4 + a][:, 0:P], Dm[:, a, :], 1.0, 0.0, ALU.mult, ALU.add,
                                       mst[:, a, 5:6]).then_inc(m_sm, 1)

            def m_out(u):
                c, h = divmod(u, MH)
                a = u % 2
                dve.wait_ge(m_num, u + 1)
                dve.wait_ge(m_sm, u + 1)
                if c == 1:
                    step(V.tensor_scalar(numt[:, a, :], bank[a][:, 0:MV], mst[:, a, 4:5], None, ALU.mult))
                    V.scalar_tensor_tensor(out=mst[:, a, 5:6], in0=bank[a][:, MV:MV + 1], scalar=mst[:, a, 4:5],
                                           in1=mst[:, a, 5:6], op0=ALU.mult, op1=ALU.add)
                    step(V.tensor_tensor(numt[:, a, :], bank[2 + a][:, 0:MV], numt[:, a, :], ALU.add))
                else:
                    step(V.tensor_copy(numt[:, a, :], bank[2 + a][:, 0:MV]))
                step(V.tensor_scalar(mst[:, a, 6:7], mst[:, a, 5:6], -1.0, None, ALU.mult))
                step(V.tensor_tensor(mst[:, a, 6:7], mst[:, a, 6:7], mst[:, a, 5:6], ALU.max))
                step(V.tensor_tensor(mst[:, a, 6:7], mst[:, a, 6:7], mst[:, a, 3:4], ALU.max))
                step(V.reciprocal(mst[:, a, 7:8], mst[:, a, 6:7]))
                V.tensor_scalar(scr2[:, c, 1024 + h * MV:1024 + (h + 1) * MV], numt[:, a, :], mst[:, a, 7:8], None,
                                ALU.mult).then_inc(m_read, 1)

            units = MH * TB
            m_mask(0)
            m_weigh(0)
            for u in range(units):
                if u + 1 < units:
                    m_mask(u + 1)
                    m_weigh(u + 1)
                m_out(u)
            dve.wait_ge(mo_sig, 1)
            dve.wait_ge(m_read, units)
            for b in range(TB):
                for g in range(2):
                    sl = scr2[:, b, 1024 + g * 512:1024 + (g + 1) * 512]
                    last = V.tensor_tensor(sl, sl, vN2[:, 4 + g, b, :], ALU.mult)
            last.then_inc(cells, 1)
            dve.wait_ge(head_sq, 1)
            sq = region(0, 4096).rearrange("p (b d) -> p b d", b=TB)
            for b in range(TB):
                V.tensor_reduce(hss[:, b, 0:8], sq[:, b, 0:1024].rearrange("p (h e) -> p h e", h=FH), AX.X, ALU.add)
                last = V.tensor_reduce(hss[:, b, 8:12], sq[:, b, 1024:2048].rearrange("p (h e) -> p h e", h=MH), AX.X,
                                       ALU.add)
            step(last)
            V.tensor_scalar(hss[:, :, 0:8], hss[:, :, 0:8], 1.0 / DH, EPS, ALU.mult, ALU.add)
            V.tensor_scalar(hss[:, :, 8:12], hss[:, :, 8:12], 1.0 / MV, EPS, ALU.mult, ALU.add).then_inc(head_ms, 1)
            dve.wait_ge(head_rt, 1)
            step(V.reciprocal(hrt, hrt))
            for b in range(TB):
                fa = scr2[:, b, 0:1024].rearrange("p (h e) -> p h e", h=FH)
                ce = scr2[:, b, 1024:2048].rearrange("p (h e) -> p h e", h=MH)
                V.tensor_tensor(fa, fa, bc(hrt[:, b, 0:8].unsqueeze(2), [P, FH, DH]), ALU.mult)
                V.tensor_tensor(ce, ce, bc(hrt[:, b, 8:12].unsqueeze(2), [P, MH, MV]), ALU.mult).then_inc(xn_ready, 1)
            read_turned(2, "mixnorm")

            def add_out2(g):
                dve.wait_ge(slot_used[1], multiplied("out2", g, 3))
                residual(g, x2_ready)
            phase_n("out2", add_out2)

            norm(3, "norm3", 3)
            evac_t("wq")
            split("peer_u0", 0, 0)
            dve.wait_ge(qs_copied, 8)

            def top16(rows_, step_):
                for v, tv, ti in rows_:
                    last = V.max(tv[:, 0:8], v)
                step_(last)
                for v, tv, ti in rows_:
                    V.max_index(ti[:, 0:8], tv[:, 0:8], v)
                for v, tv, ti in rows_:
                    last = V.match_replace(v, tv[:, 0:8], v, LOWEST)
                step_(last)
                for v, tv, ti in rows_:
                    last = V.max(tv[:, 8:16], v)
                step_(last)
                for v, tv, ti in rows_:
                    last = V.max_index(ti[:, 8:16], tv[:, 8:16], v)
                return last

            key_groups = TB * 2 * PH // 8
            for slot in range(RING * key_groups):
                split("peer_u0", *divmod(slot + 1, RING))
                step(top16([(scores[:, u, :], topv[:, u, :], topi[:, u, :]) for u in (2 * slot, 2 * slot + 1)], step))

            def choose(b, n):
                side, part = divmod(n - 6, 3)
                if n == 0:
                    step(V.tensor_copy(topf[:, 16 * b:16 * b + 16], topi[:, 16 * b:16 * b + 16]))
                    tv4 = topv[:, 16 * b:16 * b + 16].rearrange("p (h s) k -> p h s k", s=2)
                    step(V.tensor_tensor(cand[:, b].rearrange("p h (i j) -> p h i j", i=TOPK),
                                         bc(tv4[:, :, 0, :].unsqueeze(3), [P, PH, TOPK, TOPK]),
                                         bc(tv4[:, :, 1, :].unsqueeze(2), [P, PH, TOPK, TOPK]), ALU.add))
                elif n <= 4:
                    step(top16([(cand[:, b, h, :], finv[:, b, h, :], fini[:, b, h, :])
                                for h in (2 * n - 2, 2 * n - 1)], step))
                elif n == 5:
                    pos = fini[:, b].rearrange("p h k -> p (h k)")
                    V.tensor_scalar(fab_u[:, 0, b, :], pos, 4, None, ALU.logical_shift_right)
                    step(V.tensor_scalar(fab_u[:, 1, b, :], pos, 15, None, ALU.bitwise_and))
                    for s in range(2):
                        last = V.tensor_copy(fab[:, s, b].rearrange("p h k -> p (h k)"), fab_u[:, s, b, :])
                    step(last)
                    step(V.tensor_copy(zs[:, b, :], finv[:, b, :, 0]))
                    V.tensor_tensor(finv[:, b], finv[:, b], bc(zs[:, b, :].unsqueeze(2), [P, PH, TOPK]),
                                    ALU.subtract).then_inc(gate_arg, 1)
                elif part == 0:
                    step(V.tensor_tensor(onehots[:, b], bc(fab[:, side, b].unsqueeze(3), [P, PH, TOPK, TOPK]),
                                         bc(prm("iota", 0, TOPK).unsqueeze(1).unsqueeze(1), [P, PH, TOPK, TOPK]),
                                         ALU.is_equal))
                elif part == 1:
                    tf4 = topf[:, 16 * b:16 * b + 16].rearrange("p (h s) k -> p h s k", s=2)
                    step(V.tensor_tensor(onehots[:, b], onehots[:, b],
                                         bc(tf4[:, :, side, :].unsqueeze(2), [P, PH, TOPK, TOPK]), ALU.mult))
                else:
                    step(V.tensor_reduce(chosen[:, b, side, :].rearrange("p (h k) -> p h k", h=PH), onehots[:, b],
                                         AX.X, ALU.add))
                if n == 11:
                    dve.wait_ge(gate_exp, b + 1)
                    step(V.tensor_reduce(zs[:, b, :], finv[:, b], AX.X, ALU.add))
                    step(V.reciprocal(zs[:, b, :], zs[:, b, :]))
                    V.tensor_tensor(chosen[:, b, 2, :].rearrange("p (h k) -> p h k", h=PH), finv[:, b],
                                    bc(zs[:, b, :].unsqueeze(2), [P, PH, TOPK]), ALU.mult).then_inc(chosen_ready, 1)
            assert RING * (CHOOSE_G - key_groups) == 12 * TB
            for b in range(TB):
                for n in range(12):
                    split("peer_u0", *divmod(RING * key_groups + 12 * b + n + 1, RING))
                    choose(b, n)

            def hot_rows(i, n):
                dve.wait_ge(hot_used, i * 8 + n + 1)
                at = 2 * n % TRACK
                V.tensor_tensor(second_hot[:, at:at + 2, :], bc(prm("iota").unsqueeze(1), [P, 2, NK]),
                                bc(idxT[:, 1, bass.ds(i * 16 + 2 * n, 2)].unsqueeze(2), [P, 2, NK]), ALU.is_equal)
                for t in range(2):
                    def col(s):
                        return idxT[:, s, bass.ds(i * 16 + (2 * n + t), 1)]
                    last = V.tensor_scalar(first_hot[:, at + t, :], prm("iota"), col(0), col(2),
                                           ALU.is_equal, ALU.mult)
                last.then_inc(hot_ready, 1)

            def slot_rows(i, s):
                for n in range(4, 12):
                    if not (isinstance(i, int) and i == MAKE_G - 1 and s == RING - 1 and n >= 8):
                        hot_rows(i * 4 + s, n)
                    if n % 2 == 1:
                        m = i * 16 + (4 * s + (n - 5) // 2)
                        dve.wait_ge(hot_used, i * 32 + (8 * s + n - 5 + 2 + TRACK // 2))
                        g4 = G[:, bass.ds(m, 1), 0:EARLY, :].rearrange("p g j t -> p (g j) t")
                        V.tensor_tensor(g4, bank[4 + (n - 5) // 2][:].rearrange("p (t n) -> p n t", t=4)[:, 0:EARLY, :],
                                        g4, ALU.mult).then_inc(g_weighted, 1)
            dve.sem_inc(g_weighted, 4)
            dve.wait_ge(chosenT_copied, 1)
            for b in range(2):
                dve.wait_ge(bank_free[b], B0["peer_u0"][b] + CHOOSE_G)
            for n in range(4):
                hot_rows(0, n)
            phase("peer_u0", slot_rows, CHOOSE_G, CHOOSE_G + MAKE_G, started=True, ahead=True)

            def gate(name, lo):
                def after(i, s):
                    if s >= 2:
                        b = s - 2
                        dve.wait_ge(bank_free[b], i + lo + B0[name][b] + 1)
                        gb = gate_block(i * 4 + (4 * lo + 2 * b), 2)
                        V.tensor_tensor(gb, gb, gelu_u[:, b, :].rearrange("p (j g t) -> p g j t", j=2, t=4),
                                        ALU.mult).then_inc(gated[b], 1)
                return after

            REST = G0["peer_u0"][1] - CHOOSE_G - MAKE_G

            def gate_late(rest, at, groups):
                n = MAKE_G // groups

                def after(i, s):
                    j = i * (RING * n) + s * n
                    gb = gate_block(j + at, n)
                    V.tensor_tensor(gb, gb, late_acts[:, bass.ds(j, n), :].rearrange("p j (g t) -> p g j t", t=4),
                                    ALU.mult)
                    rest(i, s)
                return after

            def add_experts(half, ready):
                name = f"peer_v{half}"
                dve.wait_ge(slot_used[1], multiplied(name, G0[name][1] - 1, 3))
                for c in range(8):
                    xs = xres[:, c // 4, (c % 4) * 512:(c % 4 + 1) * 512]
                    V.tensor_tensor(xs, bank[c][:], xs, ALU.add).then_inc(ready, 1)

            for half in range(2):
                if half == 0:
                    dve.wait_ge(g_kept, 4 + T // 4)
                    dve.wait_ge(bank_free[1], B0["peer_u0"][1] + CHOOSE_G + MAKE_G)
                    phase("peer_u0", gate_late(gate("peer_u0", CHOOSE_G + MAKE_G), EARLY, REST), CHOOSE_G + MAKE_G,
                          started=True)
                    dve.wait_ge(g_weighted, 4 + T // 4)
                else:
                    split("peer_u1", 0, 0)
                    add_experts(0, v_read)
                    phase("peer_u1", keep, 0, MAKE_G, started=True, ahead=True)
                    dve.wait_ge(gates_in, 16 * RING * MAKE_G)
                    dve.wait_ge(bank_free[1], B0["peer_u1"][1] + MAKE_G)
                    phase("peer_u1", gate_late(gate("peer_u1", MAKE_G), 0, MAKE_G), MAKE_G, 2 * MAKE_G, started=True,
                          ahead=True)
                    phase("peer_u1", gate("peer_u1", 2 * MAKE_G), 2 * MAKE_G, started=True)
                for b in range(2):
                    dve.wait_ge(gated[b], 1 + REST + half * (G0["peer_u1"][1] - MAKE_G))
                with dve.Fori(0, G0["peer_v0"][1]) as i:
                    for s in range(RING):
                        split(f"peer_v{half}", i, s)
            add_experts(1, x3_ready)
            root_mean_square(4)
            dve.wait_ge(fnw_in, 16)
            for b in range(TB):
                V.scalar_tensor_tensor(out=R[:, b * D:(b + 1) * D], in0=xres[:, b, :], scalar=rstd[:, b:b + 1],
                                       in1=raw[0][:], op0=ALU.mult, op1=ALU.mult).then_inc(result, 1)



def cols_t(w):
    k, n = w.shape
    return w.reshape(k // P, P, n // P, P).transpose(2, 1, 0, 3).reshape(n // P, P, k)


def cols_n(w):
    n = w.shape[1]
    return w.reshape(4, 4, P, n // 512, 512).transpose(3, 0, 2, 1, 4).reshape(n // 512 * 4, P, SLOT)


def on_partitions(v):
    return v.reshape(-1, P).T


def layout(i):
    f = np.float32
    cut = np.cumsum([0, POOL_W, POOL_W, 2048, 512, 512, 512, 512, 512, 512, 2048, 48])
    w1 = i["w_in"][0]
    part = [w1[:, a:b] for a, b in zip(cut[:-1], cut[1:])]
    u, gp, q, kcr, vcr, ks, vs, kw, vw, gn, gb = part
    cut2 = np.cumsum([0, 1024, 1024, 1024, 8, 512, 512, 1024, 4, 4, 1024])
    fq, fk, fv, ff, mq, mk, mv, mi, mf, mo = [i["w_in_2"][0][:, a:b] for a, b in zip(cut2[:-1], cut2[1:])]

    def cmp_w1(w):
        return w[0].reshape(RING, 8, P, CH).transpose(0, 2, 1, 3).reshape(RING, P, SLOT)

    pool_out = cols_t(i["w_pool_out"][0]).reshape(8, 2, P, 1024).transpose(0, 2, 1, 3).reshape(8, P, SLOT)
    def narrow(columns):
        w = np.zeros((D, 2 * P), np.float32)
        for at, c in columns:
            w[:, at:at + c.shape[1]] = c
        return cols_t(w)

    gb3 = gb.reshape(D, HQ, 3)[:, :, [1, 2, 0]].reshape(D, 3 * HQ)
    peer_u = i["peer_u_2"][0].reshape(NK, P, KC, P).transpose(0, 3, 2, 1).reshape(NK, P, SLOT)
    peer_v = i["peer_v_2"][0].reshape(NK, P, SLOT)
    stream = np.concatenate([
        *(cols_t(w) for w in (u, gp, kcr, vcr, ks, kw, q, gn)), cols_n(vs), cols_n(vw), narrow([(0, gb3)]),
        cmp_w1(i["cmp_w1_k"]), cmp_w1(i["cmp_w1_v"]), cols_t(i["w_merge"][0]).reshape(8, 4, P, D)[list(MERGE_ORDER)].reshape(32, P, D), pool_out,
        cols_t(i["w_nsa_out"][0]), cols_n(i["w_out"][0]),
        *(cols_t(w) for w in (fq, fk, mq, mk)), narrow(zip(ROW_AT, (ff, mi, mf))), *(cols_n(w) for w in (fv, mv, mo)),
        cols_n(i["w_out_2"][0]), cols_t(i["peer_w_q_2"][0]),
        *(w[half * HALF:(half + 1) * HALF] for half in range(2) for w in (peer_u, peer_v))])

    t = np.arange(T)
    inv = (f(10000.0) ** (-np.arange(64, dtype=f) / f(64))).astype(f)

    def rot(pos):
        ang = (pos.astype(f)[None, :] * inv[:, None]).astype(f)
        c, s = np.cos(ang), np.sin(ang)
        return np.concatenate([c, c]).astype(f), np.concatenate([-s, s]).astype(f)

    cos, sin = rot(t)
    ccos, csin = (np.tile(a, (1, HKV)) for a in rot(np.arange(NCMP) * CS + CB - 1))
    tri = np.where(np.arange(P)[None, :] <= np.arange(P)[:, None], 0, NEG)
    valid = (np.arange(NCMP) * CS + CB - 1)[None, :] <= t[:, None]
    per_block = lambda a: a.reshape(TB, P, NCMP).transpose(1, 0, 2).reshape(P, TB * NCMP)
    table = {
        "ident": np.eye(P), "mask": np.concatenate([np.zeros((P, P)), tri], 1), "cos": cos, "sin": sin,
        "ccos": ccos, "csin": csin, "cmask": per_block(np.where(valid | ~valid.any(1, keepdims=True), 0, NEG)), "cvalid": per_block(valid),
        "iota": np.tile(np.arange(P), (P, 1)), "cone": np.ones((P, 1)),
        "norm1": on_partitions(i["norm_w"][0]), "norm2": on_partitions(i["norm1_w_2"][0]),
        "norm3": on_partitions(i["norm2_w_2"][0]),
        "mixnorm": on_partitions(np.concatenate([i["fox_out_norm_w_2"][0], i["mlstm_out_norm_w_2"][0]])),
        "pscale": on_partitions(i["pool_scale"][0]), "bmerge": on_partitions(i["b_merge"][0]),
        "pek": i["cmp_pe_k"][0].T, "pev": i["cmp_pe_v"][0].T,
        "convw": i["mlstm_conv_w_2"][0].reshape(4, 8, P).transpose(2, 1, 0).reshape(P, 32),
        "convb": on_partitions(i["mlstm_conv_b_2"][0]),
        "fbias": i["fox_f_bias_2"][0][:, None], "ibias": i["mlstm_i_bias_2"][0][:, None],
        "mfbias": i["mlstm_f_bias_2"][0][:, None],
        "keysT": i["peer_keys_2"][0].transpose(2, 0, 1).reshape(P, 2 * NK),
    }
    cnt = np.minimum(t[None, :] + 1, np.array(WINDOWS)[:, None]).astype(f)
    table1 = {
        "invcnt": np.tile((f(1) / cnt[:, :16]).reshape(1, NG * 16), (P, 1)),
        "w2k": i["cmp_w2_k"][0].reshape(2, P, DH).transpose(1, 0, 2).reshape(P, 2 * DH),
        "w2v": i["cmp_w2_v"][0].reshape(2, P, DH).transpose(1, 0, 2).reshape(P, 2 * DH),
    }

    def packed(names, values):
        off, n = offsets(names)
        a = np.zeros((P, n), f)
        for name, (o, w) in off.items():
            v = values[name]
            assert v.shape[1] == w, name
            a[:v.shape[0], o:o + w] = v
        return a

    return {"x": i["x"], "stream": stream, "params": packed(PARAMS, table), "stage1": packed(STAGE1, table1),
            "mixw": i["pool_mix"][0].reshape(NG, 2, P, 256).transpose(2, 0, 1, 3).reshape(P, 2048), "fnw1": i["final_norm_w"], "fnw": i["final_norm_w_2"]}


def kernel(**inputs):
    import concourse.bacc as bacc
    from concourse.bass_utils import run_bass_kernel_spmd

    arrays = {n: np.ascontiguousarray(a) for n, a in layout({k: np.asarray(v) for k, v in inputs.items()}).items()}
    nc = bacc.Bacc("TRN2", target_bir_lowering=False, num_devices=1)
    args = [nc.dram_tensor(n, a.shape, F32, kind="ExternalInput").ap() for n, a in arrays.items()]
    out = nc.dram_tensor("out", (1, T, D), F32, kind="ExternalOutput").ap()
    gates_dram = nc.dram_tensor("gates_dram", (T // 4, P, HALF * 4), F32, kind="Internal").ap()
    build_two_blocks(nc, *args, gates_dram, out)
    r = run_bass_kernel_spmd(nc, [arrays], core_ids=[0])
    return r.results[0]["out"]
```
